# Optimizing a Trainium2 kernel written in Bass

```python
import jax
import jax.numpy as jnp
from jax import lax
import numpy as np
import jax, jax.numpy as jnp

D_MODEL = 1024
BATCH = 1
SEQ = 512
DEPTH = 1

GRID_W = 64
CTX_LEN = 256
MIX_WIDTH = D_MODEL
HG_WIDTH = MIX_WIDTH // 2
HG_HEADS = 4
HG_KDIM = 128
HG_KEYS = HG_HEADS * HG_KDIM
HG_VDIM = HG_WIDTH // HG_HEADS
SC_WIDTH = MIX_WIDTH - HG_WIDTH
CONV_W = 3
CHUNK = 32
N_EXPERTS = 16
EC_CAPACITY = 2
EXPERT_DFF = 2 * D_MODEL
N_MOD = 6
EPS = 1e-6
IN_COLS = 3 * HG_KEYS + 2 * HG_WIDTH + 3 * SC_WIDTH


def rms_norm(x, gain):
    xf = x.astype(jnp.float32)
    y = xf * lax.rsqrt(jnp.mean(xf * xf, axis=-1, keepdims=True) + EPS)
    return (y * gain.astype(jnp.float32)).astype(x.dtype)

def modulate(h, shift, scale):
    return h * (1 + scale) + shift

def adaln(cond, w, b):
    return jnp.split(jax.nn.silu(cond) @ w + b, N_MOD, axis=-1)

def dwconv3(u, w):
    pad = [(0, 0)] * (u.ndim - 2) + [(1, 1), (0, 0)]
    up = jnp.pad(u, pad)
    return w[0] * up[..., :-2, :] + w[1] * up[..., 1:-1, :] + w[2] * up[..., 2:, :]

def split_proj(z):
    cuts = [HG_KEYS, 2 * HG_KEYS, 3 * HG_KEYS, 3 * HG_KEYS + HG_WIDTH, 3 * HG_KEYS + 2 * HG_WIDTH,
            3 * HG_KEYS + 2 * HG_WIDTH + SC_WIDTH, 3 * HG_KEYS + 2 * HG_WIDTH + 2 * SC_WIDTH]
    return jnp.split(z, cuts, axis=-1)

def hgrn2_gates(zf, lb):
    b, t, _ = zf.shape
    f = lb + (1.0 - lb) * jax.nn.sigmoid(zf.astype(jnp.float32))
    return jnp.log(f).reshape(b, t, HG_HEADS, HG_KDIM), (1.0 - f).reshape(b, t, HG_HEADS, HG_KDIM)

def gla_chunked(q, k, v, log_f, s0):
    b, t, h, _ = q.shape
    dv = v.shape[-1]
    n = t // CHUNK
    q, k, v, log_f = [a.astype(jnp.float32).reshape(b, n, CHUNK, h, a.shape[-1]) for a in (q, k, v, log_f)]
    cum = jnp.cumsum(log_f, axis=2)
    last = cum[:, :, -1:]
    q_dec = q * jnp.exp(cum)
    k_inv = k * jnp.exp(-cum)
    k_end = k * jnp.exp(last - cum)
    lower = jnp.tril(jnp.ones((CHUNK, CHUNK), jnp.bool_))
    scores = jnp.where(lower, jnp.einsum('bnihd,bnjhd->bnhij', q_dec, k_inv), 0.0)
    o_intra = jnp.einsum('bnhij,bnjhv->bnihv', scores, v)
    kv = jnp.einsum('bnjhd,bnjhv->bnhdv', k_end, v)
    decay = jnp.exp(last[:, :, 0])

    def step(s, inp):
        dec, kv_n = inp
        return dec[..., None] * s + kv_n, s

    s_final, s_prev = lax.scan(step, s0.astype(jnp.float32),
                               (jnp.moveaxis(decay, 1, 0), jnp.moveaxis(kv, 1, 0)))
    o_inter = jnp.einsum('bnihd,nbhdv->bnihv', q_dec, s_prev)
    return (o_intra + o_inter).reshape(b, t, h, dv), s_final

def gla_final_state(k, v, log_f):
    cum = jnp.cumsum(log_f, axis=1)
    return jnp.einsum('bthd,bthv->bhdv', k * jnp.exp(cum[:, -1:] - cum), v)

def hgrn2_mix(q, i, zf_f, zf_b, g, lb_f, lb_b, s0_f, s0_b, gain):
    b, t, _ = q.shape
    qh = q.reshape(b, t, HG_HEADS, HG_KDIM)
    vh = i.reshape(b, t, HG_HEADS, HG_VDIM)
    logf_f, k_f = hgrn2_gates(zf_f, lb_f)
    logf_b, k_b = hgrn2_gates(zf_b, lb_b)
    rev = lambda a: jnp.flip(a, axis=1)
    o_f, s_f = gla_chunked(qh, k_f, vh, logf_f, s0_f)
    o_b, s_b = gla_chunked(rev(qh), rev(k_b), rev(vh), rev(logf_b), s0_b)
    o = (o_f + rev(o_b)).astype(q.dtype)
    o = rms_norm(o, gain) * jax.nn.silu(g.reshape(b, t, HG_HEADS, HG_VDIM))
    return o.reshape(b, t, HG_WIDTH), s_f, s_b

def hgrn2_context_states(zf_f, zf_b, i, lb_f, lb_b):
    b, t, _ = i.shape
    vh = i.astype(jnp.float32).reshape(b, t, HG_HEADS, HG_VDIM)
    logf_f, k_f = hgrn2_gates(zf_f, lb_f)
    logf_b, k_b = hgrn2_gates(zf_b, lb_b)
    s_f = gla_final_state(k_f, vh, logf_f)
    s_b = gla_final_state(jnp.flip(k_b, 1), jnp.flip(vh, 1), jnp.flip(logf_b, 1))
    return s_f, s_b

def token_mix(h, w_in_l, w_out_l, lb_f, lb_b, hg_gain, conv_l, s0_f, s0_b, grid_rows):
    b, t, _ = h.shape
    q, zf_f, zf_b, i, g, gate_b, gate_c, v = split_proj(h @ w_in_l)
    o_hg, s_f, s_b = hgrn2_mix(q, i, zf_f, zf_b, g, lb_f, lb_b, s0_f, s0_b, hg_gain)
    u = gate_c * v
    if grid_rows is None:
        y = dwconv3(u, conv_l)
    else:
        y = dwconv3(u.reshape(b, grid_rows, GRID_W, SC_WIDTH), conv_l).reshape(b, t, SC_WIDTH)
    y = gate_b * y
    return jnp.concatenate([o_hg, y], axis=-1) @ w_out_l, s_f, s_b

def expert_choice_ffn(h, w_router, w_gate, w_up, w_down):
    b, t, d = h.shape
    cap = EC_CAPACITY * t // N_EXPERTS
    aff = jax.nn.softmax(jnp.einsum('btd,de->bte', h, w_router).astype(jnp.float32), axis=-1)
    gate, idx = lax.top_k(jnp.swapaxes(aff, 1, 2), cap)
    xs = jax.vmap(lambda hb, ib: hb[ib])(h, idx)
    hid = jax.nn.silu(jnp.einsum('becd,edf->becf', xs, w_gate)) * jnp.einsum('becd,edf->becf', xs, w_up)
    ys = jnp.einsum('becf,efd->becd', hid, w_down) * gate[..., None].astype(h.dtype)
    return jax.vmap(lambda ib, yb: jnp.zeros((t, d), yb.dtype).at[ib.reshape(-1)].add(yb.reshape(-1, d)))(idx, ys)

def first_inputs(seed: int = 0) -> dict:
    key = jax.random.key(seed)
    ks = jax.random.split(key, 20)
    nrm = lambda k, shape, s: jax.random.normal(k, shape, jnp.float32) * s
    return {
        'x': nrm(ks[0], (BATCH, SEQ, D_MODEL), 1.0),
        'c': nrm(ks[1], (BATCH, D_MODEL), 1.0),
        'ctx': nrm(ks[2], (BATCH, CTX_LEN, D_MODEL), 1.0),
        'c_ctx': nrm(ks[3], (D_MODEL,), 1.0),
        'w_ada': nrm(ks[4], (DEPTH, D_MODEL, N_MOD * D_MODEL), 0.5 * D_MODEL ** -0.5),
        'b_ada': nrm(ks[5], (DEPTH, N_MOD * D_MODEL), 0.02),
        'norm_mix': 1.0 + nrm(ks[6], (DEPTH, D_MODEL), 0.02),
        'norm_ffn': 1.0 + nrm(ks[7], (DEPTH, D_MODEL), 0.02),
        'w_in': nrm(ks[8], (DEPTH, D_MODEL, IN_COLS), D_MODEL ** -0.5),
        'lb_logits': nrm(ks[9], (DEPTH + 1, 2, HG_KEYS), 0.3),
        'hg_norm': 1.0 + nrm(ks[10], (DEPTH, HG_VDIM), 0.02),
        'conv_w': nrm(ks[11], (DEPTH, CONV_W, SC_WIDTH), CONV_W ** -0.5),
        'w_out': nrm(ks[12], (DEPTH, MIX_WIDTH, D_MODEL), MIX_WIDTH ** -0.5),
        'w_router': nrm(ks[13], (DEPTH, D_MODEL, N_EXPERTS), D_MODEL ** -0.5),
        'w_gate': nrm(ks[14], (DEPTH, N_EXPERTS, D_MODEL, EXPERT_DFF), D_MODEL ** -0.5),
        'w_up': nrm(ks[15], (DEPTH, N_EXPERTS, D_MODEL, EXPERT_DFF), D_MODEL ** -0.5),
        'w_down': nrm(ks[16], (DEPTH, N_EXPERTS, EXPERT_DFF, D_MODEL), EXPERT_DFF ** -0.5),
        'norm_final': 1.0 + nrm(ks[17], (D_MODEL,), 0.02),
    }

def first_block(x, c, ctx, c_ctx, w_ada, b_ada, norm_mix, norm_ffn, w_in, lb_logits, hg_norm, conv_w,
              w_out, w_router, w_gate, w_up, w_down, norm_final):
    b = x.shape[0]
    rows = x.shape[1] // GRID_W
    lower_bounds = jnp.cumsum(jax.nn.softmax(lb_logits.astype(jnp.float32), axis=0), axis=0)
    cx = ctx
    for l in range(DEPTH):
        sh1, sc1, g1, sh2, sc2, g2 = [m[:, None] for m in adaln(c, w_ada[l], b_ada[l])]
        csh1, csc1, cg1, csh2, csc2, cg2 = adaln(c_ctx, w_ada[l], b_ada[l])
        lb_f, lb_b = lower_bounds[l, 0], lower_bounds[l, 1]
        hc = modulate(rms_norm(cx, norm_mix[l]), csh1, csc1)
        if l == DEPTH - 1:
            zf_f, zf_b, i_c = jnp.split(hc @ w_in[l][:, HG_KEYS:3 * HG_KEYS + HG_WIDTH],
                                        [HG_KEYS, 2 * HG_KEYS], axis=-1)
            s_f, s_b = hgrn2_context_states(zf_f, zf_b, i_c, lb_f, lb_b)
        else:
            zero = jnp.zeros((b, HG_HEADS, HG_KDIM, HG_VDIM), jnp.float32)
            mc, s_f, s_b = token_mix(hc, w_in[l], w_out[l], lb_f, lb_b, hg_norm[l], conv_w[l],
                                     zero, zero, None)
            cx = cx + cg1 * mc
            hc2 = modulate(rms_norm(cx, norm_ffn[l]), csh2, csc2)
            cx = cx + cg2 * expert_choice_ffn(hc2, w_router[l], w_gate[l], w_up[l], w_down[l])
        hx = modulate(rms_norm(x, norm_mix[l]), sh1, sc1)
        mx, _, _ = token_mix(hx, w_in[l], w_out[l], lb_f, lb_b, hg_norm[l], conv_w[l], s_f, s_b, rows)
        x = x + g1 * mx
        hx2 = modulate(rms_norm(x, norm_ffn[l]), sh2, sc2)
        x = x + g2 * expert_choice_ffn(hx2, w_router[l], w_gate[l], w_up[l], w_down[l])
    return rms_norm(x, norm_final)


PLE_DIM = 256
NSA_HEADS = 8
NSA_GROUPS = 2
NSA_HPG = NSA_HEADS // NSA_GROUPS
HEAD_DIM = 64
CMP_LEN = 32
CMP_STRIDE = 16
CMP_HIDDEN = 256
SEL_LEN = 64
SEL_TOP = 16
WINDOW = 512
Q_BLOCK = 128
FORCE_SCORE = 1e4
CONV_CH = 512
CONV_WIDTH = 31
D_FF = 2816
FFN_CONV_WIDTH = 3
NEG = -1e30

NSA_Q = NSA_HEADS * HEAD_DIM
NSA_KV = 3 * 2 * NSA_GROUPS * HEAD_DIM
NSA_GATE = 3 * NSA_HEADS
CONV_IN = 2 * CONV_CH
MERGE = 2 * D_MODEL
N_IN = NSA_Q + NSA_KV + NSA_GATE + CONV_IN + MERGE
IN_SPLITS = (NSA_Q, NSA_Q + NSA_KV, NSA_Q + NSA_KV + NSA_GATE, NSA_Q + NSA_KV + NSA_GATE + CONV_IN)


def rmsnorm(x, g):
    xf = x.astype(jnp.float32)
    y = xf * lax.rsqrt(jnp.mean(xf * xf, axis=-1, keepdims=True) + EPS)
    return (y * g.astype(jnp.float32)).astype(x.dtype)

def layernorm(x, g, b):
    xf = x.astype(jnp.float32)
    mu = jnp.mean(xf, axis=-1, keepdims=True)
    xc = xf - mu
    y = xc * lax.rsqrt(jnp.mean(xc * xc, axis=-1, keepdims=True) + EPS)
    return (y * g.astype(jnp.float32) + b.astype(jnp.float32)).astype(x.dtype)

def causal_dwconv(x, w, b):
    k = w.shape[0]
    c = x.shape[-1]
    y = lax.conv_general_dilated(x, w[:, None, :].astype(x.dtype), window_strides=(1,),
                                 padding=((k - 1, 0),), dimension_numbers=('NWC', 'WIO', 'NWC'),
                                 feature_group_count=c)
    return y + b

def masked_softmax(logits, mask):
    logits = jnp.where(mask, logits.astype(jnp.float32), NEG)
    return jnp.where(mask, jax.nn.softmax(logits, axis=-1), 0.0)

def compress(kv, pos, w1, w2):
    s = kv.shape[2]
    n_cmp = (s - CMP_LEN) // CMP_STRIDE + 1
    idx = np.arange(n_cmp)[:, None] * CMP_STRIDE + np.arange(CMP_LEN)[None, :]
    blocks = kv[:, :, idx] + pos
    flat = blocks.reshape(blocks.shape[0], blocks.shape[1], n_cmp, CMP_LEN * HEAD_DIM)
    return jax.nn.gelu(flat @ w1) @ w2

def cmp_to_sel_matrix(n_cmp, n_sel):
    c0 = np.arange(n_cmp) * CMP_STRIDE
    j0 = np.arange(n_sel) * SEL_LEN
    lo = np.maximum(c0[:, None], j0[None, :])
    hi = np.minimum(c0[:, None] + CMP_LEN, j0[None, :] + SEL_LEN)
    return (np.maximum(hi - lo, 0) / CMP_LEN).astype(np.float32)

def nsa_attention(q, kc, vc, ks, vs, kw, vw):
    b, g, hg, s, dh = q.shape
    scale = dh ** -0.5
    n_cmp = kc.shape[2]
    n_sel = s // SEL_LEN
    top = min(SEL_TOP, n_sel)
    cmp_end = jnp.arange(n_cmp) * CMP_STRIDE + CMP_LEN - 1
    sel_map = jnp.asarray(cmp_to_sel_matrix(n_cmp, n_sel))
    ks_blk = ks.reshape(b, g, n_sel, SEL_LEN, dh)
    vs_blk = vs.reshape(b, g, n_sel, SEL_LEN, dh)
    kw_pad = jnp.pad(kw, ((0, 0), (0, 0), (WINDOW, 0), (0, 0)))
    vw_pad = jnp.pad(vw, ((0, 0), (0, 0), (WINDOW, 0), (0, 0)))
    bi = jnp.arange(b)[:, None, None, None]
    gi = jnp.arange(g)[None, :, None, None]
    jsel = jnp.arange(n_sel)

    def query_block(qb_idx):
        t0 = qb_idx * Q_BLOCK
        qb = lax.dynamic_slice_in_dim(q, t0, Q_BLOCK, axis=3) * scale
        t = t0 + jnp.arange(Q_BLOCK)
        lc = jnp.einsum('bghqd,bgcd->bghqc', qb, kc)
        pc = masked_softmax(lc, cmp_end[None, :] <= t[:, None])
        o_c = jnp.einsum('bghqc,bgcd->bghqd', pc.astype(vc.dtype), vc)
        imp = jnp.einsum('bghqc,cj->bgqj', pc, sel_map)
        cur = (t // SEL_LEN)[:, None]
        forced = (jsel[None, :] == 0) | (jsel[None, :] == cur) | (jsel[None, :] == cur - 1)
        valid = jsel[None, :] <= cur
        imp = jnp.where(valid, jnp.where(forced, FORCE_SCORE, imp), NEG)
        _, sel_idx = lax.top_k(imp, top)
        kg = ks_blk[bi, gi, sel_idx]
        vg = vs_blk[bi, gi, sel_idx]
        ls = jnp.einsum('bghqd,bgqnkd->bghqnk', qb, kg).reshape(b, g, hg, Q_BLOCK, top * SEL_LEN)
        kpos = sel_idx[..., None] * SEL_LEN + jnp.arange(SEL_LEN)
        ms = (kpos <= t[None, None, :, None, None]).reshape(b, g, 1, Q_BLOCK, top * SEL_LEN)
        ps = masked_softmax(ls, ms).reshape(b, g, hg, Q_BLOCK, top, SEL_LEN)
        o_s = jnp.einsum('bghqnk,bgqnkd->bghqd', ps.astype(vg.dtype), vg)
        kwb = lax.dynamic_slice_in_dim(kw_pad, t0, WINDOW + Q_BLOCK, axis=2)
        vwb = lax.dynamic_slice_in_dim(vw_pad, t0, WINDOW + Q_BLOCK, axis=2)
        spos = t0 - WINDOW + jnp.arange(WINDOW + Q_BLOCK)
        dist = t[:, None] - spos[None, :]
        mw = (dist >= 0) & (dist < WINDOW) & (spos[None, :] >= 0)
        lw = jnp.einsum('bghqd,bgkd->bghqk', qb, kwb)
        pw = masked_softmax(lw, mw)
        o_w = jnp.einsum('bghqk,bgkd->bghqd', pw.astype(vwb.dtype), vwb)
        return (o_c, o_s, o_w)

    o_c, o_s, o_w = lax.map(query_block, jnp.arange(s // Q_BLOCK))

    def unblock(o):
        return jnp.transpose(o, (1, 2, 3, 0, 4, 5)).reshape(b, g, hg, s, dh)

    return (unblock(o_c), unblock(o_s), unblock(o_w))

def second_inputs(seed: int = 0) -> dict:
    key = jax.random.key(seed)
    ks = jax.random.split(key, 32)
    f32 = jnp.float32

    def nrm(k, shape, fan_in):
        return jax.random.normal(k, shape, f32) * (fan_in ** -0.5)

    def gain(k, shape):
        return 1.0 + 0.05 * jax.random.normal(k, shape, f32)

    def small(k, shape):
        return 0.02 * jax.random.normal(k, shape, f32)

    L = DEPTH
    return {
        "x": jax.random.normal(ks[0], (BATCH, SEQ, D_MODEL), f32),
        "p": jax.random.normal(ks[1], (DEPTH, BATCH, SEQ, PLE_DIM), f32),
        "g_mix": gain(ks[2], (L, D_MODEL)),
        "w_in": nrm(ks[3], (L, D_MODEL, N_IN), D_MODEL),
        "cmp_pos_k": small(ks[4], (L, CMP_LEN, HEAD_DIM)),
        "cmp_pos_v": small(ks[5], (L, CMP_LEN, HEAD_DIM)),
        "w_cmp_k1": nrm(ks[6], (L, CMP_LEN * HEAD_DIM, CMP_HIDDEN), CMP_LEN * HEAD_DIM),
        "w_cmp_k2": nrm(ks[7], (L, CMP_HIDDEN, HEAD_DIM), CMP_HIDDEN),
        "w_cmp_v1": nrm(ks[8], (L, CMP_LEN * HEAD_DIM, CMP_HIDDEN), CMP_LEN * HEAD_DIM),
        "w_cmp_v2": nrm(ks[9], (L, CMP_HIDDEN, HEAD_DIM), CMP_HIDDEN),
        "w_o_nsa": nrm(ks[10], (L, NSA_Q, D_MODEL), NSA_Q),
        "conv_w": nrm(ks[11], (L, CONV_WIDTH, CONV_CH), CONV_WIDTH),
        "conv_b": small(ks[12], (L, CONV_CH)),
        "conv_ln_g": gain(ks[13], (L, CONV_CH)),
        "conv_ln_b": small(ks[14], (L, CONV_CH)),
        "w_conv_out": nrm(ks[15], (L, CONV_CH, D_MODEL), CONV_CH),
        "b_conv_out": small(ks[16], (L, D_MODEL)),
        "w_out": nrm(ks[17], (L, D_MODEL, D_MODEL), D_MODEL),
        "g_ffn": gain(ks[18], (L, D_MODEL)),
        "w_up": nrm(ks[19], (L, D_MODEL, 2 * D_FF), D_MODEL),
        "ffn_conv_w": nrm(ks[20], (L, FFN_CONV_WIDTH, 2 * D_FF), FFN_CONV_WIDTH),
        "ffn_conv_b": small(ks[21], (L, 2 * D_FF)),
        "w_down": nrm(ks[22], (L, D_FF, D_MODEL), D_FF),
        "g_ple": gain(ks[23], (L, D_MODEL)),
        "w_ple_gate": nrm(ks[24], (L, D_MODEL, D_MODEL), D_MODEL),
        "w_ple": nrm(ks[25], (L, PLE_DIM, D_MODEL), PLE_DIM),
        "g_final": gain(ks[26], (D_MODEL,)),
    }

def second_block(x, p, g_mix, w_in, cmp_pos_k, cmp_pos_v, w_cmp_k1, w_cmp_k2, w_cmp_v1, w_cmp_v2,
              w_o_nsa, conv_w, conv_b, conv_ln_g, conv_ln_b, w_conv_out, b_conv_out, w_out,
              g_ffn, w_up, ffn_conv_w, ffn_conv_b, w_down, g_ple, w_ple_gate, w_ple, g_final):
    b, s, _ = x.shape
    h = x
    for i in range(DEPTH):
        u = rmsnorm(h, g_mix[i])
        z = u @ w_in[i]
        zq, zkv, zg, zc, zm = jnp.split(z, IN_SPLITS, axis=-1)

        q = jnp.transpose(zq.reshape(b, s, NSA_GROUPS, NSA_HPG, HEAD_DIM), (0, 2, 3, 1, 4))
        kv = jnp.transpose(zkv.reshape(b, s, 6, NSA_GROUPS, HEAD_DIM), (2, 0, 3, 1, 4))
        kc = compress(kv[0], cmp_pos_k[i], w_cmp_k1[i], w_cmp_k2[i])
        vc = compress(kv[1], cmp_pos_v[i], w_cmp_v1[i], w_cmp_v2[i])
        o_c, o_s, o_w = nsa_attention(q, kc, vc, kv[2], kv[3], kv[4], kv[5])
        gates = jnp.transpose(jax.nn.sigmoid(zg.reshape(b, s, 3, NSA_GROUPS, NSA_HPG)),
                              (2, 0, 3, 4, 1))[..., None]
        o = gates[0] * o_c + gates[1] * o_s + gates[2] * o_w
        o = jnp.transpose(o, (0, 3, 1, 2, 4)).reshape(b, s, NSA_Q)
        y_a = o @ w_o_nsa[i]

        c_val, c_gate = jnp.split(zc, 2, axis=-1)
        c = c_val * jax.nn.sigmoid(c_gate)
        c = causal_dwconv(c, conv_w[i], conv_b[i])
        c = jax.nn.silu(layernorm(c, conv_ln_g[i], conv_ln_b[i]))
        y_b = c @ w_conv_out[i] + b_conv_out[i]

        ga, gb = jnp.split(jax.nn.sigmoid(zm), 2, axis=-1)
        h = h + (ga * y_a + gb * y_b) @ w_out[i]

        v = rmsnorm(h, g_ffn[i]) @ w_up[i]
        v = causal_dwconv(v, ffn_conv_w[i], ffn_conv_b[i])
        v_gate, v_val = jnp.split(v, 2, axis=-1)
        h = h + (jax.nn.gelu(v_gate) * v_val) @ w_down[i]

        gate = jax.nn.sigmoid(rmsnorm(h, g_ple[i]) @ w_ple_gate[i])
        h = h + gate * (p[i] @ w_ple[i])
    return rmsnorm(h, g_final)


def setup_inputs(seed=0):
    out = dict(first_inputs(seed))
    for name, value in second_inputs(seed + 1).items():
        if name != "x":
            out[name + "_2"] = value
    return out


def reference(
    x, c, ctx, c_ctx, w_ada, b_ada, norm_mix, norm_ffn, w_in, lb_logits, hg_norm, conv_w, w_out,
    w_router, w_gate, w_up, w_down, norm_final, p_2, g_mix_2, w_in_2, cmp_pos_k_2, cmp_pos_v_2,
    w_cmp_k1_2, w_cmp_k2_2, w_cmp_v1_2, w_cmp_v2_2, w_o_nsa_2, conv_w_2, conv_b_2, conv_ln_g_2,
    conv_ln_b_2, w_conv_out_2, b_conv_out_2, w_out_2, g_ffn_2, w_up_2, ffn_conv_w_2,
    ffn_conv_b_2, w_down_2, g_ple_2, w_ple_gate_2, w_ple_2, g_final_2,
):
    x = first_block(
        x, c, ctx, c_ctx, w_ada, b_ada, norm_mix, norm_ffn, w_in, lb_logits, hg_norm, conv_w,
        w_out, w_router, w_gate, w_up, w_down, norm_final,
    )
    return second_block(
        x, p_2, g_mix_2, w_in_2, cmp_pos_k_2, cmp_pos_v_2, w_cmp_k1_2, w_cmp_k2_2, w_cmp_v1_2,
        w_cmp_v2_2, w_o_nsa_2, conv_w_2, conv_b_2, conv_ln_g_2, conv_ln_b_2, w_conv_out_2,
        b_conv_out_2, w_out_2, g_ffn_2, w_up_2, ffn_conv_w_2, ffn_conv_b_2, w_down_2, g_ple_2,
        w_ple_gate_2, w_ple_2, g_final_2,
    )


_drawn_inputs = setup_inputs


def setup_inputs(seed=0):
    import zlib

    import numpy as np

    out = dict(_drawn_inputs(seed))
    spreads = {}
    factors = {'ctx': 7.592,
     'c_ctx': 8.0,
     'norm_mix': 4.583,
     'norm_ffn': 7.118,
     'hg_norm': 8.0,
     'g_mix_2': 2.791,
     'cmp_pos_k_2': 24.063,
     'cmp_pos_v_2': 22.939,
     'conv_b_2': 4.027,
     'conv_ln_g_2': 2.899,
     'conv_ln_b_2': 8.0,
     'b_conv_out_2': 4.956,
     'ffn_conv_b_2': 4.112,
     'g_ple_2': 27.463}
    for name, (base, spread) in spreads.items():
        noise = np.random.default_rng([zlib.crc32(name.encode()), seed]).standard_normal(out[name].shape)
        drawn = base * np.exp(spread * noise) if base else spread * noise
        out[name] = jnp.asarray(drawn.astype(out[name].dtype))
    for name, factor in factors.items():
        out[name] = (out[name] * factor).astype(out[name].dtype)
    return out
```

```python
from contextlib import ExitStack

import concourse.bass as bass
from concourse import mybir

F32 = mybir.dt.float32
I32 = mybir.dt.int32
ALU = mybir.AluOpType
ACT = mybir.ActivationFunctionType
AX = mybir.AxisListType

P = 128
T = 512
D = 1024
NS = 4
SLOT = 4096
EPS = 1e-6
NEG = -1e30


class Lane:

    def __init__(self, sem):
        self.sem, self.n, self.queue, self.seen = sem, 0, [], {}

    def wait(self, *tokens):
        for tok in tokens:
            if tok is None:
                continue
            if isinstance(tok, list):
                self.wait(*tok)
                continue
            sem, value = tok
            if self.seen.get(id(sem), 0) < value:
                self.seen[id(sem)] = value
                self.queue.append(lambda e, sem=sem, value=value: e.wait_ge(sem, value))

    def counted(self, make):
        self.n += 1
        self.queue.append(lambda e, make=make: make(e).then_inc(self.sem, 1))
        return (self.sem, self.n)

    def silent(self, make):
        self.queue.append(lambda e, make=make: make(e))


def build_program(nc, I, out):
    ctx = ExitStack()
    with ctx:
        def sem(name):
            return ctx.enter_context(nc.semaphore(name))

        PE, V, A, G, SP = (Lane(sem(n)) for n in ("s_pe", "s_ve", "s_ac", "s_po", "s_sp"))

        def chained(lane, make, waits, chain=True):
            lane.wait(*waits)
            if chain and lane.n:
                lane.wait((lane.sem, lane.n))
            return lane.counted(make)

        NW = 52960
        arena = ctx.enter_context(nc.sbuf_tensor("arena", [P, NW], F32))
        banks = [ctx.enter_context(nc.psum_tensor(f"bank{i}", [P, 512], F32)) for i in range(8)]
        cursor = [0]

        def mem(n, at=None):
            if at is None:
                at = cursor[0]
                cursor[0] += n
            assert at + n <= NW, (at, n)
            return arena[:, at:at + n]

        def v3(ap, a):
            return ap.rearrange("p (a b) -> p a b", a=a)

        def flat(ap):
            return ap.rearrange("p a b -> p (a b)")

        def now(*lanes):
            return [(l.sem, l.n) for l in lanes if l.n]

        def act(func, o, i, *waits, bias=0.0, scale=1.0, accum=None, chain=True):
            if accum is None:
                return chained(A, lambda e: e.activation(o, i, func, bias=bias, scale=scale), waits, chain)
            return chained(A, lambda e: e.activation(o, i, func, bias=bias, scale=scale, accum_out=accum), waits, chain)

        def tt(o, a, b, op, *waits, chain=True, lane=None):
            return chained(lane or V, lambda e: e.tensor_tensor(o, a, b, op), waits, chain)

        def ts(o, a, s1, s2, op0, op1, *waits, chain=True, lane=None):
            if s2 is None:
                return chained(lane or V, lambda e: e.tensor_scalar(o, a, s1, None, op0), waits, chain)
            return chained(lane or V, lambda e: e.tensor_scalar(o, a, s1, s2, op0, op1), waits, chain)

        def stt(o, a, s, b, op0, op1, *waits, chain=True):
            return chained(V, lambda e: e.scalar_tensor_tensor(out=o, in0=a, scalar=s, in1=b, op0=op0, op1=op1),
                           waits, chain)

        def vcopy(o, i, *waits, chain=True):
            return chained(V, lambda e: e.tensor_copy(o, i), waits, chain)

        def acopy(o, i, *waits, chain=True):
            return chained(A, lambda e: e.activation(o, i, ACT.Copy), waits, chain)

        def vset(o, val, *waits, chain=True):
            return chained(V, lambda e: e.memset(o, val), waits, chain)

        def reduce(o, i, op, *waits):
            return chained(V, lambda e: e.tensor_reduce(o, i, AX.X, op), waits)

        def recip(o, i, *waits):
            return chained(V, lambda e: e.reciprocal(o, i), waits)

        def mms(items, *waits, skip=False):
            PE.wait(*waits)
            for n, (o, l, r, st, sp) in enumerate(items):
                mk = lambda e, o=o, l=l, r=r, st=st, sp=sp: e.matmul(o, l, r, start=st, stop=sp, skip_group_check=skip)
                if n == len(items) - 1:
                    return PE.counted(mk)
                PE.silent(mk)

        def group(o, pairs, *waits):
            last = len(pairs) - 1
            return mms([(o, l, r, n == 0, n == last) for n, (l, r) in enumerate(pairs)], *waits)

        def transposes(items, *waits):
            PE.wait(*waits)
            for n, (o, i) in enumerate(items):
                k = i.shape[0]
                mk = lambda e, o=o, i=i, k=k: e.transpose(o, i, ident[0:k, 0:k])
                if n == len(items) - 1:
                    return PE.counted(mk)
                PE.silent(mk)

        free = [None] * 8
        turn = {"order": list(range(8)), "i": 0}

        def take():
            b = turn["order"][turn["i"] % len(turn["order"])]
            turn["i"] += 1
            PE.wait(free[b])
            return b

        ring = [mem(SLOT) for _ in range(NS)]
        landed = [sem(f"s_w{i}") for i in range(NS)]
        slot_count = [0] * NS
        released = []
        chunks = [0]

        def load(parts):
            c = chunks[0]
            chunks[0] += 1
            s = c % NS
            if c >= NS:
                assert released[c - NS] is not None
                SP.wait(released[c - NS])
            for dst, src in parts(ring[s]):
                slot_count[s] += 16
                SP.silent(lambda e, dst=dst, src=src, s=s: e.dma_start(dst, src).then_inc(landed[s], 16))
            released.append(None)
            return c, ring[s], (landed[s], slot_count[s])

        def cols(w, c0, n):
            def parts(slot):
                dst = slot[:, 0:8 * n].rearrange("p (k n) -> p k n", k=8)
                return [(dst, w[:, c0:c0 + n].rearrange("(k p) n -> p k n", p=P))]
            return parts

        def rows(w, r0, nk):
            def parts(slot):
                dst = slot[:, 0:nk * D].rearrange("p (k n) -> p k n", k=nk)
                return [(dst, w[r0:r0 + nk * P, :].rearrange("(k p) n -> p k n", p=P))]
            return parts

        ident = mem(128)
        onesD = mem(128)
        onesC = mem(128)
        ones256 = mem(256)
        epst = mem(1)
        blkmask = [mem(128) for _ in range(2)]
        resets = mem(T)
        iota1 = mem(64)
        causal = mem(T)
        cmask = v3(mem(4 * 32), 4)
        sel = mem(2)
        PT = v3(mem(5 * 128), 5)
        adaT = mem(96).rearrange("p (t r) -> p t r", r=2)
        mod = v3(mem(3 * 8), 3)
        small = mem(600)
        gainrow = mem(128)
        WR = v3(mem(128), 8)
        W2k, W2v = v3(mem(128), 2), v3(mem(128), 2)
        CP = v3(mem(8 * 32), 8)
        pT = v3(mem(2 * T), 2)
        XT = v3(mem(8 * T), 8)
        M = cursor[0]
        assert NW - M >= 27136, NW - M

        def gp(make, *w):
            return chained(G, make, w)

        def setg(o, val, *w):
            return gp(lambda e: e.memset(o, val), *w)

        def asel(o, op, fill, base, pattern, mult, *w):
            return gp(lambda e: e.affine_select(out=o, in_=o, compare_op=op, fill=fill, base=base,
                                                pattern=pattern, channel_multiplier=mult), *w)

        setg(ident, 0.0)
        t_id = asel(ident, ALU.not_equal, 1.0, 0, [[-1, 128]], 1)
        setg(epst, EPS)
        setg(sel, 0.0)
        for q in range(4):
            t_sel = asel(sel, ALU.not_equal, 1.0, -32 * q, [[-1, 2]], 1)
        setg(onesD, 1.0 / D)
        setg(onesC, 1.0 / 512)
        setg(ones256, 1.0)
        for m in blkmask:
            setg(m, 0.0)
            for c in range(4):
                setg(m[32 * c:32 * c + 32, 32 * c:32 * c + 32], 1.0)
        asel(blkmask[0], ALU.is_ge, 0.0, 0, [[1, 128]], -1)
        asel(blkmask[1], ALU.is_ge, 0.0, 0, [[-1, 128]], 1)
        setg(resets, 1.0)
        setg(resets.rearrange("p (n c) -> p n c", c=32)[:, :, 0:1], 0.0)
        setg(causal, 0.0)
        asel(causal[:, 384:512], ALU.is_ge, NEG, 0, [[-1, 128]], 1)
        setg(flat(cmask), 0.0)
        for t in range(4):
            asel(cmask[:, t, :], ALU.is_ge, NEG, 128 * t - 31, [[-16, 32]], 1)
        setg(cmask[:, :, 31:32], NEG)
        gp(lambda e: e.iota(iota1.bitcast(I32), pattern=[[1, 64]], base=1, channel_multiplier=0))
        t_const = gp(lambda e: e.tensor_copy(iota1, iota1.bitcast(I32)))

        xtok = v3(mem(4 * D, M), 4)
        xn = v3(mem(4 * D, M + 4096), 4)
        ctok = v3(mem(2 * D, M + 8192), 2)
        ptok = v3(mem(4 * 256, M + 10240), 4)
        stage = v3(mem(5 * 128, M + 11264), 5)
        s_st, s_x, s_p = sem("s_st"), sem("s_x"), sem("s_p")
        t_stz = vset(flat(stage), 0.0)
        col, fill_at, n_st = {}, [0] * 5, [0]

        def lrows(name, src, n, tile):
            r0 = fill_at[tile]
            fill_at[tile] += n
            assert fill_at[tile] <= 128
            n_st[0] += 16
            A.silent(lambda e, d=stage[r0:r0 + n, tile, :], s=src: e.dma_start(d, s).then_inc(s_st, 16))
            col[name] = PT[:, tile, r0:r0 + n]

        SP.silent(lambda e: e.dma_start(xtok, I["x"][0].rearrange("(t p) d -> p t d", p=P)).then_inc(s_x, 16))
        SP.silent(lambda e: e.dma_start(ctok, I["ctx"][0].rearrange("(t p) d -> p t d", p=P)).then_inc(s_x, 16))
        A.wait(t_stz)
        R = "(r c) -> r c"
        lrows("c", I["c"][0].rearrange(R, c=P), 8, 0)
        lrows("c_ctx", I["c_ctx"].rearrange(R, c=P), 8, 0)
        lrows("b_ada", I["b_ada"][0].rearrange(R, c=P), 48, 0)
        lrows("norm_mix", I["norm_mix"][0].rearrange(R, c=P), 8, 0)
        lrows("norm_ffn", I["norm_ffn"][0].rearrange(R, c=P), 8, 0)
        lrows("norm_final", I["norm_final"].rearrange(R, c=P), 8, 0)
        lrows("lb", I["lb_logits"].rearrange("a b (r c) -> (a b r) c", c=P), 16, 0)
        lrows("conv_w", I["conv_w"][0].rearrange("k (r c) -> (k r) c", c=P), 12, 0)
        lrows("conv_w_2", I["conv_w_2"][0].rearrange("k (r c) -> (k r) c", c=P), 124, 1)
        lrows("fcw01", I["ffn_conv_w_2"][0][0:2, :].rearrange("k (r c) -> (k r) c", c=P), 88, 2)
        lrows("g_mix", I["g_mix_2"][0].rearrange(R, c=P), 8, 2)
        lrows("conv_b", I["conv_b_2"][0].rearrange(R, c=P), 4, 2)
        lrows("ln_g", I["conv_ln_g_2"][0].rearrange(R, c=P), 4, 2)
        lrows("ln_b", I["conv_ln_b_2"][0].rearrange(R, c=P), 4, 2)
        lrows("b_co", I["b_conv_out_2"][0].rearrange(R, c=P), 8, 2)
        lrows("fcw2", I["ffn_conv_w_2"][0][2:3, :].rearrange("k (r c) -> (k r) c", c=P), 44, 3)
        lrows("fcb", I["ffn_conv_b_2"][0].rearrange(R, c=P), 44, 3)
        lrows("g_ffn", I["g_ffn_2"][0].rearrange(R, c=P), 8, 3)
        lrows("g_ple", I["g_ple_2"][0].rearrange(R, c=P), 8, 3)
        lrows("g_final", I["g_final_2"].rearrange(R, c=P), 8, 3)
        lrows("pos_k", I["cmp_pos_k_2"][0].rearrange("(m l) d -> m (l d)", l=2), 16, 3)
        lrows("pos_v", I["cmp_pos_v_2"][0].rearrange("(m l) d -> m (l d)", l=2), 16, 4)
        for dst, src in (
            (gainrow, I["hg_norm"].to_broadcast([P, 128])),
            (ptok, I["p_2"][0, 0].rearrange("(t p) d -> p t d", p=P)),
            (WR, I["w_router"][0].rearrange("(k p) n -> p k n", p=P)),
            (W2k, I["w_cmp_k2_2"][0].rearrange("(k p) n -> p k n", p=P)),
            (W2v, I["w_cmp_v2_2"][0].rearrange("(k p) n -> p k n", p=P)),
        ):
            A.silent(lambda e, dst=dst, src=src: e.dma_start(dst, src).then_inc(s_p, 16))
        t_stage, t_xin, t_pin = (s_st, n_st[0]), (s_x, 32), (s_p, 80)

        b = take()
        tk = transposes([(banks[b][:, 128 * i:128 * i + 128], stage[:, i, :]) for i in range(4)], t_stage, t_id)
        b2 = take()
        tk2 = transposes([(banks[b2][:, 0:128], stage[:, 4, :])])
        free[b] = vcopy(flat(PT[:, 0:4, :]), banks[b][:, :], tk)
        t_pt = free[b2] = vcopy(PT[:, 4, :], banks[b2][:, 0:128], tk2)

        t_cz = vset(flat(CP), 0.0)
        act(ACT.Silu, CP[:, :, 0], col["c"], t_cz, t_pt)
        t_cp = act(ACT.Silu, CP[:, :, 1], col["c_ctx"])

        adatmp = [mem(512, M + 25600 + 512 * i) for i in range(2)]
        ada_free = [None, None]

        def ada_chunk(c):
            n, slot, arrived = load(cols(I["w_ada"][0], 512 * c, 512))
            w = v3(slot, 8)
            b = take()
            released[n] = tk = mms([(banks[b][32 * (k % 4):32 * (k % 4) + 32, :], CP[:, k, :], w[:, k, :], k < 4, k >= 4)
                                    for k in range(8)], arrived, t_cp)
            free[b] = t1 = acopy(adatmp[c % 2], banks[b][:, :], tk, ada_free[c % 2])
            b = take()
            tk = mms([(banks[b][:, 2 * j:2 * j + 2], adatmp[c % 2][:, 128 * j:128 * j + 128], sel, True, True)
                      for j in range(4)], t1, t_sel)
            ada_free[c % 2] = tk
            bb = col["b_ada"][:, 4 * c:4 * c + 4].unsqueeze(2).to_broadcast([P, 4, 2])
            free[b] = tt(adaT[:, 4 * c:4 * c + 4, :], banks[b][:, 0:8].rearrange("p (t r) -> p t r", r=2), bb,
                         ALU.add, tk, t_pt)
            return free[b]

        for c in range(4):
            ada_chunk(c)
        stt(mod[:, 0, :], adaT[:, 8:16, 0], 1.0, col["norm_mix"], ALU.add, ALU.mult)
        t_mod = stt(mod[:, 1, :], adaT[:, 8:16, 1], 1.0, col["norm_mix"], ALU.add, ALU.mult)

        lb, oml, noml = small[:, 0:8], small[:, 8:16], small[:, 16:24]
        tm, e0, e1 = small[:, 24:32], small[:, 32:40], small[:, 40:48]
        a0, a1 = col["lb"][:, 0:8], col["lb"][:, 8:16]
        tt(tm, a0, a1, ALU.max)
        tt(e0, a0, tm, ALU.subtract)
        t1 = tt(e1, a1, tm, ALU.subtract)
        act(ACT.Exp, e0, e0, t1)
        t1 = act(ACT.Exp, e1, e1)
        tt(tm, e0, e1, ALU.add, t1)
        recip(tm, tm)
        tt(lb, e0, tm, ALU.mult)
        ts(oml, lb, -1.0, 1.0, ALU.mult, ALU.add)
        t_lb = ts(noml, oml, -1.0, None, ALU.mult, None)

        HT = v3(mem(4096, M + 14336), 8)
        HC = v3(mem(2048, M + 18432), 8)
        ss = small[:, 48:54]
        for i in range(6):
            src = xtok[:, i, :] if i < 4 else ctok[:, i - 4, :]
            act(ACT.Square, xn[:, 3, :], src, t_xin, accum=ss[:, i:i + 1])
        t1 = act(ACT.Sqrt, ss, ss, t_const, bias=epst, scale=1.0 / D)
        t_rs = recip(ss, ss, t1)

        def turn_tok(src, t, half, *waits):
            b = take()
            tk = transposes([(banks[b][:, 128 * j:128 * j + 128],
                              src[:, t, 512 * half + 128 * j:512 * half + 128 * j + 128]) for j in range(4)], *waits)
            return b, tk

        for t in range(4):
            for half in range(2):
                b, tk = turn_tok(xtok, t, half, t_xin)
                free[b] = (vcopy if half else acopy)(XT[:, 4 * half:4 * half + 4, 128 * t:128 * t + 128],
                                                     v3(banks[b][:, :], 4), tk)
        for t in range(4):
            t1 = ts(xn[:, t, :], xtok[:, t, :], ss[:, t:t + 1], None, ALU.mult, None, t_rs)
            for half in range(2):
                b, tk = turn_tok(xn, t, half, t1)
                for j in range(4):
                    d = 4 * half + j
                    o, i_ = HT[:, d, 128 * t:128 * t + 128], banks[b][:, 128 * j:128 * j + 128]
                    if half:
                        free[b] = act(ACT.Identity, o, i_, tk, t_mod, scale=mod[:, 0, d:d + 1], bias=adaT[:, d, 0:1],
                                      chain=(j == 0))
                    else:
                        free[b] = ts(o, i_, mod[:, 0, d:d + 1], adaT[:, d, 0:1], ALU.mult, ALU.add, tk, chain=(j == 0))
        t_ht = now(V, A)
        for t in range(2):
            t1 = ts(ctok[:, t, :], ctok[:, t, :], ss[:, 4 + t:5 + t], None, ALU.mult, None)
            for half in range(2):
                b, tk = turn_tok(ctok, t, half, t1)
                for j in range(4):
                    d = 4 * half + j
                    free[b] = act(ACT.Identity, HC[:, d, 128 * t:128 * t + 128], banks[b][:, 128 * j:128 * j + 128],
                                  tk, t_mod, scale=mod[:, 1, d:d + 1], bias=adaT[:, d, 1:2], chain=(j == 0))
        t_hc = now(A)
        for j in range(2):
            b = take()
            tk = transposes([(banks[b][:, 128 * t:128 * t + 128], ptok[:, t, 128 * j:128 * j + 128])
                             for t in range(4)], t_pin)
            free[b] = acopy(pT[:, j, :], banks[b][:, :], tk)
        t_pre = now(V, A, PE)

        def proj(src, slot, n, j, *waits):
            w = slot[:, 0:8 * n].rearrange("p (k n) -> p k n", k=8)
            b = take()
            return b, group(banks[b][:, :], [(w[:, k, 128 * j:128 * j + 128], src[:, k, :]) for k in range(8)], *waits)

        def projtok(src, slot, n, c0, nc_, t, *waits):
            w = slot[:, 0:8 * n].rearrange("p (k n) -> p k n", k=8)
            b = take()
            return b, group(banks[b][:, 0:nc_], [(src[:, k, 128 * t:128 * t + 128], w[:, k, c0:c0 + nc_])
                                                 for k in range(8)], *waits)

        win = I["w_in"][0]
        gA, gB, gD, gE = (v3(mem(2048, M + 2048 * i), 4) for i in range(4))
        qT = v3(mem(2048, M + 8192), 4)
        vtok = v3(mem(2048, M + 10240), 4)
        gtok = v3(mem(2048, M + 12288), 4)
        S0 = mem(1024, M + 20480).rearrange("p (d h v) -> p d h v", d=2, h=4)
        U = v3(mem(2048, M + 21504), 4)
        Sring = mem(1024, M + 23552).rearrange("p (r h v) -> p r h v", r=2, h=4)
        scT = [mem(512, M + 24576 + 512 * i) for i in range(2)]
        dec = small[:, 54:118].rearrange("p (h n) -> p h n", h=4)
        last = small[:, 118:122]
        cA, cB = v3(mem(1024, M + 4096), 4), v3(mem(1024, M + 5120), 4)
        cK, vctx = v3(mem(1024, M + 6144), 2), v3(mem(1024, M + 7168), 2)
        gK = [gA, U]

        turn["order"] = [4, 5, 6, 7]

        def gate_scalars(d, h):
            i = 4 * d + h
            return lb[:, i:i + 1], oml[:, i:i + 1], noml[:, i:i + 1]

        def ctx_gate(slot, arrived, d, *waits):
            w = v3(slot, 8)
            for h2 in range(2):
                b = take()
                tk = mms([(banks[b][:, 256 * hh:256 * hh + 256], w[:, k, 256 * h2 + 128 * hh:256 * h2 + 128 * hh + 128],
                           HC[:, k, :], k == 0, k == 7) for hh in range(2) for k in range(8)], arrived, t_hc)
                free[b] = act(ACT.Sigmoid, cA[:, 2 * h2:2 * h2 + 2, :], v3(banks[b][:, :], 2), tk, *waits)
            for h in range(4):
                l_, o_, _ = gate_scalars(d, h)
                t1 = act(ACT.Ln, cB[:, h, :], cA[:, h, :], t_lb, *waits, scale=o_, bias=l_)
            for h in range(4):
                _, o_, n_ = gate_scalars(d, h)
                x_ = cB[:, h, ::-1] if d else cB[:, h, :]
                chained(V, lambda e, x_=x_: e.tensor_tensor_scan(x_, ones256, x_, 0.0, ALU.mult, ALU.add), (t1, t_const))
                ts(cA[:, h, :], cA[:, h, :], n_, o_, ALU.mult, ALU.add)
            t2 = vcopy(last, cB[:, :, 0 if d else 255])
            for h in range(4):
                t3 = act(ACT.Exp, cB[:, h, :], cB[:, h, :], t2, scale=-1.0, bias=last[:, h:h + 1])
            t4 = tt(cA, cA, cB, ALU.mult, t3)
            for t in range(2):
                b = take()
                tk = transposes([(banks[b][:, 128 * h:128 * h + 128], cA[:, h, 128 * t:128 * t + 128])
                                 for h in range(4)], t4)
                free[b] = vcopy(cK[:, t, :], banks[b][:, :], tk)
            return free[b]

        def ctx_state(d, t_k, t_vc):
            b = take()
            tk = mms([(banks[b][:, 128 * h:128 * h + 128], cK[:, t, 128 * h:128 * h + 128],
                       vctx[:, t, 128 * h:128 * h + 128], t == 0, t == 1) for h in range(4) for t in range(2)], t_k, t_vc)
            free[b] = vcopy(S0[:, d, :, :].rearrange("p h v -> p (h v)"), banks[b][:, :], tk)
            return free[b]

        def gates_math(d, t_sig, t_q, *waits):
            K = gK[d]
            for h in range(4):
                l_, o_, _ = gate_scalars(d, h)
                t1 = act(ACT.Ln, gB[:, h, :], K[:, h, :], t_sig, *waits, scale=o_, bias=l_)
            for h in range(4):
                _, o_, n_ = gate_scalars(d, h)
                x_ = gB[:, h, ::-1] if d else gB[:, h, :]
                chained(V, lambda e, x_=x_: e.tensor_tensor_scan(x_, resets, x_, 0.0, ALU.mult, ALU.add),
                        (t1, t_const, *waits))
                t2 = ts(K[:, h, :], K[:, h, :], n_, o_, ALU.mult, ALU.add)
            act(ACT.Exp, dec, gB.rearrange("p h (n c) -> p h n c", c=32)[:, :, :, 0 if d else 31], t2)
            t_e = act(ACT.Exp, gE, gB, scale=-1.0)
            t_d = act(ACT.Exp, gD, gB)
            tt(gE, gE, K, ALU.mult, t_e)
            tt(gD, gD, qT, ALU.mult, t_d, t_q)
            db = dec.rearrange("p h n -> p (h n)").unsqueeze(2).to_broadcast([P, 64, 32])
            return tt(K.rearrange("p h (n c) -> p (h n) c", c=32), gE.rearrange("p h (n c) -> p (h n) c", c=32), db,
                      ALU.mult)

        fillers = []

        def fill(n=1):
            for _ in range(n):
                if fillers:
                    fillers.pop(0)()

        def gla(d, t_gates, t_v):
            K = gK[d]
            for t in range(4):
                b = take()
                tk = transposes([(banks[b][:, 128 * h:128 * h + 128], K[:, h, 128 * t:128 * t + 128])
                                 for h in range(4)], t_gates)
                free[b] = t_kt = vcopy(gB[:, t, :], banks[b][:, :], tk)
            for i in range(2):
                vset(scT[i], 0.0, *now(PE))
            read = [None, None]
            for t in range(4):
                b = take()
                s_ = slice(128 * t, 128 * t + 128)
                tk = mms([(banks[b][:, 128 * h:128 * h + 128], gE[:, h, s_], gD[:, h, s_], True, True)
                          for h in range(4)], t_gates)
                mk = blkmask[d].bitcast(I32).unsqueeze(1).to_broadcast([P, 4, 128])
                sc, bk = v3(scT[t % 2], 4), v3(banks[b][:, :], 4)
                free[b] = chained(V, lambda e, sc=sc, mk=mk, bk=bk: e.copy_predicated(sc, mk, bk),
                                  (tk, t_const, read[t % 2]))
                read[t % 2] = tk = mms([(banks[t][:, 128 * h:128 * h + 128], scT[t % 2][:, 128 * h:128 * h + 128],
                                         vtok[:, t, 128 * h:128 * h + 128], d == 0 and h == 0, False)
                                        for h in range(4)], free[b], t_v, skip=True)
            prev, t_prev = S0[:, d, :, :], t_s0[d]
            ring_read = [None, None]
            for i, n in enumerate(range(15, -1, -1) if d else range(16)):
                t, c = n // 4, n % 4
                pp = slice(32 * c, 32 * c + 32)
                if i < 15:
                    b = take()
                    tkv = mms([(banks[b][:, 128 * h:128 * h + 128], gB[pp, t, 128 * h:128 * h + 128],
                                vtok[pp, t, 128 * h:128 * h + 128], True, True) for h in range(4)], t_kt, t_v)
                tk = mms([(banks[t][pp, 128 * h:128 * h + 128], gD[:, h, 32 * n:32 * n + 32], prev[:, h, :],
                           False, False) for h in range(4)], t_prev, skip=True)
                if i > 0:
                    ring_read[(i - 1) % 2] = tk
                if i < 15:
                    nxt = Sring[:, i % 2, :, :]
                    V.wait(*now(V))
                    for h in range(4):
                        t_prev = stt(nxt[:, h, :], prev[:, h, :], dec[:, h, n:n + 1],
                                     banks[b][:, 128 * h:128 * h + 128], ALU.mult, ALU.add, tkv,
                                     ring_read[i % 2], chain=False)
                    free[b] = t_prev
                    prev = nxt
                if i % 2 == 1:
                    fill()
            return tk

        t_s0 = [None, None]
        n, slot, arrived = load(cols(win, 512, 512))
        t_k0 = ctx_gate(slot, arrived, 0, *t_pre)
        for h in range(4):
            b, tk = proj(HT, slot, 512, h, *t_ht)
            free[b] = t_sig = act(ACT.Sigmoid, gA[:, h, :], banks[b][:, :], tk, *t_pre)
        released[n] = tk
        n, slot, arrived = load(cols(win, 1536, 512))
        for t in range(2):
            b, tk = projtok(HC, slot, 512, 0, 512, t, arrived)
            free[b] = t_vc = acopy(vctx[:, t, :], banks[b][:, :], tk)
        for t in range(4):
            b, tk = projtok(HT, slot, 512, 0, 512, t)
            free[b] = t_v = acopy(vtok[:, t, :], banks[b][:, :], tk)
        released[n] = tk
        t_s0[0] = ctx_state(0, t_k0, t_vc)
        n, slot, arrived = load(cols(win, 1024, 512))
        t_k1 = ctx_gate(slot, arrived, 1, t_s0[0])
        for h in range(4):
            b, tk = proj(HT, slot, 512, h)
            free[b] = t_sigb = act(ACT.Sigmoid, U[:, h, :], banks[b][:, :], tk)
        released[n] = tk
        t_s0[1] = ctx_state(1, t_k1, t_vc)
        n, slot, arrived = load(cols(win, 0, 512))
        for h in range(4):
            b, tk = proj(HT, slot, 512, h, arrived)
            free[b] = t_q = acopy(qT[:, h, :], banks[b][:, :], tk)
        released[n] = tk
        t_g0 = gates_math(0, t_sig, t_q, t_s0[1])
        n, slot, arrived = load(cols(win, 2048, 512))
        grow = gainrow.unsqueeze(1).to_broadcast([P, 4, 128])
        for t in range(4):
            b, tk = projtok(HT, slot, 512, 0, 512, t, arrived)
            free[b] = t1 = act(ACT.Silu, gtok[:, t, :], banks[b][:, :], tk)
            tt(v3(gtok[:, t, :], 4), v3(gtok[:, t, :], 4), grow, ALU.mult, t1, t_pin)
        released[n] = tk

        u, ymix = v3(mem(2048, M + 18432), 4), gA
        cur = {}
        gt_read = [None, None]

        def conv_a(j, which):
            def run():
                if j == 0:
                    cur[which] = load(cols(win, {"c": 3072, "v": 3584, "b": 2560}[which], 512))
                n, slot, arrived = cur[which]
                b, tk = proj(HT, slot, 512, j, arrived)
                if j == 3:
                    released[n] = tk
                if which == "c":
                    free[b] = cur["gc", j] = acopy(u[:, j, :], banks[b][:, :], tk, t_s0[1])
                elif which == "v":
                    free[b] = tt(u[:, j, :], banks[b][:, :], u[:, j, :], ALU.mult, tk, cur["gc", j])
                    cw = col["conv_w"]
                    y, x_ = (z.rearrange("p (r c) -> p r c", c=64) for z in (ymix[:, j, :], u[:, j, :]))
                    ts(ymix[:, j, :], u[:, j, :], cw[:, 4 + j:5 + j], None, ALU.mult, None, cur["ga"])
                    stt(y[:, :, 1:64], x_[:, :, 0:63], cw[:, j:j + 1], y[:, :, 1:64], ALU.mult, ALU.add)
                    stt(y[:, :, 0:63], x_[:, :, 1:64], cw[:, 8 + j:9 + j], y[:, :, 0:63], ALU.mult, ALU.add)
                else:
                    free[b] = cur["y"] = tt(ymix[:, j, :], banks[b][:, :], ymix[:, j, :], ALU.mult, tk)
            return run

        def ada_late(c):
            def run():
                cur["ada"] = ada_chunk(c)
            return run

        fillers += [conv_a(j, "c") for j in range(4)] + [ada_late(c) for c in range(4, 8)]
        gla(0, t_g0, t_v)
        fill(8)
        cur["ga"] = now(PE)[0]
        t_g1 = gates_math(1, t_sigb, t_q, *now(PE))
        for j in range(4):
            conv_a(j, "v")()
        fillers += [conv_a(j, "b") for j in range(4)] + [ada_late(c) for c in range(8, 12)]
        t_gla = gla(1, t_g1, t_v)
        fill(8)

        osb = gE
        ssq = small[:, 122:138]
        sq = v3(mem(2048, M + 2048), 4)
        t_ = now(PE)
        for t in range(4):
            free[t] = acopy(osb[:, t, :], banks[t][:, :], t_gla, *t_)
        t1 = act(ACT.Square, flat(sq), flat(osb))
        reduce(ssq, sq.rearrange("p t (h v) -> p (t h) v", h=4), ALU.add, t1)
        t1 = act(ACT.Sqrt, ssq, ssq, *now(V), bias=epst, scale=1.0 / 128)
        recip(ssq, ssq, t1)
        o16 = osb.rearrange("p t (h v) -> p (t h) v", h=4)
        tt(o16, o16, ssq.unsqueeze(2).to_broadcast([P, 16, 128]), ALU.mult)
        t1 = tt(flat(osb), flat(osb), flat(gtok), ALU.mult)
        turn["order"] = list(range(8))
        for t in range(4):
            b = take()
            tk = transposes([(banks[b][:, 128 * h:128 * h + 128], osb[:, t, 128 * h:128 * h + 128])
                             for h in range(4)], t1)
            free[b] = t_mix = acopy(gD[:, :, 128 * t:128 * t + 128], v3(banks[b][:, :], 4), tk)
        mix = [gD[:, k, :] for k in range(4)] + [ymix[:, k, :] for k in range(4)]
        t_xt = [None] * 8
        for half in range(2):
            n, slot, arrived = load(cols(I["w_out"][0], 512 * half, 512))
            w = v3(slot, 8)
            for j in range(4):
                d = 4 * half + j
                b = take()
                tk = group(banks[b][:, :], [(w[:, k, 128 * j:128 * j + 128], mix[k]) for k in range(8)],
                           arrived, t_mix, cur["y"])
                free[b] = t_xt[d] = stt(XT[:, d, :], banks[b][:, :], adaT[:, 16 + d, 0:1], XT[:, d, :],
                                        ALU.mult, ALU.add, tk, cur["ada"])
            released[n] = tk

        sqt = [mem(512, M + 18432 + 512 * i) for i in range(2)]
        rstd = mem(512, M + 19456)

        def rms(t_x, *waits):
            b = take()
            read = [None, None]
            for d in range(8):
                t1 = act(ACT.Square, sqt[d % 2], XT[:, d, :], t_x[d], read[d % 2], *waits)
                read[d % 2] = tk = mms([(banks[b][:, :], onesD, sqt[d % 2], d == 0, d == 7)], t1)
            act(ACT.Ln, rstd, banks[b][:, :], tk, bias=epst)
            t1 = act(ACT.Exp, rstd, rstd, scale=-0.5)
            free[b] = t1
            return t1

        def scaled(o, gain, t_r, *waits):
            toks = []
            for d in range(8):
                toks.append(stt(o[:, d, :], XT[:, d, :], gain[:, d:d + 1], rstd, ALU.mult, ALU.mult, t_r, *waits,
                                chain=(d == 0)))
            return toks

        t1 = stt(mod[:, 2, :], adaT[:, 32:40, 0], 1.0, col["norm_ffn"], ALU.add, ALU.mult)
        t_r = rms(t_xt, *now(PE))
        toks = scaled(HT, mod[:, 2, :], t_r, *now(PE))
        t_h = []
        for d in range(8):
            t_h.append(act(ACT.Identity, HT[:, d, :], HT[:, d, :], toks[d], bias=adaT[:, 24 + d, 0:1], chain=(d == 0)))
        b = take()
        tk = mms([(banks[b][:, 16 * t:16 * t + 16], HT[:, k, 128 * t:128 * t + 128], WR[:, k, :], k == 0, k == 7)
                  for t in range(4) for k in range(8)], *t_h, t_pin)
        aff = v3(mem(64, M + 20000), 4)
        slotT = v3(mem(64, M + 20064), 4)
        red = small[:, 138:142]
        rb = red.unsqueeze(2).to_broadcast([P, 4, 16])
        free[b] = vcopy(flat(aff), banks[b][:, 0:64], tk)
        reduce(red, aff, ALU.max)
        t1 = tt(aff, aff, rb, ALU.subtract)
        t1 = act(ACT.Exp, flat(aff), flat(aff), t1)
        reduce(red, aff, ALU.add, t1)
        recip(red, red)
        t1 = tt(aff, aff, rb, ALU.mult)
        b = take()
        tk = transposes([(banks[b][0:16, 128 * t:128 * t + 128], aff[:, t, :]) for t in range(4)], t1)
        wk = [mem(512, M + 20480 + 512 * i)[0:16, :] for i in range(2)]
        top = small[0:16, 144:208]
        free[b] = vcopy(wk[0], banks[b][0:16, :], tk)
        for r in range(8):
            o8 = top[:, 8 * r:8 * r + 8]
            chained(V, lambda e, o8=o8, s=wk[r % 2]: e.max(o8, s), ())
            chained(V, lambda e, o8=o8, s=wk[r % 2], o=wk[1 - r % 2]:
                    e.match_replace(out=o, in_to_replace=o8, in_values=s, imm_value=-1.0), ())
        ts(wk[0], wk[0], 0.0, None, ALU.is_lt, None)
        ones_row = mem(512, M + 21504)[0:16, :]
        vset(ones_row, 1.0)
        chained(V, lambda e: e.tensor_tensor_scan(wk[1], ones_row, wk[0], 0.0, ALU.mult, ALU.add), ())
        t1 = tt(wk[1], wk[1], wk[0], ALU.mult)

        H2 = v3(mem(4096, M), 4)
        for t in range(4):
            for half in range(2):
                b = take()
                tk = transposes([(banks[b][:, 128 * j:128 * j + 128], HT[:, 4 * half + j, 128 * t:128 * t + 128])
                                 for j in range(4)])
                free[b] = t_h2 = acopy(H2[:, t, 512 * half:512 * half + 512], banks[b][:, :], tk)
        b = take()
        tk = transposes([(banks[b][:, 16 * t:16 * t + 16], wk[1][:, 128 * t:128 * t + 128]) for t in range(4)], t1)
        free[b] = t_slot = vcopy(flat(slotT), banks[b][:, 0:64], tk)
        t_rt = now(V, A, PE)

        xsT = [v3(mem(1024, M + 4096 + 1024 * i), 8) for i in range(2)]
        Sp = [v3(mem(512, M + 6144 + 512 * i), 4) for i in range(2)]
        Sg = [v3(mem(512, M + 7168 + 512 * i), 4) for i in range(2)]
        SgT = [mem(512, M + 8192 + 512 * i) for i in range(2)]
        ab = [mem(2048, M + 9216), mem(2048, M + 21504)]
        hT = [v3(mem(2048, M + 11264), 16), v3(mem(2048, M + 23552), 16)]
        ys = mem(1024, M + 13312)
        stm = [mem(512, M + 14336 + 512 * i) for i in range(2)]
        xs_read, sp_read, sg_read, sgt_read = [None] * 2, [None] * 2, [None] * 2, [None] * 2
        ab_read, h_read, stm_read = [None] * 2, [None] * 2, [None] * 2
        ys_read = [None]
        gathered = {}

        def gather(p):
            i = p % 2
            s4 = Sp[i].rearrange("p t (e s) -> p t e s", e=2)
            g4 = Sg[i].rearrange("p t (e s) -> p t e s", e=2)
            io = iota1.unsqueeze(1).unsqueeze(1).to_broadcast([P, 4, 2, 64])
            sl = slotT[:, :, 2 * p:2 * p + 2].unsqueeze(3).to_broadcast([P, 4, 2, 64])
            af = aff[:, :, 2 * p:2 * p + 2].unsqueeze(3).to_broadcast([P, 4, 2, 64])
            t1 = tt(s4, io, sl, ALU.is_equal, *t_rt, sp_read[i])
            t2 = tt(g4, s4, af, ALU.mult, sg_read[i])
            for half in range(2):
                b = take()
                tk = mms([(banks[b][:, 128 * j:128 * j + 128],
                           H2[:, t, 512 * half + 128 * j:512 * half + 128 * j + 128], Sp[i][:, t, :], t == 0, t == 3)
                          for j in range(4) for t in range(4)], t1, t_h2)
                free[b] = t_x = vcopy(flat(xsT[i][:, 4 * half:4 * half + 4, :]), banks[b][:, :], tk, xs_read[i])
            sp_read[i] = tk
            b = take()
            sg_read[i] = tk = transposes([(banks[b][:, 128 * t:128 * t + 128], Sg[i][:, t, :]) for t in range(4)], t2)
            free[b] = t_s = vcopy(SgT[i], banks[b][:, :], tk, sgt_read[i])
            gathered[p] = (t_x, t_s)

        def pair_chunks(w, p, parts):
            a, b_ = load(parts(w[0, 2 * p])), load(parts(w[0, 2 * p + 1]))
            return a, b_

        def up(w, p, fc):
            (n0, s0_, a0_), (n1, s1_, a1_) = pair_chunks(w, p, lambda x_: cols(x_, 512 * fc, 512))
            b = take()
            ws = [v3(s0_, 8), v3(s1_, 8)]
            items = [(banks[b][64 * e:64 * e + 64, :], xsT[p % 2][:, k, 64 * e:64 * e + 64], ws[e][:, k, :],
                      k == 0, k == 7) for k in range(8) for e in range(2)]
            tk = mms(items, a0_, a1_, gathered[p][0])
            released[n0] = released[n1] = tk
            return b, tk

        def turn_h(p, fc, t_a):
            b = take()
            tk = transposes([(banks[b][:, 128 * j:128 * j + 128], ab[p % 2][:, 512 * fc + 128 * j:512 * fc + 128 * j + 128])
                             for j in range(4)], t_a)
            free[b] = vcopy(flat(hT[p % 2][:, 4 * fc:4 * fc + 4, :]), banks[b][:, :], tk, h_read[p % 2])
            return tk, free[b]

        gather(0)
        for p in range(8):
            i = p % 2
            late = None
            for fc in range(4):
                b, tk = up(I["w_gate"], p, fc)
                free[b] = t1 = act(ACT.Silu, stm[fc % 2], banks[b][:, :], tk, stm_read[fc % 2])
                b, tk = up(I["w_up"], p, fc)
                free[b] = t_a = tt(ab[i][:, 512 * fc:512 * fc + 512], banks[b][:, :], stm[fc % 2], ALU.mult, tk, t1,
                                   ab_read[i])
                stm_read[fc % 2] = t_a
                if late is not None:
                    turn_h(p, fc - 1, late)
                late = t_a
            xs_read[i] = tk
            if p < 7:
                gather(p + 1)
            ab_read[i], t_hid = turn_h(p, 3, late)
            yb = [take(), take()]
            for kc in range(4):
                (n0, s0_, a0_), (n1, s1_, a1_) = pair_chunks(I["w_down"], p, lambda x_: rows(x_, 512 * kc, 4))
                ws = [v3(s0_, 4), v3(s1_, 4)]
                tk = mms([(banks[yb[f]][64 * e:64 * e + 64, :], hT[i][:, 4 * kc + k, 64 * e:64 * e + 64],
                           ws[e][:, k, 512 * f:512 * f + 512], kc + k == 0, kc == 3 and k == 3)
                          for k in range(4) for f in range(2) for e in range(2)], a0_, a1_, t_hid)
                released[n0] = released[n1] = tk
            h_read[i] = tk
            free[yb[0]] = acopy(ys[:, 0:512], banks[yb[0]][:, :], tk, ys_read[0])
            free[yb[1]] = t_y = acopy(ys[:, 512:1024], banks[yb[1]][:, :], tk)
            for d in range(8):
                b = take()
                tk = mms([(banks[b][:, :], ys[:, 128 * d:128 * d + 128], SgT[i], True, True)], t_y, gathered[p][1])
                free[b] = t_xt[d] = stt(XT[:, d, :], banks[b][:, :], adaT[:, 40 + d, 0:1], XT[:, d, :],
                                        ALU.mult, ALU.add, tk)
            ys_read[0] = sgt_read[i] = tk

        t_r = rms(t_xt, *now(PE))
        toks = scaled(XT, col["norm_final"], t_r)

        UT = HT
        win2 = I["w_in_2"][0]
        t_r = rms(toks, *now(V))
        t_u = scaled(UT, col["g_mix"], t_r, *now(PE))
        q2 = v3(mem(2048, M), 4)
        KZ = mem(2048, M + 2048).rearrange("p (b g t) -> p b g t", b=2, g=2)
        VS = mem(1024, M + 4096).rearrange("p (b t n) -> p b t n", b=2, t=4)
        OT = v3(mem(2048, M + 5120), 4)
        kcat = [v3(mem(1024, M + 7168 + 1024 * i), 2) for i in range(2)]
        pcT = v3(mem(1024, M + 9216), 2)
        CO = v3(mem(2048, M + 10240), 4)
        CI = v3(mem(2048, M + 12288), 4)
        vt = [mem(512, M + 20480 + 512 * i) for i in range(2)]
        t_b2 = now(PE, A)

        n, slot, arrived = load(cols(win2, 1816, 512))
        for j in range(4):
            b, tk = proj(UT, slot, 512, j, arrived, *t_u)
            free[b] = t_cg = act(ACT.Sigmoid, CO[:, j, :], banks[b][:, :], tk)
        released[n] = tk
        n, slot, arrived = load(cols(win2, 1304, 512))
        for j in range(4):
            b, tk = proj(UT, slot, 512, j, arrived)
            free[b] = t_ci = tt(CI[:, j, :], banks[b][:, :], CO[:, j, :], ALU.mult, tk, t_cg, *t_b2)
        released[n] = tk
        vset(KZ.rearrange("p b g t -> p (b g t)"), 0.0)
        KC = v3(small_kc := small[:, 208:272], 2)
        HID = small[:, 272:400].rearrange("p (h g n) -> p h g n", h=2, g=2)
        VC = v3(small[:, 400:528], 2)
        vset(small_kc, 0.0)
        vset(small[:, 272:400], 0.0)

        taps = []
        cw2 = col["conv_w_2"]
        for j in range(4):
            def first(j=j):
                return ts(CO[:, j, :], CI[:, j, :], cw2[:, 120 + j:121 + j], col["conv_b"][:, j:j + 1],
                          ALU.mult, ALU.add)
            taps.append(first)
            for s in range(1, 31):
                def tap(j=j, s=s):
                    k = 4 * (30 - s) + j
                    return stt(CO[:, j, s:], CI[:, j, :T - s], cw2[:, k:k + 1], CO[:, j, s:], ALU.mult, ALU.add)
                taps.append(tap)

        def conv_taps(n):
            for _ in range(n):
                if taps:
                    cur["conv"] = taps.pop(0)()

        n, slot, arrived = load(cols(win2, 512, 512))
        for w_ in range(2):
            b, tk = proj(UT, slot, 512, w_, arrived)
            for g in range(2):
                for l2 in range(2):
                    free[b] = t_kc = acopy(kcat[w_][64 * l2:64 * l2 + 64, g, 0:512 - l2],
                                           banks[b][64 * g:64 * g + 64, l2:512], tk, *t_b2)
        b, tk = proj(UT, slot, 512, 2)
        for g in range(2):
            free[b] = acopy(KZ[64 * g:64 * g + 64, 0, g, :], banks[b][64 * g:64 * g + 64, :], tk, *now(V))
        for t in range(4):
            b, tk = projtok(UT, slot, 512, 384, 128, t)
            free[b] = acopy(VS[:, 0, t, :], banks[b][:, 0:128], tk)
        released[n] = tk
        conv_taps(40)
        n, slot, arrived = load(cols(win2, 1024, 280))
        b, tk = proj(UT, slot, 280, 0, arrived)
        for g in range(2):
            free[b] = acopy(KZ[64 * g:64 * g + 64, 1, g, :], banks[b][64 * g:64 * g + 64, :], tk)
        for t in range(4):
            b, tk = projtok(UT, slot, 280, 128, 128, t)
            free[b] = acopy(VS[:, 1, t, :], banks[b][:, 0:128], tk)
        GT = small_gt = v3(mem(96, M + 27500 - 512), 4)
        for t in range(4):
            b, tk = projtok(UT, slot, 280, 256, 24, t)
            free[b] = t_gt = act(ACT.Sigmoid, GT[:, t, :], banks[b][:, 0:24], tk)
        released[n] = tk

        def qparts(slot):
            dst = slot.rearrange("p (k i g c) -> p k i g c", k=8, i=4, g=2)
            return [(dst[:, :, i, g, :], win2[:, 256 * g + 64 * i:256 * g + 64 * i + 64].rearrange("(k p) c -> p k c", p=P))
                    for g in range(2) for i in range(4)]
        n, slot, arrived = load(qparts)
        w = v3(slot, 8)
        for i in range(4):
            b = take()
            tk = group(banks[b][:, :], [(w[:, k, 128 * i:128 * i + 128], UT[:, k, :]) for k in range(8)], arrived)
            free[b] = t_q2 = act(ACT.Copy, q2[:, i, :], banks[b][:, :], tk, scale=0.125)
        released[n] = tk
        conv_taps(40)

        RB = mem(992, M + 21504).rearrange("p (m g n) -> p m g n", m=16, g=2)
        t_rb = None
        for w_, (w1, pos) in enumerate(((I["w_cmp_k1_2"], col["pos_k"]), (I["w_cmp_v1_2"], col["pos_v"]))):
            for m in range(16):
                src = kcat[w_][:, :, 2 * m:2 * m + 481:16]
                t1 = ts(RB[:, m, :, :], src, pos[:, m:m + 1], None, ALU.add, None, t_kc, t_rb, *t_b2, chain=(m == 0))

            def w1parts(slot, w1=w1):
                return [(slot.rearrange("p (m n) -> p m n", m=16), w1[0].rearrange("(m p) n -> p m n", p=P))]
            n, slot, arrived = load(w1parts)
            w = v3(slot, 16)
            b = take()
            tk = mms([(banks[b][:, 64 * h:64 * h + 62], w[:, m, 128 * h:128 * h + 128],
                       RB[:, m, :, :].rearrange("p g n -> p (g n)"), m == 0, m == 15)
                      for h in range(2) for m in range(16)], arrived, t1)
            t_rb = released[n] = tk
            for h in range(2):
                free[b] = t1 = act(ACT.Gelu_apprx_tanh, HID[:, h, :, 0:31],
                                   v3(banks[b][:, 64 * h:64 * h + 62], 2), tk, *now(V), *now(PE))
            b = take()
            if w_ == 0:
                tk = mms([(banks[b][64 * g:64 * g + 64, 0:32], W2k[:, h, :], HID[:, h, g, :], h == 0, h == 1)
                          for g in range(2) for h in range(2)], t1, t_pin)
                for g in range(2):
                    free[b] = t_kcz = vcopy(KC[64 * g:64 * g + 64, g, :], banks[b][64 * g:64 * g + 64, 0:32], tk)
            else:
                tk = mms([(banks[b][0:32, 64 * g:64 * g + 64], HID[:, h, g, :], W2v[:, h, :], h == 0, h == 1)
                          for g in range(2) for h in range(2)], t1, t_pin)
                for i in range(4):
                    free[b] = t_vcz = vcopy(flat(VC[32 * i:32 * i + 32, :, :]), banks[b][0:32, 0:128], tk)
        t_cmp = now(PE, V)

        pcs = [mem(256, M + 21504 + 256 * i) for i in range(2)]
        pc_read = [None, None]
        mx, sm = small[:, 528:536], small[:, 536:544]
        for t in range(4):
            b = take()
            tk = mms([(banks[b][:, 32 * (4 * g + i):32 * (4 * g + i) + 32], q2[:, i, 128 * t:128 * t + 128], KC[:, g, :],
                       True, True) for g in range(2) for i in range(4)], t_q2, t_kcz)
            pc = pcs[t % 2].rearrange("p (j c) -> p j c", j=8)
            cm = cmask[:, t, :].unsqueeze(1).to_broadcast([P, 8, 32])
            free[b] = tt(pc, banks[b][:, 0:256].rearrange("p (j c) -> p j c", j=8), cm, ALU.add, tk, pc_read[t % 2], *t_cmp)
            reduce(mx, pc, ALU.max)
            ts(mx, mx, NEG / 10, None, ALU.max, None)
            t1 = tt(pc, pc, mx.unsqueeze(2).to_broadcast([P, 8, 32]), ALU.subtract)
            t1 = act(ACT.Exp, pc, pc, t1)
            reduce(sm, pc, ALU.add, t1)
            ts(sm, sm, 1e-30, None, ALU.max, None)
            recip(sm, sm)
            tt(sm, sm, GT[:, t, 0:8], ALU.mult, t_gt)
            t1 = tt(pc, pc, sm.unsqueeze(2).to_broadcast([P, 8, 32]), ALU.mult)
            b = take()
            pc_read[t % 2] = tk = transposes([(banks[b][:, 128 * g:128 * g + 128], pcs[t % 2][:, 128 * g:128 * g + 128])
                                              for g in range(2)], t1)
            free[b] = t_pct = vcopy(pcT[:, :, 128 * t:128 * t + 128], v3(banks[b][:, 0:256], 2), tk)

        PS = [mem(2560, M + 18432 + 2560 * i) for i in range(2)]
        PTr = mem(2560, M + 23552)
        off = [0, 128, 384, 768]
        offk = [0, 512, 896, 1152]
        t_at = now(PE, V, A)
        turn["order"] = [2, 3, 4, 5, 6, 7]
        st = [small[:, 544 + 24 * i:544 + 24 * i + 24] for i in range(2)]
        ps_read = [None, None]
        t_scaled = {}

        def scores(un):
            i, br = un // 2, un % 2
            Pb = PS[un % 2]
            nm, su, ri = st[un % 2][:, 0:8], st[un % 2][:, 8:16], st[un % 2][:, 16:24]
            for g in range(2):
                for t in range(4):
                    N = 128 * (t + 1)
                    b = take()
                    tk = mms([(banks[b][:, 0:N], q2[:, i, 128 * t:128 * t + 128], KZ[:, br, g, 0:N], True, True)], *t_at)
                    o = Pb[:, 1280 * g + off[t]:1280 * g + off[t] + N]
                    j = 4 * g + t
                    free[b] = chained(V, lambda e, o=o, b=b, N=N, j=j, nm=nm: e.tensor_tensor_reduce(
                        o, banks[b][:, 0:N], causal[:, 512 - N:512], 1.0, -3e38, ALU.add, ALU.max, nm[:, j:j + 1]),
                        (tk, ps_read[un % 2], *t_at), chain=(t == 0))
                t1 = ts(nm[:, 4 * g:4 * g + 4], nm[:, 4 * g:4 * g + 4], -1.0, None, ALU.mult, None)
                for t in range(4):
                    N = 128 * (t + 1)
                    o = Pb[:, 1280 * g + off[t]:1280 * g + off[t] + N]
                    j = 4 * g + t
                    t2 = act(ACT.Exp, o, o, t1, bias=nm[:, j:j + 1], accum=su[:, j:j + 1], chain=(t == 0))
                t3 = recip(ri[:, 4 * g:4 * g + 4], su[:, 4 * g:4 * g + 4], t2)
                for t in range(4):
                    N = 128 * (t + 1)
                    o = Pb[:, 1280 * g + off[t]:1280 * g + off[t] + N]
                    j = 4 * g + t
                    gi = 8 * (1 + br) + 4 * g + i
                    t_scaled[un, g, t] = ts(o, o, ri[:, j:j + 1], GT[:, t, gi:gi + 1], ALU.mult, ALU.mult, t3, t_gt,
                                            lane=G, chain=(t == 0))

        ptr_read = [None]

        def values(un):
            i, br = un // 2, un % 2
            Pb = PS[un % 2]
            ob = i % 2
            for g in range(2):
                for kt in range(4):
                    b = take()
                    tk = transposes([(banks[b][:, 128 * t:128 * t + 128],
                                      Pb[:, 1280 * g + off[t] + 128 * kt:1280 * g + off[t] + 128 * kt + 128])
                                     for t in range(kt, 4)], *[t_scaled[un, g, t] for t in range(kt, 4)])
                    o = PTr[:, 1280 * g + offk[kt]:1280 * g + offk[kt] + 512 - 128 * kt]
                    free[b] = (vcopy if kt % 2 else acopy)(o, banks[b][:, 128 * kt:512], tk, ptr_read[0])
            ps_read[un % 2] = tk
            items = []
            if br == 0:
                PE.wait(free[ob])
                items += [(banks[ob][64 * g:64 * g + 64, :], VC[32 * i:32 * i + 32, g, :], pcT[32 * i:32 * i + 32, g, :],
                           True, False) for g in range(2)]
            for kt in range(4):
                items += [(banks[ob][64 * g:64 * g + 64, 128 * kt:512], VS[:, br, kt, 64 * g:64 * g + 64],
                           PTr[:, 1280 * g + offk[kt]:1280 * g + offk[kt] + 512 - 128 * kt], False, False)
                          for g in range(2)]
            ptr_read[0] = tk = mms(items, *now(V, A), skip=True)
            if br == 1:
                free[ob] = acopy(OT[:, i, :], banks[ob][:, :], tk)

        scores(0)
        for un in range(8):
            if un < 7:
                scores(un + 1)
            conv_taps(6)
            values(un)
        conv_taps(200)
        t_ot = now(A)
        turn["order"] = list(range(8))

        b = take()
        tk = group(banks[b][:, :], [(onesC, CO[:, j, :]) for j in range(4)], cur["conv"])
        for j in range(4):
            t1 = tt(CO[:, j, :], CO[:, j, :], banks[b][:, :], ALU.subtract, tk)
        free[b] = t1
        b = take()
        read = [None, None]
        for j in range(4):
            t2 = act(ACT.Square, vt[j % 2], CO[:, j, :], t1, read[j % 2], *now(PE))
            read[j % 2] = tk = mms([(banks[b][:, :], onesC, vt[j % 2], j == 0, j == 3)], t2)
        rs2 = vt[0]
        act(ACT.Ln, rs2, banks[b][:, :], tk, bias=epst)
        free[b] = t1 = act(ACT.Exp, rs2, rs2, scale=-0.5)
        t_co = []
        for j in range(4):
            t1 = tt(CO[:, j, :], CO[:, j, :], rs2, ALU.mult, free[b])
            t_co.append(act(ACT.Silu, CO[:, j, :], CO[:, j, :], t1, scale=col["ln_g"][:, j:j + 1],
                            bias=col["ln_b"][:, j:j + 1]))

        YA = v3(mem(4096, M), 8)
        ytmp = [mem(512, M + 18432 + 512 * i) for i in range(2)]
        YAo = v3(mem(4096, M + 19456), 8)

        def oparts(slot):
            dst = v3(slot, 4)
            src = I["w_o_nsa_2"][0].rearrange("(g i d) n -> g d i n", g=2, i=4)
            return [(dst[64 * g:64 * g + 64, :, :], src[g]) for g in range(2)]
        n, slot, arrived = load(oparts)
        w = v3(slot, 4)
        for d in range(8):
            b = take()
            tk = group(banks[b][:, :], [(w[:, i, 128 * d:128 * d + 128], OT[:, i, :]) for i in range(4)], arrived, t_ot)
            free[b] = t_ya = acopy(YAo[:, d, :], banks[b][:, :], tk, *t_co, *now(V, PE))
        released[n] = tk
        yt_read = [None, None]
        for c in range(2):
            n, slot, arrived = load(cols(win2, 2328 + 512 * c, 512))
            for j in range(4):
                d = 4 * c + j
                b, tk = proj(UT, slot, 512, j, arrived)
                free[b] = t1 = act(ACT.Sigmoid, ytmp[d % 2], banks[b][:, :], tk, yt_read[d % 2], *t_co)
                yt_read[d % 2] = tt(YAo[:, d, :], YAo[:, d, :], ytmp[d % 2], ALU.mult, t1, t_ya)
            released[n] = tk
        YB = v3(mem(4096, M), 8)
        n, slot, arrived = load(rows(I["w_conv_out_2"][0], 0, 4))
        w = v3(slot, 4)
        for d in range(8):
            b = take()
            tk = group(banks[b][:, :], [(w[:, i, 128 * d:128 * d + 128], CO[:, i, :]) for i in range(4)], arrived, *t_co)
            free[b] = t_yb = act(ACT.Identity, YB[:, d, :], banks[b][:, :], tk, bias=col["b_co"][:, d:d + 1])
        released[n] = tk
        for c in range(2):
            n, slot, arrived = load(cols(win2, 3352 + 512 * c, 512))
            for j in range(4):
                d = 4 * c + j
                b, tk = proj(UT, slot, 512, j, arrived)
                free[b] = t1 = act(ACT.Sigmoid, ytmp[d % 2], banks[b][:, :], tk, yt_read[d % 2])
                yt_read[d % 2] = tt(ytmp[d % 2], ytmp[d % 2], YB[:, d, :], ALU.mult, t1, t_yb)
                t_m = tt(YAo[:, d, :], YAo[:, d, :], ytmp[d % 2], ALU.add)
                yt_read[d % 2] = t_m
            released[n] = tk
        for half in range(2):
            n, slot, arrived = load(cols(I["w_out_2"][0], 512 * half, 512))
            for j in range(4):
                d = 4 * half + j
                b, tk = proj(YAo, slot, 512, j, arrived, t_m)
                free[b] = t_xt[d] = tt(XT[:, d, :], banks[b][:, :], XT[:, d, :], ALU.add, tk)
            released[n] = tk

        t_r = rms(t_xt, *now(PE, V))
        t_u = scaled(UT, col["g_ffn"], t_r, *now(PE))
        GTt = v3(mem(22 * 512, M), 22)
        fg = [mem(512, M + 20480 + 512 * i) for i in range(2)]
        fv = [mem(512, M + 21504 + 512 * i) for i in range(2)]
        f_read = [None, None]
        wup = I["w_up_2"][0]

        def upparts(c):
            def parts(slot):
                v = slot.rearrange("p (k n) -> p k n", k=8)
                return [(v[:, :, 256 * h:256 * h + 256],
                         wup[:, 2816 * h + 256 * c:2816 * h + 256 * c + 256].rearrange("(k p) n -> p k n", p=P))
                        for h in range(2)]
            return parts

        def conv3(o, b, tk, t, *waits):
            w0, w1_, w2_ = col["fcw01"][:, t:t + 1], col["fcw01"][:, 44 + t:45 + t], col["fcw2"][:, t:t + 1]
            t1 = act(ACT.Identity, o, banks[b][:, :], tk, *waits, scale=w2_, bias=col["fcb"][:, t:t + 1])
            stt(o[:, 1:], banks[b][:, 0:T - 1], w1_, o[:, 1:], ALU.mult, ALU.add, t1)
            return stt(o[:, 2:], banks[b][:, 0:T - 2], w0, o[:, 2:], ALU.mult, ALU.add)

        t_f0 = now(PE, V)
        for c in range(11):
            n, slot, arrived = load(upparts(c))
            for j in range(2):
                t = 2 * c + j
                b, tk = proj(UT, slot, 512, j, arrived, *t_u)
                free[b] = t1 = conv3(fg[t % 2], b, tk, t, f_read[t % 2], *t_f0)
                t2 = act(ACT.Gelu_apprx_tanh, fg[t % 2], fg[t % 2], t1)
                b, tk = proj(UT, slot, 512, 2 + j)
                free[b] = t1 = conv3(fv[t % 2], b, tk, 22 + t, f_read[t % 2])
                f_read[t % 2] = t_gg = tt(GTt[:, t, :], fg[t % 2], fv[t % 2], ALU.mult, t2)
            released[n] = tk
        for d in range(8):
            def dparts(slot, d=d):
                return [(slot[:, 0:2816].rearrange("p (k n) -> p k n", k=22),
                         I["w_down_2"][0][:, 128 * d:128 * d + 128].rearrange("(k p) n -> p k n", p=P))]
            n, slot, arrived = load(dparts)
            w = v3(slot[:, 0:2816], 22)
            b = take()
            released[n] = tk = group(banks[b][:, :], [(w[:, k, :], GTt[:, k, :]) for k in range(22)], arrived, t_gg)
            free[b] = t_xt[d] = tt(XT[:, d, :], banks[b][:, :], XT[:, d, :], ALU.add, tk)

        t_r = rms(t_xt, *now(PE))
        t_u = scaled(UT, col["g_ple"], t_r, *now(PE))
        pn, pslot, parr = load(lambda slot: [(slot[:, 0:2048].rearrange("p (k n) -> p k n", k=2),
                                              I["w_ple_2"][0].rearrange("(k p) n -> p k n", p=P))])
        wp = v3(pslot[:, 0:2048], 2)
        for half in range(2):
            n, slot, arrived = load(cols(I["w_ple_gate_2"][0], 512 * half, 512))
            for j in range(4):
                d = 4 * half + j
                b, tk = proj(UT, slot, 512, j, arrived, *t_u)
                free[b] = t1 = act(ACT.Sigmoid, fg[d % 2], banks[b][:, :], tk, *now(V))
                b = take()
                tk2 = group(banks[b][:, :], [(wp[:, k, 128 * d:128 * d + 128], pT[:, k, :]) for k in range(2)], parr)
                free[b] = tt(fg[d % 2], fg[d % 2], banks[b][:, :], ALU.mult, t1, tk2)
                t_xt[d] = tt(XT[:, d, :], XT[:, d, :], fg[d % 2], ALU.add)
            released[n] = tk
        t_r = rms(t_xt)
        toks = scaled(XT, col["g_final"], t_r)
        OUTT = v3(mem(4096, M), 4)
        s_out = sem("s_out")
        t_o = now(PE, V)
        o_v = out[0].rearrange("(t p) d -> p t d", p=P)
        for t in range(4):
            for half in range(2):
                b = take()
                tk = transposes([(banks[b][:, 128 * j:128 * j + 128], XT[:, 4 * half + j, 128 * t:128 * t + 128])
                                 for j in range(4)], *toks)
                free[b] = (vcopy if half else acopy)(OUTT[:, t, 512 * half:512 * half + 512], banks[b][:, :], tk, *t_o)
            SP.wait(*now(V, A))
            SP.silent(lambda e, t=t: e.dma_start(o_v[:, t, :], OUTT[:, t, :]).then_inc(s_out, 16))
        SP.wait((s_out, 64))

        block = ctx.enter_context(nc.Block())

        def play(lane):
            def body(e):
                for make in lane.queue:
                    make(e)
            return body

        block.sync(play(SP))
        block.scalar(play(A))
        block.vector(play(V))
        block.gpsimd(play(G))
        block.tensor(play(PE))


_INS = ["x", "c", "ctx", "c_ctx", "w_ada", "b_ada", "norm_mix", "norm_ffn", "w_in", "lb_logits", "hg_norm", "conv_w",
        "w_out", "w_router", "w_gate", "w_up", "w_down", "norm_final", "p_2", "g_mix_2", "w_in_2", "cmp_pos_k_2",
        "cmp_pos_v_2", "w_cmp_k1_2", "w_cmp_k2_2", "w_cmp_v1_2", "w_cmp_v2_2", "w_o_nsa_2", "conv_w_2", "conv_b_2",
        "conv_ln_g_2", "conv_ln_b_2", "w_conv_out_2", "b_conv_out_2", "w_out_2", "g_ffn_2", "w_up_2", "ffn_conv_w_2",
        "ffn_conv_b_2", "w_down_2", "g_ple_2", "w_ple_gate_2", "w_ple_2", "g_final_2"]


def kernel(**inputs):
    import numpy as _np
    import concourse.bacc as _bacc
    from concourse import mybir as _mybir
    from concourse.bass_utils import run_bass_kernel_spmd as _run

    nc = _bacc.Bacc("TRN2", target_bir_lowering=False, num_devices=1)
    arrays, aps = {}, {}
    for name in _INS:
        a = _np.ascontiguousarray(inputs[name])
        arrays[f"in_{name}_dram"] = a
        aps[name] = nc.dram_tensor(f"in_{name}_dram", a.shape, _mybir.dt.from_np(a.dtype), kind="ExternalInput").ap()
    out = nc.dram_tensor("out_0_dram", (1, 512, 1024), _mybir.dt.float32, kind="ExternalOutput").ap()
    build_program(nc, aps, out)
    r = _run(nc, [arrays], core_ids=[0])
    return r.results[0]["out_0_dram"]
```

```python
from contextlib import ExitStack

import concourse.bass as bass
from concourse import mybir

F32 = mybir.dt.float32
F32R = mybir.dt.float32r
I32 = mybir.dt.int32
ALU = mybir.AluOpType
ACT = mybir.ActivationFunctionType
AX = mybir.AxisListType

P = 128
T = 512
D = 1024
NS = 4
SLOT = 4096
EPS = 1e-6
NEG = -1e30


class Lane:

    def __init__(self, sem):
        self.sem, self.n, self.queue, self.seen = sem, 0, [], {}

    def wait(self, *tokens):
        for tok in tokens:
            if tok is None:
                continue
            if isinstance(tok, list):
                self.wait(*tok)
                continue
            sem, value = tok
            if self.seen.get(id(sem), 0) < value:
                self.seen[id(sem)] = value
                self.queue.append(lambda e, sem=sem, value=value: e.wait_ge(sem, value))

    def counted(self, make):
        self.n += 1
        self.queue.append(lambda e, make=make: make(e).then_inc(self.sem, 1))
        return (self.sem, self.n)

    def silent(self, make):
        self.queue.append(lambda e, make=make: make(e))


def build_program(nc, I, out):
    ctx = ExitStack()
    with ctx:
        def sem(name):
            return ctx.enter_context(nc.semaphore(name))

        PE, V, A, G, SP = (Lane(sem(n)) for n in ("s_pe", "s_ve", "s_ac", "s_po", "s_sp"))

        def chained(lane, make, waits, chain=True):
            lane.wait(*waits)
            if chain and lane.n:
                lane.wait((lane.sem, lane.n))
            return lane.counted(make)

        NW = 52960
        M = 24832
        def lay(name, at, n, kind):
            if at == 0:
                with nc.sbuf_tensor(name, [P, n], kind) as piece:
                    return piece
            with nc.sbuf_tensor(f"below_{name}", [P, at], F32), nc.sbuf_tensor(name, [P, n], kind) as piece:
                return piece

        low, high = lay("low", 0, M, F32), lay("high", M, NW - M, F32)
        banks = [ctx.enter_context(nc.psum_tensor(f"bank{i}", [P, 512], F32)) for i in range(8)]
        cursor = [0]

        rounded, full = {}, {}

        def mem(n, at=None):
            if at is None:
                at = cursor[0]
                cursor[0] += n
            assert at + n <= NW, (at, n)
            assert at + n <= M or at >= M
            return low[:, at:at + n] if at < M else high[:, at - M:at - M + n]

        def memR(n, at):
            if (at, n) not in rounded:
                rounded[at, n] = lay(f"r_{at}_{n}", at, n, F32R)
            return rounded[at, n][:, :]

        def own(n, at):
            if (at, n) not in full:
                full[at, n] = lay(f"f_{at}_{n}", at, n, F32)
            return full[at, n][:, :]

        def v3(ap, a):
            return ap.rearrange("p (a b) -> p a b", a=a)

        def flat(ap):
            return ap.rearrange("p a b -> p (a b)")

        def now(*lanes):
            return [(l.sem, l.n) for l in lanes if l.n]

        def act(func, o, i, *waits, bias=0.0, scale=1.0, accum=None, chain=True):
            if accum is None:
                return chained(A, lambda e: e.activation(o, i, func, bias=bias, scale=scale), waits, chain)
            return chained(A, lambda e: e.activation(o, i, func, bias=bias, scale=scale, accum_out=accum), waits, chain)

        def tt(o, a, b, op, *waits, chain=True, lane=None):
            return chained(lane or V, lambda e: e.tensor_tensor(o, a, b, op), waits, chain)

        def ts(o, a, s1, s2, op0, op1, *waits, chain=True, lane=None):
            if s2 is None:
                return chained(lane or V, lambda e: e.tensor_scalar(o, a, s1, None, op0), waits, chain)
            return chained(lane or V, lambda e: e.tensor_scalar(o, a, s1, s2, op0, op1), waits, chain)

        def stt(o, a, s, b, op0, op1, *waits, chain=True):
            return chained(V, lambda e: e.scalar_tensor_tensor(out=o, in0=a, scalar=s, in1=b, op0=op0, op1=op1),
                           waits, chain)

        def vcopy(o, i, *waits, chain=True):
            return chained(V, lambda e: e.tensor_copy(o, i), waits, chain)

        def acopy(o, i, *waits, chain=True):
            return chained(A, lambda e: e.activation(o, i, ACT.Copy), waits, chain)

        def vset(o, val, *waits, chain=True):
            return chained(V, lambda e: e.memset(o, val), waits, chain)

        def reduce(o, i, op, *waits):
            return chained(V, lambda e: e.tensor_reduce(o, i, AX.X, op), waits)

        def recip(o, i, *waits):
            return chained(V, lambda e: e.reciprocal(o, i), waits)

        def mms(items, *waits, skip=False):
            PE.wait(*waits)
            for n, (o, l, r, st, sp, *tok) in enumerate(items):
                PE.wait(*tok)
                mk = lambda e, o=o, l=l, r=r, st=st, sp=sp: e.matmul(o, l, r, start=st, stop=sp, skip_group_check=skip)
                if n == len(items) - 1:
                    return PE.counted(mk)
                PE.silent(mk)

        def group(o, pairs, *waits):
            last = len(pairs) - 1
            return mms([(o, l, r, n == 0, n == last) for n, (l, r) in enumerate(pairs)], *waits)

        def transposes(items, *waits):
            PE.wait(*waits)
            for n, (o, i) in enumerate(items):
                k = i.shape[0]
                mk = lambda e, o=o, i=i, k=k: e.transpose(o, i, ident[0:k, 0:k])
                if n == len(items) - 1:
                    return PE.counted(mk)
                PE.silent(mk)

        free = [None] * 8
        turn = {"order": list(range(8)), "i": 0}

        def take():
            b = turn["order"][turn["i"] % len(turn["order"])]
            turn["i"] += 1
            PE.wait(free[b])
            return b

        slot_at = [cursor[0] + SLOT * i for i in range(NS)]
        cursor[0] += SLOT * NS
        landed = [sem(f"s_w{i}") for i in range(NS)]
        slot_count = [0] * NS
        slot_free = [None] * NS
        turns = {"plain": 0, "pair": 0}

        def fetch(s, parts):
            slot = own(SLOT, slot_at[s])
            for dst, src in parts(slot):
                slot_count[s] += 16
                SP.silent(lambda e, dst=dst, src=src: e.dma_start(dst, src).then_inc(landed[s], 16))
            return slot, (landed[s], slot_count[s])

        def load(parts):
            s = turns["plain"] % NS
            turns["plain"] += 1
            SP.wait(slot_free[s])
            slot, tok = fetch(s, parts)
            return s, slot, tok

        specs, prepared = [], []

        def prep():
            if not specs:
                return
            parts, words, divide = specs.pop(0)
            p = turns["pair"] % 2
            turns["pair"] += 1
            a, b_ = 2 * p, 2 * p + 1
            SP.wait(slot_free[a], slot_free[b_])
            slot, arrived = fetch(a, parts)
            if not divide:
                prepared.append((a, b_, slot, None, None, [arrived]))
                return
            hi, lo, raw = memR(SLOT, slot_at[b_]), memR(SLOT, slot_at[a]), slot
            toks = []
            step = words // 2
            for i in range(2):
                s_ = slice(step * i, step * i + step)
                t1 = chained(A, lambda e, s_=s_: e.activation(hi[:, s_], raw[:, s_], ACT.Copy),
                             (arrived, slot_free[b_]))
                t2 = chained(G, lambda e, s_=s_: e.tensor_tensor(lo[:, s_], raw[:, s_], hi[:, s_].bitcast(F32),
                                                                 ALU.subtract), (t1, arrived))
                toks.append(t2)
            prepared.append((a, b_, slot, hi[:, 0:words], lo[:, 0:words], toks))

        def chunk():
            return prepared.pop(0)

        def release(ch, tok):
            slot_free[ch[0]] = slot_free[ch[1]] = tok

        def split(at_hi, at_full, words, *waits, lane=None):
            whole = own(words, at_full)
            hi, lo = memR(words, at_hi), memR(words, at_full)
            t1 = chained(A, lambda e: e.activation(hi, whole, ACT.Copy), waits)
            t2 = chained(lane or V, lambda e: e.tensor_tensor(lo, whole, hi.bitcast(F32), ALU.subtract), (t1, *waits))
            return hi, lo, t2

        def three(o, wh, wl, xh, xl, st, sp, *tok):
            return [(o, wh, xh, st, False, *tok), (o, wl, xh, False, False), (o, wh, xl, False, sp)]

        def cols(w, c0, n):
            def parts(slot):
                dst = slot[:, 0:8 * n].rearrange("p (k n) -> p k n", k=8)
                return [(dst, w[:, c0:c0 + n].rearrange("(k p) n -> p k n", p=P))]
            return parts

        def rows(w, r0, nk):
            def parts(slot):
                dst = slot[:, 0:nk * D].rearrange("p (k n) -> p k n", k=nk)
                return [(dst, w[r0:r0 + nk * P, :].rearrange("(k p) n -> p k n", p=P))]
            return parts

        ident = mem(128)
        onesD = mem(128)
        onesC = mem(128)
        ones256 = mem(256)
        epst = mem(1)
        blkmask = [mem(128) for _ in range(2)]
        resets = mem(T)
        iota1 = mem(64)
        causal = mem(T)
        cmask = v3(mem(4 * 32), 4)
        sel = mem(2)
        PT = v3(mem(5 * 128), 5)
        adaT = mem(96).rearrange("p (t r) -> p t r", r=2)
        mod = v3(mem(3 * 8), 3)
        small = mem(600)
        gainrow = mem(128)
        WR = v3(mem(128), 8)
        W2k, W2v = v3(mem(128), 2), v3(mem(128), 2)
        CP = v3(mem(8 * 32), 8)
        XT_AT = cursor[0]
        mem(8 * T)
        XT = v3(own(8 * T, XT_AT), 8)
        assert cursor[0] <= M and NW - M >= 28128, (cursor[0], M)

        def gp(make, *w):
            return chained(G, make, w)

        def setg(o, val, *w):
            return gp(lambda e: e.memset(o, val), *w)

        def asel(o, op, fill, base, pattern, mult, *w):
            return gp(lambda e: e.affine_select(out=o, in_=o, compare_op=op, fill=fill, base=base,
                                                pattern=pattern, channel_multiplier=mult), *w)

        setg(ident, 0.0)
        t_id = asel(ident, ALU.not_equal, 1.0, 0, [[-1, 128]], 1)
        setg(epst, EPS)
        setg(sel, 0.0)
        for q in range(4):
            t_sel = asel(sel, ALU.not_equal, 1.0, -32 * q, [[-1, 2]], 1)
        setg(onesD, 1.0 / D)
        setg(onesC, 1.0 / 512)
        setg(ones256, 1.0)
        for m in blkmask:
            setg(m, 0.0)
            for c in range(4):
                setg(m[32 * c:32 * c + 32, 32 * c:32 * c + 32], 1.0)
        asel(blkmask[0], ALU.is_ge, 0.0, 0, [[1, 128]], -1)
        asel(blkmask[1], ALU.is_ge, 0.0, 0, [[-1, 128]], 1)
        setg(resets, 1.0)
        setg(resets.rearrange("p (n c) -> p n c", c=32)[:, :, 0:1], 0.0)
        setg(causal, 0.0)
        asel(causal[:, 384:512], ALU.is_ge, NEG, 0, [[-1, 128]], 1)
        setg(flat(cmask), 0.0)
        for t in range(4):
            asel(cmask[:, t, :], ALU.is_ge, NEG, 128 * t - 31, [[-16, 32]], 1)
        setg(cmask[:, :, 31:32], NEG)
        gp(lambda e: e.iota(iota1.bitcast(I32), pattern=[[1, 64]], base=1, channel_multiplier=0))
        t_const = gp(lambda e: e.tensor_copy(iota1, iota1.bitcast(I32)))

        xtok = v3(mem(4 * D, M), 4)
        xn = v3(mem(4 * D, M + 4096), 4)
        ctok = v3(mem(2 * D, M + 8192), 2)
        stage = v3(mem(5 * 128, M + 11264), 5)
        s_st0, s_st, s_c, s_p, s_pt = (sem(n) for n in ("s_st0", "s_st", "s_c", "s_p", "s_pt"))
        s_x = [sem("s_x0"), sem("s_x1")]
        t_stz = vset(flat(stage), 0.0)
        col, fill_at, n_st = {}, [0] * 5, [0, 0]

        def lrows(name, src, n, tile):
            r0 = fill_at[tile]
            fill_at[tile] += n
            assert fill_at[tile] <= 128
            n_st[min(tile, 1)] += 16
            lane, s_ = (G, s_st) if tile else (A, s_st0)
            lane.silent(lambda e, d=stage[r0:r0 + n, tile, :], s=src: e.dma_start(d, s).then_inc(s_, 16))
            col[name] = PT[:, tile, r0:r0 + n]

        x_v = I["x"][0].rearrange("(t p) d -> p t d", p=P)
        for i in range(2):
            SP.silent(lambda e, i=i: e.dma_start(xtok[:, 2 * i:2 * i + 2, :], x_v[:, 2 * i:2 * i + 2, :])
                      .then_inc(s_x[i], 16))
        A.wait(t_stz)
        R = "(r c) -> r c"
        lrows("c", I["c"][0].rearrange(R, c=P), 8, 0)
        lrows("c_ctx", I["c_ctx"].rearrange(R, c=P), 8, 0)
        lrows("b_ada", I["b_ada"][0].rearrange(R, c=P), 48, 0)
        lrows("norm_mix", I["norm_mix"][0].rearrange(R, c=P), 8, 0)
        lrows("norm_ffn", I["norm_ffn"][0].rearrange(R, c=P), 8, 0)
        lrows("norm_final", I["norm_final"].rearrange(R, c=P), 8, 0)
        lrows("lb", I["lb_logits"].rearrange("a b (r c) -> (a b r) c", c=P), 16, 0)
        lrows("conv_w", I["conv_w"][0].rearrange("k (r c) -> (k r) c", c=P), 12, 0)

        def late_loads():
            G.wait(t_stz)
            lrows("conv_w_2", I["conv_w_2"][0].rearrange("k (r c) -> (k r) c", c=P), 124, 1)
            lrows("fcw01", I["ffn_conv_w_2"][0][0:2, :].rearrange("k (r c) -> (k r) c", c=P), 88, 2)
            lrows("g_mix", I["g_mix_2"][0].rearrange(R, c=P), 8, 2)
            lrows("conv_b", I["conv_b_2"][0].rearrange(R, c=P), 4, 2)
            lrows("ln_g", I["conv_ln_g_2"][0].rearrange(R, c=P), 4, 2)
            lrows("ln_b", I["conv_ln_b_2"][0].rearrange(R, c=P), 4, 2)
            lrows("b_co", I["b_conv_out_2"][0].rearrange(R, c=P), 8, 2)
            lrows("fcw2", I["ffn_conv_w_2"][0][2:3, :].rearrange("k (r c) -> (k r) c", c=P), 44, 3)
            lrows("fcb", I["ffn_conv_b_2"][0].rearrange(R, c=P), 44, 3)
            lrows("g_ffn", I["g_ffn_2"][0].rearrange(R, c=P), 8, 3)
            lrows("g_ple", I["g_ple_2"][0].rearrange(R, c=P), 8, 3)
            lrows("g_final", I["g_final_2"].rearrange(R, c=P), 8, 3)
            lrows("pos_k", I["cmp_pos_k_2"][0].rearrange("(m l) d -> m (l d)", l=2), 16, 3)
            lrows("pos_v", I["cmp_pos_v_2"][0].rearrange("(m l) d -> m (l d)", l=2), 16, 4)
            for dst, src in (
                (gainrow, I["hg_norm"].to_broadcast([P, 128])),
                (WR, I["w_router"][0].rearrange("(k p) n -> p k n", p=P)),
                (W2k, I["w_cmp_k2_2"][0].rearrange("(k p) n -> p k n", p=P)),
                (W2v, I["w_cmp_v2_2"][0].rearrange("(k p) n -> p k n", p=P)),
            ):
                G.silent(lambda e, dst=dst, src=src: e.dma_start(dst, src).then_inc(s_p, 16))

        late_loads()
        t_pin = (s_p, 64)
        t_stage, t_late = (s_st0, n_st[0]), (s_st, n_st[1])

        ada_at = [slot_at[2], slot_at[3], M + 14336, M + 18432]
        s_ada = [sem(f"s_ada{c}") for c in range(4)]
        win = I["w_in"][0]

        def ada_load(c):
            slot = own(4096, ada_at[c])
            for dst, src in cols(I["w_ada"][0], 512 * c, 512)(slot):
                SP.silent(lambda e, dst=dst, src=src: e.dma_start(dst, src).then_inc(s_ada[c], 16))
            return slot, (s_ada[c], 16)

        specs += [(cols(win, c0, 512), 4096, True) for c0 in (512, 1536, 1024, 0, 2048, 3072)]
        specs += [(cols(I["w_ada"][0], 512 * c, 512), 4096, False) for c in range(4, 8)]
        specs += [(cols(win, c0, 512), 4096, True) for c0 in (3584, 2560)]
        specs += [(cols(I["w_ada"][0], 512 * c, 512), 4096, False) for c in range(8, 12)]
        specs += [(cols(I["w_out"][0], 512 * h, 512), 4096, True) for h in range(2)]
        early = [ada_load(0), ada_load(1)]

        ss = small[:, 48:54]
        for i in range(4):
            act(ACT.Square, xn[:, i, :], xtok[:, i, :], (s_x[i // 2], 16), accum=ss[:, i:i + 1])
        t1 = act(ACT.Sqrt, ss[:, 0:4], ss[:, 0:4], t_const, bias=epst, scale=1.0 / D)
        t_rs = recip(ss[:, 0:4], ss[:, 0:4], t1)
        prep()

        def turn_tok(src, t, half, *waits):
            b = take()
            tk = transposes([(banks[b][:, 128 * j:128 * j + 128],
                              src[:, t, 512 * half + 128 * j:512 * half + 128 * j + 128]) for j in range(4)], *waits)
            return b, tk

        for t in range(4):
            t1 = ts(xn[:, t, :], xtok[:, t, :], ss[:, t:t + 1], None, ALU.mult, None, t_rs)
            for half in range(2):
                b, tk = turn_tok(xn, t, half, t1, t_id)
                free[b] = (vcopy if half else acopy)(XT[:, 4 * half:4 * half + 4, 128 * t:128 * t + 128],
                                                     v3(banks[b][:, :], 4), tk)
        t_tr = now(V, A)
        t_xn = now(PE)

        b = take()
        tk = transposes([(banks[b][:, 0:128], stage[:, 0, :])], t_stage, t_id)
        free[b] = t_pt = vcopy(PT[:, 0, :], banks[b][:, 0:128], tk)

        t_cz = vset(flat(CP), 0.0)
        act(ACT.Silu, CP[:, :, 0], col["c"], t_cz, t_pt)
        t_cp = act(ACT.Silu, CP[:, :, 1], col["c_ctx"])

        adatmp = [mem(512, M + 25600 + 512 * i) for i in range(2)]
        ada_free = [None, None]

        def ada_chunk(c):
            if c < 4:
                slot, arrived = early[c]
            else:
                ch = chunk()
                slot, arrived = ch[2], ch[5]
                prep()
            w = v3(slot, 8)
            b = take()
            tk = mms([(banks[b][32 * (k % 4):32 * (k % 4) + 32, :], CP[:, k, :], w[:, k, :], k < 4, k >= 4)
                      for k in range(8)], arrived, t_cp)
            if c >= 4:
                release(ch, tk)
            elif c < 2:
                slot_free[2 + c] = tk
            free[b] = t1 = acopy(adatmp[c % 2], banks[b][:, :], tk, ada_free[c % 2])
            b = take()
            tk = mms([(banks[b][:, 2 * j:2 * j + 2], adatmp[c % 2][:, 128 * j:128 * j + 128], sel, True, True)
                      for j in range(4)], t1, t_sel)
            ada_free[c % 2] = tk
            bb = col["b_ada"][:, 4 * c:4 * c + 4].unsqueeze(2).to_broadcast([P, 4, 2])
            free[b] = tt(adaT[:, 4 * c:4 * c + 4, :], banks[b][:, 0:8].rearrange("p (t r) -> p t r", r=2), bb,
                         ALU.add, tk, t_pt)
            return free[b]

        early += [ada_load(2), ada_load(3)]
        SP.silent(lambda e: e.dma_start(ctok, I["ctx"][0].rearrange("(t p) d -> p t d", p=P)).then_inc(s_c, 16))
        for c in range(4):
            ada_chunk(c)
            if c == 1:
                for i in range(2):
                    act(ACT.Square, xn[:, 3, :], ctok[:, i, :], (s_c, 16), *t_xn, accum=ss[:, 4 + i:5 + i])
                t1 = act(ACT.Sqrt, ss[:, 4:6], ss[:, 4:6], bias=epst, scale=1.0 / D)
                t_rc = recip(ss[:, 4:6], ss[:, 4:6], t1)
        stt(mod[:, 0, :], adaT[:, 8:16, 0], 1.0, col["norm_mix"], ALU.add, ALU.mult)
        t_mod = stt(mod[:, 1, :], adaT[:, 8:16, 1], 1.0, col["norm_mix"], ALU.add, ALU.mult)

        lb, oml, noml = small[:, 0:8], small[:, 8:16], small[:, 16:24]
        tm, e0, e1 = small[:, 24:32], small[:, 32:40], small[:, 40:48]
        a0, a1 = col["lb"][:, 0:8], col["lb"][:, 8:16]
        tt(tm, a0, a1, ALU.max)
        tt(e0, a0, tm, ALU.subtract)
        t1 = tt(e1, a1, tm, ALU.subtract)
        act(ACT.Exp, e0, e0, t1)
        t1 = act(ACT.Exp, e1, e1)
        tt(tm, e0, e1, ALU.add, t1)
        recip(tm, tm)
        tt(lb, e0, tm, ALU.mult)
        ts(oml, lb, -1.0, 1.0, ALU.mult, ALU.add)
        t_lb = ts(noml, oml, -1.0, None, ALU.mult, None)

        b = take()
        tk = transposes([(banks[b][:, 128 * (i - 1):128 * i], stage[:, i, :]) for i in range(1, 5)], t_late)
        free[b] = t_pt2 = vcopy(flat(PT[:, 1:5, :]), banks[b][:, :], tk)

        UH, UL = v3(memR(4096, M + 14336), 8), v3(memR(4096, XT_AT), 8)
        HCH, HCL = v3(memR(2048, M + 18432), 8), v3(memR(2048, M + 12288), 8)
        HF, CF = XT, v3(own(2048, M + 12288), 8)
        t_pe = now(PE)
        t_u = []
        for d in range(8):
            t1 = ts(HF[:, d, :], HF[:, d, :], mod[:, 0, d:d + 1], adaT[:, d, 0:1], ALU.mult, ALU.add, *t_tr,
                    chain=(d == 0))
            t2 = chained(A, lambda e, o=UH[:, d, :], f=HF[:, d, :]: e.activation(o, f, ACT.Copy), (t1, *t_pe),
                         chain=(d == 0))
            t3 = chained(G if d % 2 else V, lambda e, o=UL[:, d, :], f=HF[:, d, :], h=UH[:, d, :]:
                         e.tensor_tensor(o, f, h.bitcast(F32), ALU.subtract),
                         (t2, t1), chain=False)
            t_u.append([t2, t3])
        t_hc = [None]

        def context():
            for t in range(2):
                t1 = ts(ctok[:, t, :], ctok[:, t, :], ss[:, 4 + t:5 + t], None, ALU.mult, None, t_rc)
                for half in range(2):
                    b, tk = turn_tok(ctok, t, half, t1)
                    free[b] = t2 = vcopy(CF[:, 4 * half:4 * half + 4, 128 * t:128 * t + 128], v3(banks[b][:, :], 4), tk)
            for d in range(8):
                t3 = ts(CF[:, d, :], CF[:, d, :], mod[:, 1, d:d + 1], adaT[:, d, 1:2], ALU.mult, ALU.add,
                        chain=(d == 0))
            t4 = chained(A, lambda e: e.activation(HCH, CF, ACT.Copy), (t3,))
            t_hc[0] = [t4, chained(G, lambda e: e.tensor_tensor(HCL, CF, HCH.bitcast(F32), ALU.subtract), (t4,))]

        def dproj(ch, n, j, t_in, xh=None, xl=None, nk=8):
            xh, xl = (UH, UL) if xh is None else (xh, xl)
            wh, wl = (z[:, 0:nk * n].rearrange("p (k n) -> p k n", k=nk) for z in (ch[3], ch[4]))
            s_ = slice(128 * j, 128 * j + 128)
            b = take()
            items = []
            for k in range(nk):
                items += three(banks[b][:, :], wh[:, k, s_], wl[:, k, s_], xh[:, k, :], xl[:, k, :], k == 0,
                               k == nk - 1, t_in[k] if t_in else None)
            return b, mms(items, *ch[5])

        def dprojtok(ch, n, c0, nc_, t, xh=None, xl=None, *waits):
            xh, xl = (UH, UL) if xh is None else (xh, xl)
            wh, wl = (z[:, 0:8 * n].rearrange("p (k n) -> p k n", k=8) for z in (ch[3], ch[4]))
            s_ = slice(128 * t, 128 * t + 128)
            b = take()
            items = []
            for k in range(8):
                items += three(banks[b][:, 0:nc_], xh[:, k, s_], xl[:, k, s_], wh[:, k, c0:c0 + nc_],
                               wl[:, k, c0:c0 + nc_], k == 0, k == 7)
            return b, mms(items, *ch[5], *waits)

        gA, gB, gD, gE = (v3(own(2048, M + 2048 * i), 4) for i in range(4))
        qT = v3(mem(2048, M + 8192), 4)
        vtok = v3(mem(2048, M + 10240), 4)
        gtok = v3(mem(2048, M + 12288), 4)
        S0 = mem(1024, M + 20480).rearrange("p (d h v) -> p d h v", d=2, h=4)
        U = v3(mem(2048, M + 21504), 4)
        Sring = mem(1024, M + 23552).rearrange("p (r h v) -> p r h v", r=2, h=4)
        scT = [mem(512, M + 24576 + 512 * i) for i in range(2)]
        dec = small[:, 54:118].rearrange("p (h n) -> p h n", h=4)
        last = small[:, 118:122]
        cA, cB = v3(mem(1024, M + 4096), 4), v3(mem(1024, M + 5120), 4)
        cK, vctx = v3(mem(1024, M + 6144), 2), v3(mem(1024, M + 7168), 2)
        gK = [gA, U]

        turn["order"] = [4, 5, 6, 7]

        def gate_scalars(d, h):
            i = 4 * d + h
            return lb[:, i:i + 1], oml[:, i:i + 1], noml[:, i:i + 1]

        def ctx_gate(ch, d, *waits):
            wh, wl = v3(ch[3], 8), v3(ch[4], 8)
            for h2 in range(2):
                b = take()
                items = []
                for hh in range(2):
                    s_ = slice(256 * h2 + 128 * hh, 256 * h2 + 128 * hh + 128)
                    for k in range(8):
                        items += three(banks[b][:, 256 * hh:256 * hh + 256], wh[:, k, s_], wl[:, k, s_], HCH[:, k, :],
                                       HCL[:, k, :], k == 0, k == 7)
                tk = mms(items, *ch[5], t_hc[0])
                free[b] = act(ACT.Sigmoid, cA[:, 2 * h2:2 * h2 + 2, :], v3(banks[b][:, :], 2), tk, *waits)
            for h in range(4):
                l_, o_, _ = gate_scalars(d, h)
                t1 = act(ACT.Ln, cB[:, h, :], cA[:, h, :], t_lb, *waits, scale=o_, bias=l_)
            for h in range(4):
                _, o_, n_ = gate_scalars(d, h)
                x_ = cB[:, h, ::-1] if d else cB[:, h, :]
                chained(V, lambda e, x_=x_: e.tensor_tensor_scan(x_, ones256, x_, 0.0, ALU.mult, ALU.add), (t1, t_const))
                ts(cA[:, h, :], cA[:, h, :], n_, o_, ALU.mult, ALU.add)
            t2 = vcopy(last, cB[:, :, 0 if d else 255])
            for h in range(4):
                t3 = act(ACT.Exp, cB[:, h, :], cB[:, h, :], t2, scale=-1.0, bias=last[:, h:h + 1])
            t4 = tt(cA, cA, cB, ALU.mult, t3)
            for t in range(2):
                b = take()
                tk = transposes([(banks[b][:, 128 * h:128 * h + 128], cA[:, h, 128 * t:128 * t + 128])
                                 for h in range(4)], t4)
                free[b] = vcopy(cK[:, t, :], banks[b][:, :], tk)
            return free[b]

        def ctx_state(d, t_k, t_vc):
            b = take()
            tk = mms([(banks[b][:, 128 * h:128 * h + 128], cK[:, t, 128 * h:128 * h + 128],
                       vctx[:, t, 128 * h:128 * h + 128], t == 0, t == 1) for h in range(4) for t in range(2)], t_k, t_vc)
            free[b] = vcopy(S0[:, d, :, :].rearrange("p h v -> p (h v)"), banks[b][:, :], tk)
            return free[b]

        def gates_math(d, t_sig, t_q, *waits):
            K = gK[d]
            for h in range(4):
                l_, o_, _ = gate_scalars(d, h)
                t1 = act(ACT.Ln, gB[:, h, :], K[:, h, :], t_sig, *waits, scale=o_, bias=l_)
            for h in range(4):
                _, o_, n_ = gate_scalars(d, h)
                x_ = gB[:, h, ::-1] if d else gB[:, h, :]
                chained(V, lambda e, x_=x_: e.tensor_tensor_scan(x_, resets, x_, 0.0, ALU.mult, ALU.add),
                        (t1, t_const, *waits))
                t2 = ts(K[:, h, :], K[:, h, :], n_, o_, ALU.mult, ALU.add)
            act(ACT.Exp, dec, gB.rearrange("p h (n c) -> p h n c", c=32)[:, :, :, 0 if d else 31], t2)
            t_e = act(ACT.Exp, gE, gB, scale=-1.0)
            t_d = act(ACT.Exp, gD, gB)
            tt(gE, gE, K, ALU.mult, t_e)
            tt(gD, gD, qT, ALU.mult, t_d, t_q)
            db = dec.rearrange("p h n -> p (h n)").unsqueeze(2).to_broadcast([P, 64, 32])
            return tt(K.rearrange("p h (n c) -> p (h n) c", c=32), gE.rearrange("p h (n c) -> p (h n) c", c=32), db,
                      ALU.mult)

        fillers = []

        def fill(n=1):
            for _ in range(n):
                if fillers:
                    fillers.pop(0)()

        def gla(d, t_gates, t_v):
            K = gK[d]
            for t in range(4):
                b = take()
                tk = transposes([(banks[b][:, 128 * h:128 * h + 128], K[:, h, 128 * t:128 * t + 128])
                                 for h in range(4)], t_gates)
                free[b] = t_kt = vcopy(gB[:, t, :], banks[b][:, :], tk)
            for i in range(2):
                vset(scT[i], 0.0, *now(PE))
            read = [None, None]
            for t in range(4):
                b = take()
                s_ = slice(128 * t, 128 * t + 128)
                tk = mms([(banks[b][:, 128 * h:128 * h + 128], gE[:, h, s_], gD[:, h, s_], True, True)
                          for h in range(4)], t_gates)
                mk = blkmask[d].bitcast(I32).unsqueeze(1).to_broadcast([P, 4, 128])
                sc, bk = v3(scT[t % 2], 4), v3(banks[b][:, :], 4)
                free[b] = chained(V, lambda e, sc=sc, mk=mk, bk=bk: e.copy_predicated(sc, mk, bk),
                                  (tk, t_const, read[t % 2]))
                read[t % 2] = tk = mms([(banks[t][:, 128 * h:128 * h + 128], scT[t % 2][:, 128 * h:128 * h + 128],
                                         vtok[:, t, 128 * h:128 * h + 128], d == 0 and h == 0, False)
                                        for h in range(4)], free[b], t_v, skip=True)
            prev, t_prev = S0[:, d, :, :], t_s0[d]
            ring_read = [None, None]
            for i, n in enumerate(range(15, -1, -1) if d else range(16)):
                t, c = n // 4, n % 4
                pp = slice(32 * c, 32 * c + 32)
                if i < 15:
                    b = take()
                    tkv = mms([(banks[b][:, 128 * h:128 * h + 128], gB[pp, t, 128 * h:128 * h + 128],
                                vtok[pp, t, 128 * h:128 * h + 128], True, True) for h in range(4)], t_kt, t_v)
                tk = mms([(banks[t][pp, 128 * h:128 * h + 128], gD[:, h, 32 * n:32 * n + 32], prev[:, h, :],
                           False, False) for h in range(4)], t_prev, skip=True)
                if i > 0:
                    ring_read[(i - 1) % 2] = tk
                if i < 15:
                    nxt = Sring[:, i % 2, :, :]
                    V.wait(*now(V))
                    for h in range(4):
                        t_prev = stt(nxt[:, h, :], prev[:, h, :], dec[:, h, n:n + 1],
                                     banks[b][:, 128 * h:128 * h + 128], ALU.mult, ALU.add, tkv,
                                     ring_read[i % 2], chain=False)
                    free[b] = t_prev
                    prev = nxt
                if i % 2 == 1:
                    fill()
            return tk

        t_s0 = [None, None]
        t_pre = now(PE, V, A)
        ch = chunk()
        for h in range(4):
            b, tk = dproj(ch, 512, h, t_u)
            free[b] = t_sig = act(ACT.Sigmoid, gA[:, h, :], banks[b][:, :], tk, *t_pre)
            if h == 0:
                prep()
            if h == 1:
                context()
        t_k0 = ctx_gate(ch, 0, *now(PE, V, A))
        release(ch, now(PE))
        ch = chunk()
        for t in range(4):
            b, tk = dprojtok(ch, 512, 0, 512, t)
            free[b] = t_v = acopy(vtok[:, t, :], banks[b][:, :], tk, *t_pre)
            if t == 1:
                prep()
        for t in range(2):
            b, tk = dprojtok(ch, 512, 0, 512, t, HCH, HCL)
            free[b] = t_vc = acopy(vctx[:, t, :], banks[b][:, :], tk, *t_pre)
        release(ch, tk)
        t_s0[0] = ctx_state(0, t_k0, t_vc)
        ch = chunk()
        t_k1 = ctx_gate(ch, 1, t_s0[0])
        for h in range(4):
            b, tk = dproj(ch, 512, h, None)
            free[b] = t_sigb = act(ACT.Sigmoid, U[:, h, :], banks[b][:, :], tk, *t_pre)
            if h == 0:
                prep()
        release(ch, tk)
        t_s0[1] = ctx_state(1, t_k1, t_vc)
        ch = chunk()
        for h in range(4):
            b, tk = dproj(ch, 512, h, None)
            free[b] = t_q = acopy(qT[:, h, :], banks[b][:, :], tk, *t_pre)
            if h == 1:
                prep()
        release(ch, tk)
        t_g0 = gates_math(0, t_sig, t_q, t_s0[1])
        ch = chunk()
        grow = gainrow.unsqueeze(1).to_broadcast([P, 4, 128])
        for t in range(4):
            b, tk = dprojtok(ch, 512, 0, 512, t)
            free[b] = t1 = act(ACT.Silu, gtok[:, t, :], banks[b][:, :], tk, t_s0[1])
            tt(v3(gtok[:, t, :], 4), v3(gtok[:, t, :], 4), grow, ALU.mult, t1, t_pin)
            if t == 1:
                prep()
        release(ch, tk)

        u, ymix = v3(mem(2048, M + 18432), 4), gA
        cur = {}
        gt_read = [None, None]

        def conv_a(j, which):
            def run():
                if j == 0:
                    cur[which] = chunk()
                ch = cur[which]
                b, tk = dproj(ch, 512, j, None)
                if j == 1:
                    prep()
                if j == 3:
                    release(ch, tk)
                if which == "c":
                    free[b] = cur["gc", j] = acopy(u[:, j, :], banks[b][:, :], tk, t_s0[1])
                elif which == "v":
                    free[b] = tt(u[:, j, :], banks[b][:, :], u[:, j, :], ALU.mult, tk, cur["gc", j])
                    cw = col["conv_w"]
                    y, x_ = (z.rearrange("p (r c) -> p r c", c=64) for z in (ymix[:, j, :], u[:, j, :]))
                    ts(ymix[:, j, :], u[:, j, :], cw[:, 4 + j:5 + j], None, ALU.mult, None, cur["ga"])
                    stt(y[:, :, 1:64], x_[:, :, 0:63], cw[:, j:j + 1], y[:, :, 1:64], ALU.mult, ALU.add)
                    stt(y[:, :, 0:63], x_[:, :, 1:64], cw[:, 8 + j:9 + j], y[:, :, 0:63], ALU.mult, ALU.add)
                else:
                    free[b] = cur["y"] = tt(ymix[:, j, :], banks[b][:, :], ymix[:, j, :], ALU.mult, tk)
            return run

        def ada_late(c):
            def run():
                cur["ada"] = ada_chunk(c)
            return run

        fillers += [conv_a(j, "c") for j in range(4)] + [ada_late(c) for c in range(4, 8)]
        gla(0, t_g0, t_v)
        fill(8)
        cur["ga"] = now(PE)[0]
        t_g1 = gates_math(1, t_sigb, t_q, *now(PE))
        for j in range(4):
            conv_a(j, "v")()
        fillers += [conv_a(j, "b") for j in range(4)] + [ada_late(c) for c in range(8, 12)]
        t_gla = gla(1, t_g1, t_v)
        fill(8)

        xres = v3(mem(4 * D, M + 8192), 4)
        t_gl = now(PE, V, A)
        SP.wait(*t_gl)
        for i in range(2):
            SP.silent(lambda e, i=i: e.dma_start(xres[:, 2 * i:2 * i + 2, :], x_v[:, 2 * i:2 * i + 2, :])
                      .then_inc(s_x[i], 16))
        YH, YL = memR(2048, M + 16384), memR(2048, M)
        t_yh = chained(A, lambda e, h=YH: e.activation(h, flat(ymix), ACT.Copy), (cur["y"], *t_gl))
        t_yl = chained(G, lambda e, l=YL, h=YH: e.tensor_tensor(l, flat(ymix), h.bitcast(F32), ALU.subtract), (t_yh,))

        osb = gE
        ssq = small[:, 122:138]
        sq = v3(mem(2048, M + 2048), 4)
        for t in range(4):
            free[t] = t1 = (vcopy if t % 2 else acopy)(osb[:, t, :], banks[t][:, :], t_gla, *t_gl)
            t1 = act(ACT.Square, sq[:, t, :], osb[:, t, :], t1)
            t_ssq = reduce(ssq[:, 4 * t:4 * t + 4], v3(sq[:, t, :], 4), ALU.add, t1)
        turn["order"] = list(range(8))
        for t in range(4):
            for half in range(2):
                b, tk = turn_tok(xres, t, half, (s_x[t // 2], 32))
                free[b] = acopy(XT[:, 4 * half:4 * half + 4, 128 * t:128 * t + 128],
                                v3(banks[b][:, :], 4), tk, *t_gl)
        t_xtok = now(A)
        t1 = act(ACT.Sqrt, ssq, ssq, t_ssq, bias=epst, scale=1.0 / 128)
        recip(ssq, ssq, t1)
        MH, ML = v3(memR(2048, M + 14336), 4), v3(memR(2048, M + 4096), 4)
        for t in range(4):
            o4 = v3(osb[:, t, :], 4)
            tt(o4, o4, ssq[:, 4 * t:4 * t + 4].unsqueeze(2).to_broadcast([P, 4, 128]), ALU.mult)
            t1 = tt(osb[:, t, :], osb[:, t, :], gtok[:, t, :], ALU.mult)
            b = take()
            tk = transposes([(banks[b][:, 128 * h:128 * h + 128], osb[:, t, 128 * h:128 * h + 128])
                             for h in range(4)], t1)
            s_ = slice(128 * t, 128 * t + 128)
            t2 = chained(A, lambda e, b=b, h=MH[:, :, s_]: e.activation(h, v3(banks[b][:, :], 4), ACT.Copy), (tk, *t_gl))
            free[b] = t_mix = chained(V, lambda e, b=b, h=MH[:, :, s_], l=ML[:, :, s_]: e.tensor_tensor(
                l, v3(banks[b][:, :], 4), h.bitcast(F32), ALU.subtract), (t2, *t_gl))
        YH, YL = v3(YH, 4), v3(YL, 4)
        mixh = [MH[:, k, :] for k in range(4)] + [YH[:, k, :] for k in range(4)]
        mixl = [ML[:, k, :] for k in range(4)] + [YL[:, k, :] for k in range(4)]
        t_xt = [None] * 8
        for half in range(2):
            ch = chunk()
            wh, wl = v3(ch[3], 8), v3(ch[4], 8)
            for j in range(4):
                d = 4 * half + j
                s_ = slice(128 * j, 128 * j + 128)
                b = take()
                items = []
                for n, k in enumerate([4, 5, 6, 7, 0, 1, 2, 3]):
                    items += three(banks[b][:, :], wh[:, k, s_], wl[:, k, s_], mixh[k], mixl[k], n == 0, n == 7,
                                   [t_yl, t_mix][n >= 4])
                tk = mms(items, *ch[5])
                free[b] = t_xt[d] = stt(XT[:, d, :], banks[b][:, :], adaT[:, 16 + d, 0:1], XT[:, d, :],
                                        ALU.mult, ALU.add, tk, cur["ada"], *t_xtok)
                if half == 0 and j == 0:
                    prep()
            release(ch, tk)

        sqt = [mem(512, M + 18432 + 512 * i) for i in range(2)]
        rstd = mem(512, M + 19456)
        HT = v3(mem(4096, M + 14336), 8)

        def rms(t_x, *waits):
            b = take()
            read = [None, None]
            for d in range(8):
                t1 = act(ACT.Square, sqt[d % 2], XT[:, d, :], t_x[d], read[d % 2], *waits)
                read[d % 2] = tk = mms([(banks[b][:, :], onesD, sqt[d % 2], d == 0, d == 7)], t1)
            act(ACT.Ln, rstd, banks[b][:, :], tk, bias=epst)
            t1 = act(ACT.Exp, rstd, rstd, scale=-0.5)
            free[b] = t1
            return t1

        def scaled(o, gain, t_r, *waits):
            toks = []
            for d in range(8):
                toks.append(stt(o[:, d, :], XT[:, d, :], gain[:, d:d + 1], rstd, ALU.mult, ALU.mult, t_r, *waits,
                                chain=(d == 0)))
            return toks

        t1 = stt(mod[:, 2, :], adaT[:, 32:40, 0], 1.0, col["norm_ffn"], ALU.add, ALU.mult)
        t_r = rms(t_xt, *now(PE))
        toks = scaled(HT, mod[:, 2, :], t_r, *now(PE))
        t_h = []
        for d in range(8):
            t_h.append(act(ACT.Identity, HT[:, d, :], HT[:, d, :], toks[d], bias=adaT[:, 24 + d, 0:1], chain=(d == 0)))
        b = take()
        tk = mms([(banks[b][:, 16 * t:16 * t + 16], HT[:, k, 128 * t:128 * t + 128], WR[:, k, :], k == 0, k == 7)
                  for t in range(4) for k in range(8)], *t_h, t_pin)
        aff = v3(mem(64, M + 20000), 4)
        slotT = v3(mem(64, M + 20064), 4)
        red = small[:, 138:142]
        rb = red.unsqueeze(2).to_broadcast([P, 4, 16])
        free[b] = vcopy(flat(aff), banks[b][:, 0:64], tk)
        reduce(red, aff, ALU.max)
        t1 = tt(aff, aff, rb, ALU.subtract)
        t1 = act(ACT.Exp, flat(aff), flat(aff), t1)
        reduce(red, aff, ALU.add, t1)
        recip(red, red)
        t1 = tt(aff, aff, rb, ALU.mult)
        b = take()
        tk = transposes([(banks[b][0:16, 128 * t:128 * t + 128], aff[:, t, :]) for t in range(4)], t1)
        wk = [mem(512, M + 20480 + 512 * i)[0:16, :] for i in range(2)]
        top = small[0:16, 144:208]
        free[b] = vcopy(wk[0], banks[b][0:16, :], tk)
        for r in range(8):
            o8 = top[:, 8 * r:8 * r + 8]
            chained(V, lambda e, o8=o8, s=wk[r % 2]: e.max(o8, s), ())
            chained(V, lambda e, o8=o8, s=wk[r % 2], o=wk[1 - r % 2]:
                    e.match_replace(out=o, in_to_replace=o8, in_values=s, imm_value=-1.0), ())
        ts(wk[0], wk[0], 0.0, None, ALU.is_lt, None)
        ones_row = mem(512, M + 21504)[0:16, :]
        vset(ones_row, 1.0)
        chained(V, lambda e: e.tensor_tensor_scan(wk[1], ones_row, wk[0], 0.0, ALU.mult, ALU.add), ())
        t1 = tt(wk[1], wk[1], wk[0], ALU.mult)

        H2 = v3(mem(4096, M), 4)
        for t in range(4):
            for half in range(2):
                b = take()
                tk = transposes([(banks[b][:, 128 * j:128 * j + 128], HT[:, 4 * half + j, 128 * t:128 * t + 128])
                                 for j in range(4)])
                free[b] = t_h2 = acopy(H2[:, t, 512 * half:512 * half + 512], banks[b][:, :], tk)
        b = take()
        tk = transposes([(banks[b][:, 16 * t:16 * t + 16], wk[1][:, 128 * t:128 * t + 128]) for t in range(4)], t1)
        free[b] = t_slot = vcopy(flat(slotT), banks[b][:, 0:64], tk)
        t_rt = now(V, A, PE)

        xsT = [v3(mem(1024, M + 4096 + 1024 * i), 8) for i in range(2)]
        Sp = [v3(mem(512, M + 6144 + 512 * i), 4) for i in range(2)]
        Sg = [v3(mem(512, M + 7168 + 512 * i), 4) for i in range(2)]
        SgT = [mem(512, M + 8192 + 512 * i) for i in range(2)]
        ab = [mem(2048, M + 9216), mem(2048, M + 21504)]
        hT = [v3(mem(2048, M + 11264), 16), v3(mem(2048, M + 23552), 16)]
        ys = mem(1024, M + 13312)
        stm = [mem(512, M + 14336 + 512 * i) for i in range(2)]
        xs_read, sp_read, sg_read, sgt_read = [None] * 2, [None] * 2, [None] * 2, [None] * 2
        ab_read, h_read, stm_read = [None] * 2, [None] * 2, [None] * 2
        ys_read = [None]
        gathered, t_gated = {}, {}

        def gather(p):
            i = p % 2
            s4 = Sp[i].rearrange("p t (e s) -> p t e s", e=2)
            g4 = Sg[i].rearrange("p t (e s) -> p t e s", e=2)
            io = iota1.unsqueeze(1).unsqueeze(1).to_broadcast([P, 4, 2, 64])
            sl = slotT[:, :, 2 * p:2 * p + 2].unsqueeze(3).to_broadcast([P, 4, 2, 64])
            af = aff[:, :, 2 * p:2 * p + 2].unsqueeze(3).to_broadcast([P, 4, 2, 64])
            t1 = tt(s4, io, sl, ALU.is_equal, *t_rt, sp_read[i])
            t2 = tt(g4, s4, af, ALU.mult, sg_read[i])

            def rows_of(half):
                def run():
                    b = take()
                    tk = mms([(banks[b][:, 128 * j:128 * j + 128],
                               H2[:, t, 512 * half + 128 * j:512 * half + 128 * j + 128], Sp[i][:, t, :], t == 0, t == 3)
                              for j in range(4) for t in range(4)], t1, t_h2)
                    free[b] = gathered[p] = vcopy(flat(xsT[i][:, 4 * half:4 * half + 4, :]), banks[b][:, :], tk,
                                                  xs_read[i])
                    sp_read[i] = tk
                return run

            def gates_of():
                b = take()
                sg_read[i] = tk = transposes([(banks[b][:, 128 * t:128 * t + 128], Sg[i][:, t, :]) for t in range(4)], t2)
                free[b] = t_gated[p] = vcopy(SgT[i], banks[b][:, :], tk, sgt_read[i])

            return [rows_of(0), rows_of(1), gates_of]

        def combine(p, t_y):
            i = p % 2

            def pair_of(d0):
                def run():
                    for d in (d0, d0 + 1):
                        b = take()
                        tk = mms([(banks[b][:, :], ys[:, 128 * d:128 * d + 128], SgT[i], True, True)], t_y, t_gated[p])
                        free[b] = t_xt[d] = stt(XT[:, d, :], banks[b][:, :], adaT[:, 40 + d, 0:1], XT[:, d, :],
                                                ALU.mult, ALU.add, tk)
                    ys_read[0] = sgt_read[i] = tk
                return run

            return [pair_of(d0) for d0 in range(0, 8, 2)]

        def pair_chunks(w, p, parts):
            a, b_ = load(parts(w[0, 2 * p])), load(parts(w[0, 2 * p + 1]))
            return a, b_

        def up(w, p, fc):
            (n0, s0_, a0_), (n1, s1_, a1_) = pair_chunks(w, p, lambda x_: cols(x_, 512 * fc, 512))
            b = take()
            ws = [v3(s0_, 8), v3(s1_, 8)]
            items = [(banks[b][64 * e:64 * e + 64, :], xsT[p % 2][:, k, 64 * e:64 * e + 64], ws[e][:, k, :],
                      k == 0, k == 7) for k in range(8) for e in range(2)]
            tk = mms(items, a0_, a1_, gathered[p])
            slot_free[n0] = slot_free[n1] = tk
            return b, tk

        def turn_h(p, fc, t_a):
            b = take()
            tk = transposes([(banks[b][:, 128 * j:128 * j + 128], ab[p % 2][:, 512 * fc + 128 * j:512 * fc + 128 * j + 128])
                             for j in range(4)], t_a)
            free[b] = vcopy(flat(hT[p % 2][:, 4 * fc:4 * fc + 4, :]), banks[b][:, :], tk, h_read[p % 2])
            return tk, free[b]

        for piece in gather(0):
            piece()
        work = []
        for p in range(8):
            i = p % 2
            late = None
            for fc in range(4):
                b, tk = up(I["w_gate"], p, fc)
                free[b] = t1 = act(ACT.Silu, stm[fc % 2], banks[b][:, :], tk, stm_read[fc % 2])
                if work:
                    work.pop(0)()
                b, tk = up(I["w_up"], p, fc)
                free[b] = t_a = tt(ab[i][:, 512 * fc:512 * fc + 512], banks[b][:, :], stm[fc % 2], ALU.mult, tk, t1,
                                   ab_read[i])
                stm_read[fc % 2] = t_a
                if late is not None:
                    turn_h(p, fc - 1, late)
                if work:
                    work.pop(0)()
                if fc == 1 and p < 7:
                    assert not work
                    work += gather(p + 1)
                late = t_a
            xs_read[i] = tk
            ab_read[i], t_hid = turn_h(p, 3, late)
            yb = [take(), take()]
            for kc in range(4):
                (n0, s0_, a0_), (n1, s1_, a1_) = pair_chunks(I["w_down"], p, lambda x_: rows(x_, 512 * kc, 4))
                ws = [v3(s0_, 4), v3(s1_, 4)]
                tk = mms([(banks[yb[f]][64 * e:64 * e + 64, :], hT[i][:, 4 * kc + k, 64 * e:64 * e + 64],
                           ws[e][:, k, 512 * f:512 * f + 512], kc + k == 0, kc == 3 and k == 3)
                          for k in range(4) for f in range(2) for e in range(2)], a0_, a1_, t_hid)
                slot_free[n0] = slot_free[n1] = tk
            h_read[i] = tk
            free[yb[0]] = acopy(ys[:, 0:512], banks[yb[0]][:, :], tk, ys_read[0])
            free[yb[1]] = t_y = acopy(ys[:, 512:1024], banks[yb[1]][:, :], tk)
            assert not work
            work = combine(p, t_y)
        for piece in work:
            piece()
        win2 = I["w_in_2"][0]
        wup = I["w_up_2"][0]

        def qparts(slot):
            dst = slot.rearrange("p (k i g c) -> p k i g c", k=8, i=4, g=2)
            return [(dst[:, :, i, g, :], win2[:, 256 * g + 64 * i:256 * g + 64 * i + 64].rearrange("(k p) c -> p k c", p=P))
                    for g in range(2) for i in range(4)]

        def w1parts(w1):
            return lambda slot: [(slot.rearrange("p (m n) -> p m n", m=16), w1[0].rearrange("(m p) n -> p m n", p=P))]

        def oparts(slot):
            dst = v3(slot, 4)
            src = I["w_o_nsa_2"][0].rearrange("(g i d) n -> g d i n", g=2, i=4)
            return [(dst[64 * g:64 * g + 64, :, :], src[g]) for g in range(2)]

        def upparts(c):
            def parts(slot):
                v = slot.rearrange("p (k n) -> p k n", k=8)
                return [(v[:, :, 256 * h:256 * h + 256],
                         wup[:, 2816 * h + 256 * c:2816 * h + 256 * c + 256].rearrange("(k p) n -> p k n", p=P))
                        for h in range(2)]
            return parts

        def downparts(h, k0, nk):
            def parts(slot):
                return [(slot[:, 0:512 * nk].rearrange("p (k n) -> p k n", k=nk),
                         I["w_down_2"][0][128 * k0:128 * (k0 + nk), 512 * h:512 * h + 512]
                         .rearrange("(k p) n -> p k n", p=P))]
            return parts

        KD = [(0, 8), (8, 8), (16, 6)]
        specs += [(cols(win2, 1816, 512), 4096, True), (cols(win2, 1304, 512), 4096, True),
                  (cols(win2, 512, 512), 4096, True), (cols(win2, 1024, 280), 2240, True), (qparts, 4096, True),
                  (w1parts(I["w_cmp_k1_2"]), 4096, False), (w1parts(I["w_cmp_v1_2"]), 4096, False),
                  (oparts, 4096, True), (cols(win2, 2328, 512), 4096, True), (cols(win2, 2840, 512), 4096, True),
                  (rows(I["w_conv_out_2"][0], 0, 4), 4096, True), (cols(win2, 3352, 512), 4096, True),
                  (cols(win2, 3864, 512), 4096, True), (cols(I["w_out_2"][0], 0, 512), 4096, True),
                  (cols(I["w_out_2"][0], 512, 512), 4096, True)]
        specs += [(upparts(c), 4096, True) for c in range(11)]
        specs += [(downparts(h, k0, nk), 512 * nk, True) for h in range(2) for k0, nk in KD]
        specs += [(lambda slot: [(slot[:, 0:2048].rearrange("p (k n) -> p k n", k=2),
                                  I["w_ple_2"][0].rearrange("(k p) n -> p k n", p=P))], 2048, True)]
        specs += [(cols(I["w_ple_gate_2"][0], 512 * h, 512), 4096, True) for h in range(2)]
        turns["pair"] = 0
        prep()

        t_r = rms(t_xt, *now(PE))
        toks = scaled(XT, col["norm_final"], t_r)
        t_x2 = list(toks)

        sqt = [mem(512, M + 20096 + 512 * i) for i in range(2)]
        rstd = mem(512, M + 19584)
        UH, UL = v3(memR(4096, M), 8), v3(memR(4096, M + 4096), 8)
        FT = [M + 22112]

        def stats(t_x, *waits):
            b = take()
            read = [None, None]
            for d in range(8):
                t1 = act(ACT.Square, sqt[d % 2], XT[:, d, :], t_x[d], read[d % 2], *waits)
                read[d % 2] = tk = mms([(banks[b][:, :], onesD, sqt[d % 2], d == 0, d == 7)], t1)
            act(ACT.Ln, rstd, banks[b][:, :], tk, *waits, bias=epst)
            free[b] = act(ACT.Exp, rstd, rstd, scale=-0.5)
            return free[b]

        def normed(gain, t_r, *waits):
            out_, f_read = [], [None, None]
            for d in range(8):
                f = mem(512, FT[0] + 512 * (d % 2))
                h, l = UH[:, d, :], UL[:, d, :]
                t1 = stt(f, XT[:, d, :], gain[:, d:d + 1], rstd, ALU.mult, ALU.mult, t_r, f_read[d % 2], *waits,
                         chain=False)
                t2 = chained(A, lambda e, f=f, h=h: e.activation(h, f, ACT.Copy), (t1, *waits))
                t3 = chained(G if d % 2 else V, lambda e, f=f, h=h, l=l:
                             e.tensor_tensor(l, f, h.bitcast(F32), ALU.subtract), (t1, t2, *waits))
                f_read[d % 2] = t3
                out_.append([t2, t3])
            return out_

        t_r = stats(t_x2, *now(V))
        t_u = normed(col["g_mix"], t_r, *now(PE))
        q2 = v3(mem(2048, M + 8192), 4)
        KZ = mem(2048, M + 10240).rearrange("p (b g t) -> p b g t", b=2, g=2)
        VS = mem(1024, M + 12288).rearrange("p (b t n) -> p b t n", b=2, t=4)
        GT = v3(mem(96, M + 13312), 4)
        kcat = [v3(mem(1024, M + 13440 + 1024 * i), 2) for i in range(2)]
        CO = v3(own(2048, M + 15488), 4)
        CI = v3(mem(2048, M + 17536), 4)
        RB = mem(992, M + 21120).rearrange("p (m g n) -> p m g n", m=16, g=2)
        pcs = [mem(256, M + 13440 + 256 * i) for i in range(2)]
        PS = [mem(2560, M + 2560 * i) for i in range(2)]
        PTr = [mem(2560, M + 5120), mem(2560, M + 21120)]
        pcT = v3(mem(1024, M + 23680), 2)
        OT = v3(own(2048, M + 24704), 4)
        t_b2 = now(PE, A, V)
        vset(KZ.rearrange("p b g t -> p (b g t)"), 0.0, *t_b2)
        KC = v3(small[:, 208:272], 2)
        HID = small[:, 272:400].rearrange("p (h g n) -> p h g n", h=2, g=2)
        VC = v3(small[:, 400:528], 2)
        t_kz = vset(small[:, 208:400], 0.0)

        ch = chunk()
        for j in range(4):
            b, tk = dproj(ch, 512, j, t_u)
            free[b] = t_cg = act(ACT.Sigmoid, CO[:, j, :], banks[b][:, :], tk, *t_b2)
            if j == 1:
                prep()
        release(ch, tk)
        ch = chunk()
        for j in range(4):
            b, tk = dproj(ch, 512, j, None)
            free[b] = t_ci = tt(CI[:, j, :], banks[b][:, :], CO[:, j, :], ALU.mult, tk, t_cg, *t_b2)
            if j == 1:
                prep()
        release(ch, tk)

        taps = []
        cw2 = col["conv_w_2"]
        for j in range(4):
            def first(j=j):
                return ts(CO[:, j, :], CI[:, j, :], cw2[:, 120 + j:121 + j], col["conv_b"][:, j:j + 1],
                          ALU.mult, ALU.add)
            taps.append(first)
            for s in range(1, 31):
                def tap(j=j, s=s):
                    k = 4 * (30 - s) + j
                    return stt(CO[:, j, s:], CI[:, j, :T - s], cw2[:, k:k + 1], CO[:, j, s:], ALU.mult, ALU.add)
                taps.append(tap)

        def conv_taps(n):
            for _ in range(n):
                if taps:
                    cur["conv"] = taps.pop(0)()

        conv_taps(58)
        ch = chunk()
        for w_ in range(2):
            b, tk = dproj(ch, 512, w_, None)
            for g in range(2):
                for l2 in range(2):
                    free[b] = t_kc = acopy(kcat[w_][64 * l2:64 * l2 + 64, g, 0:512 - l2],
                                           banks[b][64 * g:64 * g + 64, l2:512], tk, *t_b2)
        prep()
        b, tk = dproj(ch, 512, 2, None)
        for g in range(2):
            free[b] = acopy(KZ[64 * g:64 * g + 64, 0, g, :], banks[b][64 * g:64 * g + 64, :], tk, t_kz)
        for t in range(4):
            b, tk = dprojtok(ch, 512, 384, 128, t)
            free[b] = acopy(VS[:, 0, t, :], banks[b][:, 0:128], tk, *t_b2)
        release(ch, tk)
        ch = chunk()
        b, tk = dproj(ch, 280, 0, None)
        for g in range(2):
            free[b] = acopy(KZ[64 * g:64 * g + 64, 1, g, :], banks[b][64 * g:64 * g + 64, :], tk)
        prep()
        for t in range(4):
            b, tk = dprojtok(ch, 280, 128, 128, t)
            free[b] = acopy(VS[:, 1, t, :], banks[b][:, 0:128], tk)
        for t in range(4):
            b, tk = dprojtok(ch, 280, 256, 24, t)
            free[b] = t_gt = act(ACT.Sigmoid, GT[:, t, :], banks[b][:, 0:24], tk, *t_b2)
        release(ch, tk)
        ch = chunk()
        for i in range(4):
            b, tk = dproj(ch, 512, i, None)
            free[b] = t_q2 = act(ACT.Copy, q2[:, i, :], banks[b][:, :], tk, scale=0.125)
            if i == 1:
                prep()
        release(ch, tk)
        prep()

        t_rb = None
        for w_, pos in enumerate((col["pos_k"], col["pos_v"])):
            for m in range(16):
                src = kcat[w_][:, :, 2 * m:2 * m + 481:16]
                t1 = ts(RB[:, m, :, :], src, pos[:, m:m + 1], None, ALU.add, None, t_kc, t_rb, *t_b2, chain=(m == 0))
            ch = chunk()
            w = v3(ch[2], 16)
            b = take()
            tk = mms([(banks[b][:, 64 * h:64 * h + 62], w[:, m, 128 * h:128 * h + 128],
                       RB[:, m, :, :].rearrange("p g n -> p (g n)"), m == 0, m == 15)
                      for h in range(2) for m in range(16)], *ch[5], t1)
            t_rb = tk
            release(ch, tk)
            if w_ == 0:
                prep()
            for h in range(2):
                free[b] = t1 = act(ACT.Gelu_apprx_tanh, HID[:, h, :, 0:31],
                                   v3(banks[b][:, 64 * h:64 * h + 62], 2), tk, t_kz, *now(PE))
            b = take()
            if w_ == 0:
                tk = mms([(banks[b][64 * g:64 * g + 64, 0:32], W2k[:, h, :], HID[:, h, g, :], h == 0, h == 1)
                          for g in range(2) for h in range(2)], t1, t_pin)
                for g in range(2):
                    free[b] = t_kcz = vcopy(KC[64 * g:64 * g + 64, g, :], banks[b][64 * g:64 * g + 64, 0:32], tk)
            else:
                tk = mms([(banks[b][0:32, 64 * g:64 * g + 64], HID[:, h, g, :], W2v[:, h, :], h == 0, h == 1)
                          for g in range(2) for h in range(2)], t1, t_pin)
                for i in range(4):
                    free[b] = t_vcz = vcopy(flat(VC[32 * i:32 * i + 32, :, :]), banks[b][0:32, 0:128], tk)
        t_cmp = now(PE, V, A, G)

        pc_read = [None, None]

        def compressed(t):
            mx, sm = (small[:, 528 + 8 * z + 16 * (t % 2):536 + 8 * z + 16 * (t % 2)] for z in range(2))
            b = take()
            tk = mms([(banks[b][:, 32 * (4 * g + i):32 * (4 * g + i) + 32], q2[:, i, 128 * t:128 * t + 128], KC[:, g, :],
                       True, True) for g in range(2) for i in range(4)], t_q2, t_kcz)
            pc = pcs[t % 2].rearrange("p (j c) -> p j c", j=8)
            cm = cmask[:, t, :].unsqueeze(1).to_broadcast([P, 8, 32])
            free[b] = tt(pc, banks[b][:, 0:256].rearrange("p (j c) -> p j c", j=8), cm, ALU.add, tk, pc_read[t % 2], *t_cmp)
            reduce(mx, pc, ALU.max)
            ts(mx, mx, NEG / 10, None, ALU.max, None)
            t1 = tt(pc, pc, mx.unsqueeze(2).to_broadcast([P, 8, 32]), ALU.subtract)
            t1 = act(ACT.Exp, pc, pc, t1)
            reduce(sm, pc, ALU.add, t1)
            ts(sm, sm, 1e-30, None, ALU.max, None)
            recip(sm, sm)
            tt(sm, sm, GT[:, t, 0:8], ALU.mult, t_gt)
            t1 = tt(pc, pc, sm.unsqueeze(2).to_broadcast([P, 8, 32]), ALU.mult)
            b = take()
            pc_read[t % 2] = tk = transposes([(banks[b][:, 128 * g:128 * g + 128], pcs[t % 2][:, 128 * g:128 * g + 128])
                                              for g in range(2)], t1)
            free[b] = vcopy(pcT[:, :, 128 * t:128 * t + 128], v3(banks[b][:, 0:256], 2), tk)
            return free[b]

        off = [0, 128, 384, 768]
        offk = [0, 512, 896, 1152]
        turn["order"] = [2, 3, 4, 5, 6, 7]
        st = [small[:, 144 + 24 * i:144 + 24 * i + 24] for i in range(2)]
        ps_read = [[None, None], [None, None]]
        t_scaled = {}

        def scores(un, g):
            i, br = un // 2, un % 2
            Pb = PS[un % 2]
            nm, su, ri = st[un % 2][:, 0:8], st[un % 2][:, 8:16], st[un % 2][:, 16:24]
            for t in range(4):
                N = 128 * (t + 1)
                b = take()
                tk = mms([(banks[b][:, 0:N], q2[:, i, 128 * t:128 * t + 128], KZ[:, br, g, 0:N], True, True)], *t_cmp)
                o = Pb[:, 1280 * g + off[t]:1280 * g + off[t] + N]
                j = 4 * g + t
                free[b] = chained(V, lambda e, o=o, b=b, N=N, j=j, nm=nm: e.tensor_tensor_reduce(
                    o, banks[b][:, 0:N], causal[:, 512 - N:512], 1.0, -3e38, ALU.add, ALU.max, nm[:, j:j + 1]),
                    (tk, ps_read[un % 2][g], *t_cmp), chain=(t == 0))
            t1 = ts(nm[:, 4 * g:4 * g + 4], nm[:, 4 * g:4 * g + 4], -1.0, None, ALU.mult, None)
            for t in range(4):
                N = 128 * (t + 1)
                o = Pb[:, 1280 * g + off[t]:1280 * g + off[t] + N]
                j = 4 * g + t
                t2 = act(ACT.Exp, o, o, t1, bias=nm[:, j:j + 1], accum=su[:, j:j + 1], chain=(t == 0))
            t3 = recip(ri[:, 4 * g:4 * g + 4], su[:, 4 * g:4 * g + 4], t2)
            for t in range(4):
                N = 128 * (t + 1)
                o = Pb[:, 1280 * g + off[t]:1280 * g + off[t] + N]
                j = 4 * g + t
                gi = 8 * (1 + br) + 4 * g + i
                t_scaled[un, g, t] = ts(o, o, ri[:, j:j + 1], GT[:, t, gi:gi + 1], ALU.mult, ALU.mult, t3, t_gt,
                                        lane=G, chain=(t == 0))

        ptr_read = [None, None]
        t_pt2 = {}

        def turned(un, g):
            Pb, Tb = PS[un % 2], PTr[un % 2]
            for kt in range(4):
                b = take()
                tk = transposes([(banks[b][:, 128 * t:128 * t + 128],
                                  Pb[:, 1280 * g + off[t] + 128 * kt:1280 * g + off[t] + 128 * kt + 128])
                                 for t in range(kt, 4)], *[t_scaled[un, g, t] for t in range(kt, 4)])
                o = Tb[:, 1280 * g + offk[kt]:1280 * g + offk[kt] + 512 - 128 * kt]
                free[b] = t_pt2[g, kt] = (vcopy if kt % 2 else acopy)(o, banks[b][:, 128 * kt:512], tk, ptr_read[un % 2])
            ps_read[un % 2][g] = tk

        def values(un):
            i, br = un // 2, un % 2
            Tb = PTr[un % 2]
            ob = i % 2
            items = []
            if br == 0:
                PE.wait(free[ob])
                items += [(banks[ob][64 * g:64 * g + 64, :], VC[32 * i:32 * i + 32, g, :], pcT[32 * i:32 * i + 32, g, :],
                           True, False) for g in range(2)]
            for kt in range(4):
                items += [(banks[ob][64 * g:64 * g + 64, 128 * kt:512], VS[:, br, kt, 64 * g:64 * g + 64],
                           Tb[:, 1280 * g + offk[kt]:1280 * g + offk[kt] + 512 - 128 * kt], False, False,
                           t_pt2[g, kt]) for g in range(2)]
            ptr_read[un % 2] = tk = mms(items, t_pct, t_vcz, skip=True)
            if br == 1:
                free[ob] = acopy(OT[:, i, :], banks[ob][:, :], tk)

        for g in range(2):
            scores(0, g)
            compressed(2 * g)
            t_pct = compressed(2 * g + 1)
        for un in range(8):
            for g in range(2):
                if un < 7:
                    scores(un + 1, g)
                turned(un, g)
            values(un)
            conv_taps(3)
        t_at = now(PE, A, V, G)
        turn["order"] = list(range(8))

        OH, OL, t_ot = split(M + 22656, M + 24704, 2048, *t_at)
        OH, OL = v3(OH, 4), v3(OL, 4)
        FT[0] = M + 20096
        t_u = normed(col["g_mix"], t_r, *t_at)
        YAo = v3(own(4096, M + 8192), 8)
        YB = v3(mem(4096, M + 17536), 8)
        ytmp = [mem(512, M + 21632 + 512 * i) for i in range(2)]
        ch = chunk()
        for d in range(8):
            wh, wl = v3(ch[3], 4), v3(ch[4], 4)
            b = take()
            s_ = slice(128 * d, 128 * d + 128)
            items = []
            for i in range(4):
                items += three(banks[b][:, :], wh[:, i, s_], wl[:, i, s_], OH[:, i, :], OL[:, i, :], i == 0, i == 3)
            tk = mms(items, *ch[5], t_ot)
            free[b] = t_ya = acopy(YAo[:, d, :], banks[b][:, :], tk, *t_at)
            if d == 3:
                prep()
        release(ch, tk)
        yt_read = [None, None]
        for c in range(2):
            ch = chunk()
            for j in range(4):
                d = 4 * c + j
                b, tk = dproj(ch, 512, j, t_u)
                free[b] = t1 = act(ACT.Sigmoid, ytmp[d % 2], banks[b][:, :], tk, yt_read[d % 2], *t_at, t_ot)
                yt_read[d % 2] = tt(YAo[:, d, :], YAo[:, d, :], ytmp[d % 2], ALU.mult, t1, t_ya)
                conv_taps(6)
                if j == 1:
                    prep()
            release(ch, tk)
        conv_taps(200)

        b = take()
        tk = group(banks[b][:, :], [(onesC, CO[:, j, :]) for j in range(4)], cur["conv"])
        for j in range(4):
            t1 = tt(CO[:, j, :], CO[:, j, :], banks[b][:, :], ALU.subtract, tk)
        free[b] = t1
        b = take()
        read = [None, None]
        t_yt = now(V, A, PE)
        for j in range(4):
            t2 = act(ACT.Square, ytmp[j % 2], CO[:, j, :], t1, read[j % 2], *t_yt)
            read[j % 2] = tk = mms([(banks[b][:, :], onesC, ytmp[j % 2], j == 0, j == 3)], t2)
        rs2 = ytmp[0]
        act(ACT.Ln, rs2, banks[b][:, :], tk, bias=epst)
        free[b] = t2 = act(ACT.Exp, rs2, rs2, scale=-0.5)
        for j in range(4):
            t1 = tt(CO[:, j, :], CO[:, j, :], rs2, ALU.mult, t2)
            t_co = act(ACT.Silu, CO[:, j, :], CO[:, j, :], t1, scale=col["ln_g"][:, j:j + 1],
                       bias=col["ln_b"][:, j:j + 1])
        CH, CL, t_cs = split(M + 22656, M + 15488, 2048, t_co, *t_yt)
        CH, CL = v3(CH, 4), v3(CL, 4)

        ch = chunk()
        for d in range(8):
            wh, wl = v3(ch[3], 4), v3(ch[4], 4)
            b = take()
            s_ = slice(128 * d, 128 * d + 128)
            items = []
            for i in range(4):
                items += three(banks[b][:, :], wh[:, i, s_], wl[:, i, s_], CH[:, i, :], CL[:, i, :], i == 0, i == 3)
            tk = mms(items, *ch[5], t_cs)
            free[b] = t_yb = act(ACT.Identity, YB[:, d, :], banks[b][:, :], tk, t_cs, bias=col["b_co"][:, d:d + 1])
            if d == 3:
                prep()
        release(ch, tk)
        t_m = [None] * 8
        for c in range(2):
            ch = chunk()
            for j in range(4):
                d = 4 * c + j
                b, tk = dproj(ch, 512, j, None)
                free[b] = t1 = act(ACT.Sigmoid, ytmp[d % 2], banks[b][:, :], tk, yt_read[d % 2], t_co, *now(V))
                tt(ytmp[d % 2], ytmp[d % 2], YB[:, d, :], ALU.mult, t1, t_yb)
                yt_read[d % 2] = tt(YAo[:, d, :], YAo[:, d, :], ytmp[d % 2], ALU.add)
                if j == 1:
                    prep()
            release(ch, tk)
        t_zm = now(PE)
        MH, ML = v3(memR(4096, M), 8), v3(memR(4096, M + 8192), 8)
        for d in range(8):
            t1 = chained(A, lambda e, h=MH[:, d, :], f=YAo[:, d, :]: e.activation(h, f, ACT.Copy), (*t_zm, *now(V)))
            t_m[d] = chained(V, lambda e, h=MH[:, d, :], l=ML[:, d, :], f=YAo[:, d, :]:
                             e.tensor_tensor(l, f, h.bitcast(F32), ALU.subtract), (t1,))
        for half in range(2):
            ch = chunk()
            for j in range(4):
                d = 4 * half + j
                b, tk = dproj(ch, 512, j, t_m, MH, ML)
                free[b] = t_xt[d] = tt(XT[:, d, :], banks[b][:, :], XT[:, d, :], ALU.add, tk)
                if j == 1:
                    prep()
            release(ch, tk)

        sqt = [mem(512, M + 23552 + 512 * i) for i in range(2)]
        rstd = mem(512, M + 24576)
        FT[0] = M + 25088
        t_r = stats(t_xt, *now(PE, V))
        t_u = normed(col["g_ffn"], t_r, *now(PE))
        GF = v3(mem(22 * 512, M + 8192), 22)
        fg = [mem(512, M + 19456 + 512 * i) for i in range(2)]
        fv = [mem(512, M + 20480 + 512 * i) for i in range(2)]
        f_read = [None, None]
        ptok = v3(mem(4 * 256, M + 26112), 4)
        SP.wait(*now(PE, V, A))
        SP.silent(lambda e: e.dma_start(ptok, I["p_2"][0, 0].rearrange("(t p) d -> p t d", p=P)).then_inc(s_pt, 16))

        def conv3(o, b, tk, t, *waits):
            w0, w1_, w2_ = col["fcw01"][:, t:t + 1], col["fcw01"][:, 44 + t:45 + t], col["fcw2"][:, t:t + 1]
            t1 = act(ACT.Identity, o, banks[b][:, :], tk, *waits, scale=w2_, bias=col["fcb"][:, t:t + 1])
            stt(o[:, 1:], banks[b][:, 0:T - 1], w1_, o[:, 1:], ALU.mult, ALU.add, t1)
            return stt(o[:, 2:], banks[b][:, 0:T - 2], w0, o[:, 2:], ALU.mult, ALU.add)

        t_f0 = now(PE, V)
        for c in range(11):
            ch = chunk()
            for j in range(2):
                t = 2 * c + j
                b, tk = dproj(ch, 512, j, t_u)
                free[b] = t1 = conv3(fg[t % 2], b, tk, t, f_read[t % 2], *t_f0)
                t2 = act(ACT.Gelu_apprx_tanh, fg[t % 2], fg[t % 2], t1)
                b, tk = dproj(ch, 512, 2 + j, None)
                free[b] = t1 = conv3(fv[t % 2], b, tk, 22 + t, f_read[t % 2])
                f_read[t % 2] = t_gg = tt(GF[:, t, :], fg[t % 2], fv[t % 2], ALU.mult, t2)
                if j == 0:
                    prep()
            release(ch, tk)
        gh = [(memR(512, M + 21504 + 1024 * i), memR(512, M + 22016 + 1024 * i)) for i in range(2)]
        g_read = [None, None]
        for h in range(2):
            bs = [take() for _ in range(4)]
            for k0, nk in KD:
                ch = chunk()
                wh, wl = v3(ch[3], nk), v3(ch[4], nk)
                for k in range(nk):
                    kk = k0 + k
                    xh, xl = gh[kk % 2]
                    t1 = chained(A, lambda e, xh=xh, kk=kk: e.activation(xh, GF[:, kk, :], ACT.Copy),
                                 (t_gg, g_read[kk % 2]))
                    t2 = chained(V, lambda e, xh=xh, xl=xl, kk=kk: e.tensor_tensor(xl, GF[:, kk, :], xh.bitcast(F32),
                                                                                  ALU.subtract), (t1,))
                    items = []
                    for j in range(4):
                        s_ = slice(128 * j, 128 * j + 128)
                        items += three(banks[bs[j]][:, :], wh[:, k, s_], wl[:, k, s_], xh, xl, kk == 0, kk == 21)
                    g_read[kk % 2] = tk = mms(items, *ch[5], t2)
                    if k == nk // 2:
                        prep()
                release(ch, tk)
            for j in range(4):
                d = 4 * h + j
                free[bs[j]] = t_xt[d] = tt(XT[:, d, :], banks[bs[j]][:, :], XT[:, d, :], ALU.add, tk)

        PH, PL = v3(memR(1024, M + 8192), 2), v3(memR(1024, M + 9216), 2)
        E = v3(mem(4096, M + 10240), 8)
        t_e0 = now(PE, V, A)
        t_ps = []
        for j in range(2):
            b = take()
            tk = transposes([(banks[b][:, 128 * t:128 * t + 128], ptok[:, t, 128 * j:128 * j + 128])
                             for t in range(4)], (s_pt, 16))
            t1 = chained(A, lambda e, b=b, j=j: e.activation(PH[:, j, :], banks[b][:, :], ACT.Copy), (tk, *t_e0))
            free[b] = chained(V, lambda e, b=b, j=j: e.tensor_tensor(PL[:, j, :], banks[b][:, :],
                                                                     PH[:, j, :].bitcast(F32), ALU.subtract),
                              (t1, *t_e0))
            t_ps.append(free[b])
        ch = chunk()
        for d in range(8):
            b, tk = dproj(ch, 1024, d, t_ps, PH, PL, 2)
            free[b] = t_e = acopy(E[:, d, :], banks[b][:, :], tk, *t_e0)
            if d == 3:
                prep()
        release(ch, tk)
        t_r = stats(t_xt, *now(V))
        t_u = normed(col["g_ple"], t_r, *now(PE))
        for half in range(2):
            ch = chunk()
            for j in range(4):
                d = 4 * half + j
                b, tk = dproj(ch, 512, j, t_u)
                free[b] = t1 = act(ACT.Sigmoid, fg[d % 2], banks[b][:, :], tk, *now(V))
                tt(fg[d % 2], fg[d % 2], E[:, d, :], ALU.mult, t1, t_e)
                t_xt[d] = tt(XT[:, d, :], XT[:, d, :], fg[d % 2], ALU.add)
                if j == 1:
                    prep()
            release(ch, tk)
        t_r = stats(t_xt)
        toks = scaled(XT, col["g_final"], t_r)
        OUTT = v3(mem(4096, M), 4)
        s_out = sem("s_out")
        t_o = now(PE, V)
        o_v = out[0].rearrange("(t p) d -> p t d", p=P)
        for t in range(4):
            for half in range(2):
                b = take()
                tk = transposes([(banks[b][:, 128 * j:128 * j + 128], XT[:, 4 * half + j, 128 * t:128 * t + 128])
                                 for j in range(4)], *toks)
                free[b] = (vcopy if half else acopy)(OUTT[:, t, 512 * half:512 * half + 512], banks[b][:, :], tk, *t_o)
            SP.wait(*now(V, A))
            SP.silent(lambda e, t=t: e.dma_start(o_v[:, t, :], OUTT[:, t, :]).then_inc(s_out, 16))
        SP.wait((s_out, 64))

        block = ctx.enter_context(nc.Block())

        def play(lane):
            def body(e):
                for make in lane.queue:
                    make(e)
            return body

        block.sync(play(SP))
        block.scalar(play(A))
        block.vector(play(V))
        block.gpsimd(play(G))
        block.tensor(play(PE))


_INS = ["x", "c", "ctx", "c_ctx", "w_ada", "b_ada", "norm_mix", "norm_ffn", "w_in", "lb_logits", "hg_norm", "conv_w",
        "w_out", "w_router", "w_gate", "w_up", "w_down", "norm_final", "p_2", "g_mix_2", "w_in_2", "cmp_pos_k_2",
        "cmp_pos_v_2", "w_cmp_k1_2", "w_cmp_k2_2", "w_cmp_v1_2", "w_cmp_v2_2", "w_o_nsa_2", "conv_w_2", "conv_b_2",
        "conv_ln_g_2", "conv_ln_b_2", "w_conv_out_2", "b_conv_out_2", "w_out_2", "g_ffn_2", "w_up_2", "ffn_conv_w_2",
        "ffn_conv_b_2", "w_down_2", "g_ple_2", "w_ple_gate_2", "w_ple_2", "g_final_2"]


def kernel(**inputs):
    import numpy as _np
    import concourse.bacc as _bacc
    from concourse import mybir as _mybir
    from concourse.bass_utils import run_bass_kernel_spmd as _run

    nc = _bacc.Bacc("TRN2", target_bir_lowering=False, num_devices=1)
    arrays, aps = {}, {}
    for name in _INS:
        a = _np.ascontiguousarray(inputs[name])
        arrays[f"in_{name}_dram"] = a
        aps[name] = nc.dram_tensor(f"in_{name}_dram", a.shape, _mybir.dt.from_np(a.dtype), kind="ExternalInput").ap()
    out = nc.dram_tensor("out_0_dram", (1, 512, 1024), _mybir.dt.float32, kind="ExternalOutput").ap()
    build_program(nc, aps, out)
    r = _run(nc, [arrays], core_ids=[0])
    return r.results[0]["out_0_dram"]
```

```python
from contextlib import ExitStack

import concourse.bass as bass
from concourse import mybir

F32 = mybir.dt.float32
F32R = mybir.dt.float32r
I32 = mybir.dt.int32
ALU = mybir.AluOpType
ACT = mybir.ActivationFunctionType
AX = mybir.AxisListType

P = 128
T = 512
D = 1024
NS = 4
SLOT = 4096
EPS = 1e-6
NEG = -1e30


class Lane:

    def __init__(self, sem):
        self.sem, self.n, self.queue, self.seen = sem, 0, [], {}

    def wait(self, *tokens):
        for tok in tokens:
            if tok is None:
                continue
            if isinstance(tok, list):
                self.wait(*tok)
                continue
            sem, value = tok
            if self.seen.get(id(sem), 0) < value:
                self.seen[id(sem)] = value
                self.queue.append(lambda e, sem=sem, value=value: e.wait_ge(sem, value))

    def counted(self, make):
        self.n += 1
        self.queue.append(lambda e, make=make: make(e).then_inc(self.sem, 1))
        return (self.sem, self.n)

    def silent(self, make):
        self.queue.append(lambda e, make=make: make(e))


def build_program(nc, I, out):
    ctx = ExitStack()
    with ctx:
        def sem(name):
            return ctx.enter_context(nc.semaphore(name))

        PE, V, A, G, SP = (Lane(sem(n)) for n in ("s_pe", "s_ve", "s_ac", "s_po", "s_sp"))

        def chained(lane, make, waits, chain=True):
            lane.wait(*waits)
            if chain and lane.n:
                lane.wait((lane.sem, lane.n))
            return lane.counted(make)

        NW = 52960
        M = 24832
        def lay(name, at, n, kind):
            if at == 0:
                with nc.sbuf_tensor(name, [P, n], kind) as piece:
                    return piece
            with nc.sbuf_tensor(f"below_{name}", [P, at], F32), nc.sbuf_tensor(name, [P, n], kind) as piece:
                return piece

        low, high = lay("low", 0, M, F32), lay("high", M, NW - M, F32)
        banks = [ctx.enter_context(nc.psum_tensor(f"bank{i}", [P, 512], F32)) for i in range(8)]
        cursor = [0]

        rounded, full = {}, {}

        def mem(n, at=None):
            if at is None:
                at = cursor[0]
                cursor[0] += n
            assert at + n <= NW, (at, n)
            assert at + n <= M or at >= M
            return low[:, at:at + n] if at < M else high[:, at - M:at - M + n]

        def memR(n, at):
            if (at, n) not in rounded:
                rounded[at, n] = lay(f"r_{at}_{n}", at, n, F32R)
            return rounded[at, n][:, :]

        def own(n, at):
            if (at, n) not in full:
                full[at, n] = lay(f"f_{at}_{n}", at, n, F32)
            return full[at, n][:, :]

        def v3(ap, a):
            return ap.rearrange("p (a b) -> p a b", a=a)

        def flat(ap):
            return ap.rearrange("p a b -> p (a b)")

        def now(*lanes):
            return [(l.sem, l.n) for l in lanes if l.n]

        def act(func, o, i, *waits, bias=0.0, scale=1.0, accum=None, chain=True):
            if accum is None:
                return chained(A, lambda e: e.activation(o, i, func, bias=bias, scale=scale), waits, chain)
            return chained(A, lambda e: e.activation(o, i, func, bias=bias, scale=scale, accum_out=accum), waits, chain)

        def tt(o, a, b, op, *waits, chain=True, lane=None):
            return chained(lane or V, lambda e: e.tensor_tensor(o, a, b, op), waits, chain)

        def ts(o, a, s1, s2, op0, op1, *waits, chain=True, lane=None):
            if s2 is None:
                return chained(lane or V, lambda e: e.tensor_scalar(o, a, s1, None, op0), waits, chain)
            return chained(lane or V, lambda e: e.tensor_scalar(o, a, s1, s2, op0, op1), waits, chain)

        def stt(o, a, s, b, op0, op1, *waits, chain=True):
            return chained(V, lambda e: e.scalar_tensor_tensor(out=o, in0=a, scalar=s, in1=b, op0=op0, op1=op1),
                           waits, chain)

        def vcopy(o, i, *waits, chain=True):
            return chained(V, lambda e: e.tensor_copy(o, i), waits, chain)

        def acopy(o, i, *waits, chain=True):
            return chained(A, lambda e: e.activation(o, i, ACT.Copy), waits, chain)

        def vset(o, val, *waits, chain=True):
            return chained(V, lambda e: e.memset(o, val), waits, chain)

        def reduce(o, i, op, *waits):
            return chained(V, lambda e: e.tensor_reduce(o, i, AX.X, op), waits)

        def recip(o, i, *waits):
            return chained(V, lambda e: e.reciprocal(o, i), waits)

        def mms(items, *waits, skip=False):
            PE.wait(*waits)
            for n, (o, l, r, st, sp, *tok) in enumerate(items):
                PE.wait(*tok)
                mk = lambda e, o=o, l=l, r=r, st=st, sp=sp: e.matmul(o, l, r, start=st, stop=sp, skip_group_check=skip)
                if n == len(items) - 1:
                    return PE.counted(mk)
                PE.silent(mk)

        def group(o, pairs, *waits):
            last = len(pairs) - 1
            return mms([(o, l, r, n == 0, n == last) for n, (l, r) in enumerate(pairs)], *waits)

        def transposes(items, *waits):
            PE.wait(*waits)
            for n, (o, i) in enumerate(items):
                k = i.shape[0]
                mk = lambda e, o=o, i=i, k=k: e.transpose(o, i, ident[0:k, 0:k])
                if n == len(items) - 1:
                    return PE.counted(mk)
                PE.silent(mk)

        free = [None] * 8
        turn = {"order": list(range(8)), "i": 0}

        def take():
            b = turn["order"][turn["i"] % len(turn["order"])]
            turn["i"] += 1
            PE.wait(free[b])
            return b

        slot_at = [cursor[0] + SLOT * i for i in range(NS)]
        cursor[0] += SLOT * NS
        landed = [sem(f"s_w{i}") for i in range(NS)]
        slot_count = [0] * NS
        slot_free = [None] * NS
        turns = {"plain": 0, "pair": 0}

        def fetch(s, parts):
            slot = own(SLOT, slot_at[s])
            for dst, src in parts(slot):
                slot_count[s] += 16
                SP.silent(lambda e, dst=dst, src=src: e.dma_start(dst, src).then_inc(landed[s], 16))
            return slot, (landed[s], slot_count[s])

        def load(parts):
            s = turns["plain"] % NS
            turns["plain"] += 1
            SP.wait(slot_free[s])
            slot, tok = fetch(s, parts)
            return s, slot, tok

        specs, prepared = [], []

        def prep():
            prep_divide(*prep_load())

        def prep_load():
            if not specs:
                return ()
            parts, words, divide = specs.pop(0)
            p = turns["pair"] % 2
            turns["pair"] += 1
            a, b_ = 2 * p, 2 * p + 1
            SP.wait(slot_free[a], slot_free[b_])
            return (words, divide, a, b_, *fetch(a, parts))

        def prep_divide(*chunk_):
            for step in division(*chunk_):
                step()

        def division(*chunk_):
            if not chunk_:
                return []
            words, divide, a, b_, slot, arrived = chunk_
            if not divide:
                prepared.append((a, b_, slot, None, None, [arrived]))
                return []
            hi, lo = memR(SLOT, slot_at[b_]), memR(SLOT, slot_at[a])
            toks = []
            prepared.append((a, b_, slot, hi[:, 0:words], lo[:, 0:words], toks))
            was_free = slot_free[b_]
            step = words // 4

            def piece(i):
                s_ = slice(step * i, step * i + step)

                def run():
                    t1 = chained(A, lambda e: e.activation(hi[:, s_], slot[:, s_], ACT.Copy), (arrived, was_free))
                    toks.append(chained(V if i % 2 else G, lambda e: e.tensor_tensor(
                        lo[:, s_], slot[:, s_], hi[:, s_].bitcast(F32), ALU.subtract), (t1, arrived)))
                return run

            return [piece(i) for i in range(4)]

        def quarter(ch, k, nk):
            return ch[5][:((k + 1) * 4 - 1) // nk + 1]

        def chunk():
            return prepared.pop(0)

        def release(ch, tok):
            slot_free[ch[0]] = slot_free[ch[1]] = tok

        def split(at_hi, at_full, words, *waits, lane=None):
            whole = own(words, at_full)
            hi, lo = memR(words, at_hi), memR(words, at_full)
            t1 = chained(A, lambda e: e.activation(hi, whole, ACT.Copy), waits)
            t2 = chained(lane or V, lambda e: e.tensor_tensor(lo, whole, hi.bitcast(F32), ALU.subtract), (t1, *waits))
            return hi, lo, t2

        def three(o, wh, wl, xh, xl, st, sp, *tok):
            return [(o, wh, xh, st, False, *tok), (o, wl, xh, False, False), (o, wh, xl, False, sp)]

        def cols(w, c0, n):
            def parts(slot):
                dst = slot[:, 0:8 * n].rearrange("p (k n) -> p k n", k=8)
                return [(dst, w[:, c0:c0 + n].rearrange("(k p) n -> p k n", p=P))]
            return parts

        def rows(w, r0, nk):
            def parts(slot):
                dst = slot[:, 0:nk * D].rearrange("p (k n) -> p k n", k=nk)
                return [(dst, w[r0:r0 + nk * P, :].rearrange("(k p) n -> p k n", p=P))]
            return parts

        ident = mem(128)
        onesD = mem(128)
        onesC = mem(128)
        ones256 = mem(256)
        epst = mem(1)
        blkmask = [mem(128) for _ in range(2)]
        resets = mem(T)
        iota1 = mem(64)
        causal = mem(T)
        cmask = v3(mem(4 * 32), 4)
        sel = mem(2)
        PT = v3(mem(5 * 128), 5)
        adaT = mem(96).rearrange("p (t r) -> p t r", r=2)
        mod = v3(mem(3 * 8), 3)
        small = mem(600)
        gainrow = mem(128)
        WR = v3(mem(128), 8)
        W2k, W2v = v3(mem(128), 2), v3(mem(128), 2)
        CP = v3(mem(8 * 32), 8)
        XT_AT = cursor[0]
        mem(8 * T)
        XT = v3(own(8 * T, XT_AT), 8)
        assert cursor[0] <= M and NW - M >= 28128, (cursor[0], M)

        def gp(make, *w):
            return chained(G, make, w)

        def setg(o, val, *w):
            return gp(lambda e: e.memset(o, val), *w)

        def asel(o, op, fill, base, pattern, mult, *w):
            return gp(lambda e: e.affine_select(out=o, in_=o, compare_op=op, fill=fill, base=base,
                                                pattern=pattern, channel_multiplier=mult), *w)

        setg(ident, 0.0)
        t_id = asel(ident, ALU.not_equal, 1.0, 0, [[-1, 128]], 1)
        setg(epst, EPS)
        setg(sel, 0.0)
        for q in range(4):
            t_sel = asel(sel, ALU.not_equal, 1.0, -32 * q, [[-1, 2]], 1)
        setg(onesD, 1.0 / D)
        setg(onesC, 1.0 / 512)
        setg(ones256, 1.0)
        for m in blkmask:
            setg(m, 0.0)
            for c in range(4):
                setg(m[32 * c:32 * c + 32, 32 * c:32 * c + 32], 1.0)
        asel(blkmask[0], ALU.is_ge, 0.0, 0, [[1, 128]], -1)
        asel(blkmask[1], ALU.is_ge, 0.0, 0, [[-1, 128]], 1)
        setg(resets, 1.0)
        setg(resets.rearrange("p (n c) -> p n c", c=32)[:, :, 0:1], 0.0)
        setg(causal, 0.0)
        asel(causal[:, 384:512], ALU.is_ge, NEG, 0, [[-1, 128]], 1)
        setg(flat(cmask), 0.0)
        for t in range(4):
            asel(cmask[:, t, :], ALU.is_ge, NEG, 128 * t - 31, [[-16, 32]], 1)
        setg(cmask[:, :, 31:32], NEG)
        gp(lambda e: e.iota(iota1.bitcast(I32), pattern=[[1, 64]], base=1, channel_multiplier=0))
        t_const = gp(lambda e: e.tensor_copy(iota1, iota1.bitcast(I32)))

        xtok = v3(mem(4 * D, M), 4)
        xn = v3(mem(4 * D, M + 4096), 4)
        ctok = v3(mem(2 * D, M + 8192), 2)
        stage = v3(mem(5 * 128, M + 11264), 5)
        s_st0, s_st, s_c, s_p, s_pt = (sem(n) for n in ("s_st0", "s_st", "s_c", "s_p", "s_pt"))
        s_x = [sem("s_x0"), sem("s_x1")]
        t_stz = vset(flat(stage), 0.0)
        col, fill_at, n_st = {}, [0] * 5, [0, 0]

        def lrows(name, src, n, tile):
            r0 = fill_at[tile]
            fill_at[tile] += n
            assert fill_at[tile] <= 128
            n_st[min(tile, 1)] += 16
            lane, s_ = (G, s_st) if tile else (SP, s_st0)
            lane.silent(lambda e, d=stage[r0:r0 + n, tile, :], s=src: e.dma_start(d, s).then_inc(s_, 16))
            col[name] = PT[:, tile, r0:r0 + n]

        x_v = I["x"][0].rearrange("(t p) d -> p t d", p=P)
        for i in range(2):
            SP.silent(lambda e, i=i: e.dma_start(xtok[:, 2 * i:2 * i + 2, :], x_v[:, 2 * i:2 * i + 2, :])
                      .then_inc(s_x[i], 16))
        SP.wait(t_stz)
        R = "(r c) -> r c"
        lrows("c", I["c"][0].rearrange(R, c=P), 8, 0)
        lrows("c_ctx", I["c_ctx"].rearrange(R, c=P), 8, 0)
        lrows("b_ada", I["b_ada"][0].rearrange(R, c=P), 48, 0)
        lrows("norm_mix", I["norm_mix"][0].rearrange(R, c=P), 8, 0)
        lrows("norm_ffn", I["norm_ffn"][0].rearrange(R, c=P), 8, 0)
        lrows("norm_final", I["norm_final"].rearrange(R, c=P), 8, 0)
        lrows("lb", I["lb_logits"].rearrange("a b (r c) -> (a b r) c", c=P), 16, 0)
        lrows("conv_w", I["conv_w"][0].rearrange("k (r c) -> (k r) c", c=P), 12, 0)

        def late_loads():
            G.wait(t_stz)
            lrows("conv_w_2", I["conv_w_2"][0].rearrange("k (r c) -> (k r) c", c=P), 124, 1)
            lrows("fcw01", I["ffn_conv_w_2"][0][0:2, :].rearrange("k (r c) -> (k r) c", c=P), 88, 2)
            lrows("g_mix", I["g_mix_2"][0].rearrange(R, c=P), 8, 2)
            lrows("conv_b", I["conv_b_2"][0].rearrange(R, c=P), 4, 2)
            lrows("ln_g", I["conv_ln_g_2"][0].rearrange(R, c=P), 4, 2)
            lrows("ln_b", I["conv_ln_b_2"][0].rearrange(R, c=P), 4, 2)
            lrows("b_co", I["b_conv_out_2"][0].rearrange(R, c=P), 8, 2)
            lrows("fcw2", I["ffn_conv_w_2"][0][2:3, :].rearrange("k (r c) -> (k r) c", c=P), 44, 3)
            lrows("fcb", I["ffn_conv_b_2"][0].rearrange(R, c=P), 44, 3)
            lrows("g_ffn", I["g_ffn_2"][0].rearrange(R, c=P), 8, 3)
            lrows("g_ple", I["g_ple_2"][0].rearrange(R, c=P), 8, 3)
            lrows("g_final", I["g_final_2"].rearrange(R, c=P), 8, 3)
            lrows("pos_k", I["cmp_pos_k_2"][0].rearrange("(m l) d -> m (l d)", l=2), 16, 3)
            lrows("pos_v", I["cmp_pos_v_2"][0].rearrange("(m l) d -> m (l d)", l=2), 16, 4)
            for dst, src in (
                (gainrow, I["hg_norm"].to_broadcast([P, 128])),
                (WR, I["w_router"][0].rearrange("(k p) n -> p k n", p=P)),
                (W2k, I["w_cmp_k2_2"][0].rearrange("(k p) n -> p k n", p=P)),
                (W2v, I["w_cmp_v2_2"][0].rearrange("(k p) n -> p k n", p=P)),
            ):
                G.silent(lambda e, dst=dst, src=src: e.dma_start(dst, src).then_inc(s_p, 16))

        late_loads()
        t_pin = (s_p, 64)
        t_stage, t_late = (s_st0, n_st[0]), (s_st, n_st[1])

        ada_at = [slot_at[2], slot_at[3], M + 14336, M + 18432]
        s_ada = [sem(f"s_ada{c}") for c in range(4)]
        win = I["w_in"][0]

        def ada_load(c):
            slot = own(4096, ada_at[c])
            for dst, src in cols(I["w_ada"][0], 512 * c, 512)(slot):
                SP.silent(lambda e, dst=dst, src=src: e.dma_start(dst, src).then_inc(s_ada[c], 16))
            return slot, (s_ada[c], 16)

        specs += [(cols(win, c0, 512), 4096, True) for c0 in (512, 1536, 1024, 0, 2048, 3072)]
        specs += [(cols(I["w_ada"][0], 512 * c, 512), 4096, False) for c in range(4, 8)]
        specs += [(cols(win, c0, 512), 4096, True) for c0 in (3584, 2560)]
        specs += [(cols(I["w_ada"][0], 512 * c, 512), 4096, False) for c in range(8, 12)]
        specs += [(cols(I["w_out"][0], 512 * h, 512), 4096, True) for h in range(2)]
        early = [ada_load(c) for c in range(4)]
        first_chunk = prep_load()
        SP.silent(lambda e: e.dma_start(ctok, I["ctx"][0].rearrange("(t p) d -> p t d", p=P)).then_inc(s_c, 16))

        ss = small[:, 48:54]
        for i in range(4):
            act(ACT.Square, xn[:, i, :], xtok[:, i, :], (s_x[i // 2], 16), accum=ss[:, i:i + 1])
        t1 = act(ACT.Sqrt, ss[:, 0:4], ss[:, 0:4], t_const, bias=epst, scale=1.0 / D)
        t_rs = recip(ss[:, 0:4], ss[:, 0:4], t1)

        b = take()
        tk = transposes([(banks[b][:, 0:128], stage[:, 0, :])], t_stage, t_id)
        free[b] = t_pt = vcopy(PT[:, 0, :], banks[b][:, 0:128], tk)

        t_cz = vset(flat(CP), 0.0)
        act(ACT.Silu, CP[:, :, 0], col["c"], t_cz, t_pt)
        t_cp = act(ACT.Silu, CP[:, :, 1], col["c_ctx"])

        adatmp = [mem(512, M + 25600 + 512 * i) for i in range(2)]
        ada_free = [None, None]

        def ada_begin(c):
            if c < 4:
                slot, arrived = early[c]
            else:
                ch = chunk()
                slot, arrived = ch[2], ch[5]
            w = v3(slot, 8)
            b = take()
            tk = mms([(banks[b][32 * (k % 4):32 * (k % 4) + 32, :], CP[:, k, :], w[:, k, :], k < 4, k >= 4)
                      for k in range(8)], arrived, t_cp)
            if c >= 4:
                release(ch, tk)
            elif c < 2:
                slot_free[2 + c] = tk
            free[b] = ada_got[c] = acopy(adatmp[c % 2], banks[b][:, :], tk, ada_free[c % 2])
            if c >= 4 and c not in (7, 11):
                prep()

        ada_got = {}

        def ada_end(c):
            b = take()
            tk = mms([(banks[b][:, 2 * j:2 * j + 2], adatmp[c % 2][:, 128 * j:128 * j + 128], sel, True, True)
                      for j in range(4)], ada_got[c], t_sel)
            ada_free[c % 2] = tk
            bb = col["b_ada"][:, 4 * c:4 * c + 4].unsqueeze(2).to_broadcast([P, 4, 2])
            free[b] = tt(adaT[:, 4 * c:4 * c + 4, :], banks[b][:, 0:8].rearrange("p (t r) -> p t r", r=2), bb,
                         ALU.add, tk, t_pt)
            if c in (7, 11):
                prep()
            return free[b]

        def turn_tok(src, t, half, *waits):
            b = take()
            tk = transposes([(banks[b][:, 128 * j:128 * j + 128],
                              src[:, t, 512 * half + 128 * j:512 * half + 128 * j + 128]) for j in range(4)], *waits)
            return b, tk

        for t in range(4):
            if t > 1:
                ada_begin(t - 2)
                ada_end(t - 2)
            t1 = ts(xn[:, t, :], xtok[:, t, :], ss[:, t:t + 1], None, ALU.mult, None, t_rs)
            for half in range(2):
                b, tk = turn_tok(xn, t, half, t1, t_id)
                free[b] = (vcopy if half else acopy)(XT[:, 4 * half:4 * half + 4, 128 * t:128 * t + 128],
                                                     v3(banks[b][:, :], 4), tk)
        t_tr = now(V, A)
        t_xn = now(PE)

        for c in range(2, 4):
            ada_begin(c)
            ada_end(c)
        prep_divide(*first_chunk)
        stt(mod[:, 0, :], adaT[:, 8:16, 0], 1.0, col["norm_mix"], ALU.add, ALU.mult)
        t_mod = stt(mod[:, 1, :], adaT[:, 8:16, 1], 1.0, col["norm_mix"], ALU.add, ALU.mult)

        UH, UL = v3(memR(4096, M + 14336), 8), v3(memR(4096, XT_AT), 8)
        HCH, HCL = v3(memR(2048, M + 18432), 8), v3(memR(2048, M + 12288), 8)
        HF = XT
        t_pe = now(PE)
        t_u = []
        for d in range(8):
            t1 = ts(HF[:, d, :], HF[:, d, :], mod[:, 0, d:d + 1], adaT[:, d, 0:1], ALU.mult, ALU.add, *t_tr,
                    chain=(d == 0))
            t2 = chained(A, lambda e, o=UH[:, d, :], f=HF[:, d, :]: e.activation(o, f, ACT.Copy), (t1, *t_pe),
                         chain=(d == 0))
            t3 = chained(G if d % 2 else V, lambda e, o=UL[:, d, :], f=HF[:, d, :], h=UH[:, d, :]:
                         e.tensor_tensor(o, f, h.bitcast(F32), ALU.subtract),
                         (t2, t1), chain=False)
            t_u.append([t2, t3])
        lb, oml, noml = small[:, 0:8], small[:, 8:16], small[:, 16:24]
        tm, e0, e1 = small[:, 24:32], small[:, 32:40], small[:, 40:48]
        a0, a1 = col["lb"][:, 0:8], col["lb"][:, 8:16]
        tt(tm, a0, a1, ALU.max)
        tt(e0, a0, tm, ALU.subtract)
        t1 = tt(e1, a1, tm, ALU.subtract)
        act(ACT.Exp, e0, e0, t1)
        t1 = act(ACT.Exp, e1, e1)
        tt(tm, e0, e1, ALU.add, t1)
        recip(tm, tm)
        tt(lb, e0, tm, ALU.mult)
        ts(oml, lb, -1.0, 1.0, ALU.mult, ALU.add)
        t_lb = ts(noml, oml, -1.0, None, ALU.mult, None)

        b = take()
        tk = transposes([(banks[b][:, 128 * (i - 1):128 * i], stage[:, i, :]) for i in range(1, 5)], t_late)
        free[b] = t_pt2 = vcopy(flat(PT[:, 1:5, :]), banks[b][:, :], tk)

        CF = v3(own(2048, M + 12288), 8)
        for i in range(2):
            act(ACT.Square, xn[:, 3, :], ctok[:, i, :], (s_c, 16), *t_xn, accum=ss[:, 4 + i:5 + i])
        t1 = act(ACT.Sqrt, ss[:, 4:6], ss[:, 4:6], bias=epst, scale=1.0 / D)
        t_rc = recip(ss[:, 4:6], ss[:, 4:6], t1)
        t_cn = [ts(ctok[:, t, :], ctok[:, t, :], ss[:, 4 + t:5 + t], None, ALU.mult, None, t_rc) for t in range(2)]

        def context():
            for t in range(2):
                for half in range(2):
                    b, tk = turn_tok(ctok, t, half, t_cn[t])
                    free[b] = acopy(CF[:, 4 * half:4 * half + 4, 128 * t:128 * t + 128], v3(banks[b][:, :], 4), tk)
            t_ctr = now(A)
            for d in range(8):
                t3 = ts(CF[:, d, :], CF[:, d, :], mod[:, 1, d:d + 1], adaT[:, d, 1:2], ALU.mult, ALU.add, *t_ctr,
                        chain=(d == 0))
            t4 = chained(A, lambda e: e.activation(HCH, CF, ACT.Copy), (t3,))
            return [t4, chained(V, lambda e: e.tensor_tensor(HCL, CF, HCH.bitcast(F32), ALU.subtract), (t4,))]

        def dproj(ch, n, j, t_in, xh=None, xl=None, nk=8):
            xh, xl = (UH, UL) if xh is None else (xh, xl)
            wh, wl = (z[:, 0:nk * n].rearrange("p (k n) -> p k n", k=nk) for z in (ch[3], ch[4]))
            s_ = slice(128 * j, 128 * j + 128)
            b = take()
            items = []
            for k in range(nk):
                items += three(banks[b][:, :], wh[:, k, s_], wl[:, k, s_], xh[:, k, :], xl[:, k, :], k == 0,
                               k == nk - 1, quarter(ch, k, nk), t_in[k] if t_in else None)
            return b, mms(items)

        def dfour(ch, n, t_in, nk=8, xh=None, xl=None):
            xh, xl = (UH, UL) if xh is None else (xh, xl)
            wh, wl = (z[:, 0:nk * n].rearrange("p (k n) -> p k n", k=nk) for z in (ch[3], ch[4]))
            bs = [take() for _ in range(4)]
            items = []
            for k in range(nk):
                for j in range(4):
                    s_ = slice(128 * j, 128 * j + 128)
                    items += three(banks[bs[j]][:, :], wh[:, k, s_], wl[:, k, s_], xh[k] if isinstance(xh, list) else xh[:, k, :],
                                   xl[:, k, :], k == 0, k == nk - 1, quarter(ch, k, nk), t_in[k])
            return bs, mms(items)

        def dprojtok(ch, n, c0, nc_, t, xh=None, xl=None, *waits):
            xh, xl = (UH, UL) if xh is None else (xh, xl)
            wh, wl = (z[:, 0:8 * n].rearrange("p (k n) -> p k n", k=8) for z in (ch[3], ch[4]))
            s_ = slice(128 * t, 128 * t + 128)
            b = take()
            items = []
            for k in range(8):
                items += three(banks[b][:, 0:nc_], xh[:, k, s_], xl[:, k, s_], wh[:, k, c0:c0 + nc_],
                               wl[:, k, c0:c0 + nc_], k == 0, k == 7, quarter(ch, k, 8))
            return b, mms(items, *waits)

        gA, gB, gD, gE = (v3(own(2048, M + 2048 * i), 4) for i in range(4))
        qT = v3(mem(2048, M + 8192), 4)
        vtok = v3(mem(2048, M + 10240), 4)
        gtok = v3(mem(2048, M + 12288), 4)
        S0 = mem(1024, M + 20480).rearrange("p (d h v) -> p d h v", d=2, h=4)
        U = v3(mem(2048, M + 21504), 4)
        Sring = mem(1024, M + 23552).rearrange("p (r h v) -> p r h v", r=2, h=4)
        scT = [mem(512, M + 24576 + 512 * i) for i in range(2)]
        dec = small[:, 54:118].rearrange("p (h n) -> p h n", h=4)
        last = small[:, 118:122]
        cA, cB = v3(mem(1024, M + 4096), 4), v3(mem(1024, M + 5120), 4)
        cK, vctx = v3(mem(1024, M + 6144), 2), v3(mem(1024, M + 7168), 2)
        gK = [gA, U]

        turn["order"] = [4, 5, 6, 7]

        def gate_scalars(d, h):
            i = 4 * d + h
            return lb[:, i:i + 1], oml[:, i:i + 1], noml[:, i:i + 1]

        def ctx_gate(ch, d, *waits):
            wh, wl = v3(ch[3], 8), v3(ch[4], 8)
            for h2 in range(2):
                b = take()
                items = []
                for hh in range(2):
                    s_ = slice(256 * h2 + 128 * hh, 256 * h2 + 128 * hh + 128)
                    for k in range(8):
                        items += three(banks[b][:, 256 * hh:256 * hh + 256], wh[:, k, s_], wl[:, k, s_], HCH[:, k, :],
                                       HCL[:, k, :], k == 0, k == 7)
                tk = mms(items, *ch[5], t_hc)
                free[b] = act(ACT.Sigmoid, cA[:, 2 * h2:2 * h2 + 2, :], v3(banks[b][:, :], 2), tk, *waits)
            for h in range(4):
                l_, o_, _ = gate_scalars(d, h)
                t1 = act(ACT.Ln, cB[:, h, :], cA[:, h, :], t_lb, *waits, scale=o_, bias=l_)
            for h in range(4):
                _, o_, n_ = gate_scalars(d, h)
                x_ = cB[:, h, ::-1] if d else cB[:, h, :]
                chained(V, lambda e, x_=x_: e.tensor_tensor_scan(x_, ones256, x_, 0.0, ALU.mult, ALU.add), (t1, t_const))
                ts(cA[:, h, :], cA[:, h, :], n_, o_, ALU.mult, ALU.add)
            t2 = vcopy(last, cB[:, :, 0 if d else 255])
            for h in range(4):
                t3 = act(ACT.Exp, cB[:, h, :], cB[:, h, :], t2, scale=-1.0, bias=last[:, h:h + 1])
            return tt(cA, cA, cB, ALU.mult, t3)

        def ctx_state(d, t_c, t_vc):
            for t in range(2):
                b = take()
                tk = transposes([(banks[b][:, 128 * h:128 * h + 128], cA[:, h, 128 * t:128 * t + 128])
                                 for h in range(4)], t_c)
                free[b] = t_k = vcopy(cK[:, t, :], banks[b][:, :], tk)
            b = take()
            tk = mms([(banks[b][:, 128 * h:128 * h + 128], cK[:, t, 128 * h:128 * h + 128],
                       vctx[:, t, 128 * h:128 * h + 128], t == 0, t == 1) for h in range(4) for t in range(2)], t_k, t_vc)
            free[b] = vcopy(S0[:, d, :, :].rearrange("p h v -> p (h v)"), banks[b][:, :], tk)
            return free[b]

        def gates_math(d, t_sig, t_q, *waits):
            K = gK[d]
            for h in range(4):
                l_, o_, _ = gate_scalars(d, h)
                t1 = act(ACT.Ln, gB[:, h, :], K[:, h, :], t_sig, *waits, scale=o_, bias=l_)
            for h in range(4):
                _, o_, n_ = gate_scalars(d, h)
                x_ = gB[:, h, ::-1] if d else gB[:, h, :]
                chained(V, lambda e, x_=x_: e.tensor_tensor_scan(x_, resets, x_, 0.0, ALU.mult, ALU.add),
                        (t1, t_const, *waits))
                t2 = ts(K[:, h, :], K[:, h, :], n_, o_, ALU.mult, ALU.add)
            act(ACT.Exp, dec, gB.rearrange("p h (n c) -> p h n c", c=32)[:, :, :, 0 if d else 31], t2)
            t_e = act(ACT.Exp, gE, gB, scale=-1.0)
            t_d = act(ACT.Exp, gD, gB)
            tt(gE, gE, K, ALU.mult, t_e)
            tt(gD, gD, qT, ALU.mult, t_d, t_q)
            db = dec.rearrange("p h n -> p (h n)").unsqueeze(2).to_broadcast([P, 64, 32])
            return tt(K.rearrange("p h (n c) -> p (h n) c", c=32), gE.rearrange("p h (n c) -> p (h n) c", c=32), db,
                      ALU.mult)

        fillers = []

        def fill(n=1):
            for _ in range(n):
                if fillers:
                    fillers.pop(0)()

        def gla(d, t_gates, t_v):
            K = gK[d]
            for t in range(4):
                b = take()
                tk = transposes([(banks[b][:, 128 * h:128 * h + 128], K[:, h, 128 * t:128 * t + 128])
                                 for h in range(4)], t_gates)
                free[b] = t_kt = vcopy(gB[:, t, :], banks[b][:, :], tk)
            for i in range(2):
                vset(scT[i], 0.0, *now(PE))
            read = [None, None]
            def scored(t):
                b = take()
                s_ = slice(128 * t, 128 * t + 128)
                tk = mms([(banks[b][:, 128 * h:128 * h + 128], gE[:, h, s_], gD[:, h, s_], True, True)
                          for h in range(4)], t_gates)
                mk = blkmask[d].bitcast(I32).unsqueeze(1).to_broadcast([P, 4, 128])
                sc, bk = v3(scT[t % 2], 4), v3(banks[b][:, :], 4)
                free[b] = chained(V, lambda e, sc=sc, mk=mk, bk=bk: e.copy_predicated(sc, mk, bk),
                                  (tk, t_const, read[t % 2]))
                return free[b]

            t_sc = scored(0)
            for t in range(4):
                t_this = t_sc
                if t < 3:
                    t_sc = scored(t + 1)
                read[t % 2] = tk = mms([(banks[t][:, 128 * h:128 * h + 128], scT[t % 2][:, 128 * h:128 * h + 128],
                                         vtok[:, t, 128 * h:128 * h + 128], d == 0 and h == 0, False)
                                        for h in range(4)], t_this, t_v, skip=True)
            prev, t_prev = S0[:, d, :, :], t_s0[d]
            ring_read = [None, None]
            for i, n in enumerate(range(15, -1, -1) if d else range(16)):
                t, c = n // 4, n % 4
                pp = slice(32 * c, 32 * c + 32)
                if i < 15:
                    b = take()
                    tkv = mms([(banks[b][:, 128 * h:128 * h + 128], gB[pp, t, 128 * h:128 * h + 128],
                                vtok[pp, t, 128 * h:128 * h + 128], True, True) for h in range(4)], t_kt, t_v)
                tk = mms([(banks[t][pp, 128 * h:128 * h + 128], gD[:, h, 32 * n:32 * n + 32], prev[:, h, :],
                           False, False) for h in range(4)], t_prev, skip=True)
                if i > 0:
                    ring_read[(i - 1) % 2] = tk
                if i < 15:
                    nxt = Sring[:, i % 2, :, :]
                    V.wait(*now(V))
                    for h in range(4):
                        t_prev = stt(nxt[:, h, :], prev[:, h, :], dec[:, h, n:n + 1],
                                     banks[b][:, 128 * h:128 * h + 128], ALU.mult, ALU.add, tkv,
                                     ring_read[i % 2], chain=False)
                    free[b] = t_prev
                    prev = nxt
                fill()
            return tk

        t_s0 = [None, None]
        t_pre = now(PE, V, A)
        ch = chunk()
        bs, tk = dfour(ch, 512, t_u)
        prep()
        for h in range(4):
            free[bs[h]] = t_sig = act(ACT.Sigmoid, gA[:, h, :], banks[bs[h]][:, :], tk, *t_pre)
        t_hc = context()
        gate_ch, ch = ch, chunk()
        t_ca = now(PE, V, A)
        for t in range(4):
            b, tk = dprojtok(ch, 512, 0, 512, t)
            free[b] = t_v = acopy(vtok[:, t, :], banks[b][:, :], tk, *t_pre)
            if t == 1:
                t_k0 = ctx_gate(gate_ch, 0, *t_ca)
                release(gate_ch, now(PE))
        prep()
        for t in range(2):
            b, tk = dprojtok(ch, 512, 0, 512, t, HCH, HCL)
            free[b] = t_vc = acopy(vctx[:, t, :], banks[b][:, :], tk, *t_ca)
        release(ch, tk)
        t_s0[0] = ctx_state(0, t_k0, t_vc)
        ch = chunk()
        t_k1 = ctx_gate(ch, 1, t_s0[0])
        for h in range(4):
            b, tk = dproj(ch, 512, h, None)
            free[b] = t_sigb = act(ACT.Sigmoid, U[:, h, :], banks[b][:, :], tk, *t_pre)
            if h == 0:
                prep()
        release(ch, tk)
        t_s0[1] = ctx_state(1, t_k1, t_vc)
        ch = chunk()
        for h in range(4):
            b, tk = dproj(ch, 512, h, None)
            free[b] = t_q = acopy(qT[:, h, :], banks[b][:, :], tk, *t_pre)
            if h == 1:
                prep()
        release(ch, tk)
        t_g0 = gates_math(0, t_sig, t_q, t_s0[1])
        ch = chunk()
        grow = gainrow.unsqueeze(1).to_broadcast([P, 4, 128])
        for t in range(4):
            b, tk = dprojtok(ch, 512, 0, 512, t)
            free[b] = t1 = act(ACT.Silu, gtok[:, t, :], banks[b][:, :], tk, t_s0[1])
            tt(v3(gtok[:, t, :], 4), v3(gtok[:, t, :], 4), grow, ALU.mult, t1, t_pin)
            if t == 1:
                prep()
        release(ch, tk)

        u, ymix = v3(mem(2048, M + 18432), 4), gA
        YH, YL = v3(memR(2048, M + 18432), 4), v3(memR(2048, M), 4)
        cur = {}
        gt_read = [None, None]

        def conv_a(j, which):
            held = {}

            def half(ch, b, ks):
                items = []
                for k in ks:
                    wh, wl = v3(ch[3], 8), v3(ch[4], 8)
                    s_ = slice(128 * j, 128 * j + 128)
                    items += three(banks[b][:, :], wh[:, k, s_], wl[:, k, s_], UH[:, k, :], UL[:, k, :], k == 0, k == 7,
                                   quarter(ch, k, 8))
                return mms(items)

            def begin():
                if j == 0:
                    cur[which] = chunk()
                held["b"] = take()
                half(cur[which], held["b"], range(4))

            def end():
                ch, b = cur[which], held["b"]
                tk = half(ch, b, range(4, 8))
                if j == 1:
                    prep()
                if j == 3:
                    release(ch, tk)
                if which == "c":
                    free[b] = cur["gc", j] = acopy(u[:, j, :], banks[b][:, :], tk, t_s0[1])
                elif which == "v":
                    free[b] = tt(u[:, j, :], banks[b][:, :], u[:, j, :], ALU.mult, tk, cur["gc", j])
                    cw = col["conv_w"]
                    y, x_ = (z.rearrange("p (r c) -> p r c", c=64) for z in (ymix[:, j, :], u[:, j, :]))
                    ts(ymix[:, j, :], u[:, j, :], cw[:, 4 + j:5 + j], None, ALU.mult, None, cur["ga"])
                    stt(y[:, :, 1:64], x_[:, :, 0:63], cw[:, j:j + 1], y[:, :, 1:64], ALU.mult, ALU.add)
                    stt(y[:, :, 0:63], x_[:, :, 1:64], cw[:, 8 + j:9 + j], y[:, :, 0:63], ALU.mult, ALU.add)
                else:
                    free[b] = t1 = tt(ymix[:, j, :], banks[b][:, :], ymix[:, j, :], ALU.mult, tk)
                    t2 = chained(A, lambda e: e.activation(YH[:, j, :], ymix[:, j, :], ACT.Copy), (t1,))
                    cur["y", j] = chained(G, lambda e: e.tensor_tensor(YL[:, j, :], ymix[:, j, :],
                                                                       YH[:, j, :].bitcast(F32), ALU.subtract), (t2,))

            return [begin, end]

        def ada_late(c):
            def end():
                cur["ada"] = ada_end(c)
            return [lambda: ada_begin(c), end]

        def pieces(*lists):
            return [piece for l in lists for piece in l]

        fillers += pieces(*[conv_a(j, "c") for j in range(4)], *[ada_late(c) for c in range(4, 8)])
        gla(0, t_g0, t_v)
        fill(len(fillers))
        cur["ga"] = now(PE)[0]
        t_g1 = gates_math(1, t_sigb, t_q, *now(PE))
        fillers += pieces(*[conv_a(j, "v") for j in range(4)])
        fill(8)
        fillers += pieces(*[conv_a(j, "b") for j in range(4)], *[ada_late(c) for c in range(8, 12)])
        t_gla = gla(1, t_g1, t_v)
        fill(len(fillers))

        stat_at = {"sq": [M + 20480, M + 20992]}
        rstd = mem(512, M + 21504)

        def hold():
            b = take()
            turn["order"] = [x_ for x_ in turn["order"] if x_ != b]
            return b

        def let_go(b):
            i_ = turn["i"] % len(turn["order"])
            turn["order"] = turn["order"][i_:] + turn["order"][:i_] + [b]
            turn["i"] = 0

        def stat_begin(gains):
            return {"banks": [hold() for _ in gains], "gains": gains, "read": [None, None], "n": 0, "k": 0, "tk": None}

        def stat_add(st_, d, *waits):
            for i_, (b, g_) in enumerate(zip(st_["banks"], st_["gains"])):
                k = st_["k"] % 2
                st_["k"] += 1
                o = mem(512, stat_at["sq"][k])
                sc = 1.0 if isinstance(g_, float) else g_[:, d:d + 1]
                t1 = act(ACT.Square, o, XT[:, d, :], t_xt[d], st_["read"][k], *waits, scale=sc)
                st_["read"][k] = st_["tk"] = mms([(banks[b][:, :], onesD, o, st_["n"] == 0, st_["n"] == 7)], t1)
            st_["n"] += 1

        def stat_end(st_, o, *waits):
            b = st_["banks"][0]
            act(ACT.Ln, o, banks[b][:, :], st_["tk"], *waits, bias=epst)
            free[b] = act(ACT.Exp, o, o, scale=-0.5)
            let_go(b)
            return free[b]

        xres = v3(mem(4 * D, M + 8192), 4)
        t_gl = now(PE, V, A, G)
        SP.wait(*t_gl)
        for i in range(2):
            SP.silent(lambda e, i=i: e.dma_start(xres[:, 2 * i:2 * i + 2, :], x_v[:, 2 * i:2 * i + 2, :])
                      .then_inc(s_x[i], 16))

        MH, ML = v3(memR(2048, M + 14336), 4), v3(memR(2048, M + 4096), 4)
        mixh = [MH[:, k, :] for k in range(4)] + [YH[:, k, :] for k in range(4)]
        mixl = [ML[:, k, :] for k in range(4)] + [YL[:, k, :] for k in range(4)]

        def wout(ch, bs, js, ks, first, last, tok):
            wh, wl = v3(ch[3], 8), v3(ch[4], 8)
            items = []
            for k in ks:
                for b, j in zip(bs, js):
                    s_ = slice(128 * j, 128 * j + 128)
                    items += three(banks[b][:, :], wh[:, k, s_], wl[:, k, s_], mixh[k], mixl[k], k == first,
                                   k == last, quarter(ch, k, 8), tok(k))
            return mms(items)

        ch = chunk()
        bs = [take() for _ in range(4)]
        wout(ch, bs, range(4), range(4, 8), 4, 3, lambda k: cur["y", k - 4])

        osb = gE
        ssq = small[:, 122:138]
        sq = v3(mem(2048, M + 2048), 4)
        for t in range(4):
            free[t] = t1 = (vcopy if t % 2 else acopy)(osb[:, t, :], banks[t][:, :], t_gla, *t_gl)
            t1 = act(ACT.Square, sq[:, t, :], osb[:, t, :], t1)
            t_ssq = reduce(ssq[:, 4 * t:4 * t + 4], v3(sq[:, t, :], 4), ALU.add, t1)
        turn["order"] = [0, 1, 2, 3]
        t1 = act(ACT.Sqrt, ssq, ssq, t_ssq, bias=epst, scale=1.0 / 128)
        recip(ssq, ssq, t1)
        t_o = []
        for t in range(4):
            o4 = v3(osb[:, t, :], 4)
            tt(o4, o4, ssq[:, 4 * t:4 * t + 4].unsqueeze(2).to_broadcast([P, 4, 128]), ALU.mult)
            t_o.append(tt(osb[:, t, :], osb[:, t, :], gtok[:, t, :], ALU.mult))
        for t in range(4):
            b = take()
            tk = transposes([(banks[b][:, 128 * h:128 * h + 128], osb[:, t, 128 * h:128 * h + 128])
                             for h in range(4)], t_o[t])
            s_ = slice(128 * t, 128 * t + 128)
            t2 = chained(A, lambda e, b=b, h=MH[:, :, s_]: e.activation(h, v3(banks[b][:, :], 4), ACT.Copy), (tk, *t_gl))
            free[b] = t_mix = chained(V, lambda e, b=b, h=MH[:, :, s_], l=ML[:, :, s_]: e.tensor_tensor(
                l, v3(banks[b][:, :], 4), h.bitcast(F32), ALU.subtract), (t2, *t_gl))
        for t in range(4):
            for half in range(2):
                b, tk = turn_tok(xres, t, half, (s_x[t // 2], 32))
                free[b] = acopy(XT[:, 4 * half:4 * half + 4, 128 * t:128 * t + 128],
                                v3(banks[b][:, :], 4), tk, *t_gl)
        t_xtok = now(A)
        t_xt = [None] * 8

        def residual(d, b, tk):
            free[b] = t_xt[d] = stt(XT[:, d, :], banks[b][:, :], adaT[:, 16 + d, 0:1], XT[:, d, :],
                                    ALU.mult, ALU.add, tk, cur["ada"], *t_xtok)

        prep()
        for j in range(4):
            tk = wout(ch, [bs[j]], [j], range(4), 4, 3, lambda k: t_mix)
            residual(j, bs[j], tk)
        release(ch, tk)
        turn["order"] = list(range(8))
        ch = chunk()
        sq_stat = stat_begin([1.0])
        for j in range(4):
            b = take()
            tk = wout(ch, [b], [j], [4, 5, 6, 7, 0, 1, 2, 3], 4, 3, lambda k: None)
            residual(4 + j, b, tk)
            stat_add(sq_stat, j)
            if j:
                stat_add(sq_stat, 3 + j)
        stat_add(sq_stat, 7)
        release(ch, tk)

        def scaled(o, gain, t_r, *waits):
            toks = []
            for d in range(8):
                toks.append(stt(o[:, d, :], XT[:, d, :], gain[:, d:d + 1], rstd, ALU.mult, ALU.mult, t_r, *waits,
                                chain=(d == 0)))
            return toks
        HT = v3(mem(4096, M + 14336), 8)

        t1 = stt(mod[:, 2, :], adaT[:, 32:40, 0], 1.0, col["norm_ffn"], ALU.add, ALU.mult)
        t_r = stat_end(sq_stat, rstd)
        toks = scaled(HT, mod[:, 2, :], t_r, *now(PE))
        t_h = []
        for d in range(8):
            t_h.append(act(ACT.Identity, HT[:, d, :], HT[:, d, :], toks[d], bias=adaT[:, 24 + d, 0:1], chain=(d == 0)))
        b = take()
        tk = mms([(banks[b][0:16, :], WR[:, k, :], HT[:, k, :], k == 0, k == 7, t_h[k]) for k in range(8)], t_pin)
        wk = [mem(512, M + 20480 + 512 * i)[0:16, :] for i in range(2)]
        ones_row = mem(512, M + 22016)[0:16, :]
        vset(ones_row, 1.0)
        free[b] = t1 = vcopy(wk[1], banks[b][0:16, :], tk)
        b = take()
        tk = transposes([(banks[b][:, 16 * t:16 * t + 16], wk[1][:, 128 * t:128 * t + 128]) for t in range(4)], t1)
        aff = v3(mem(64, M + 20000), 4)
        slotT = v3(mem(64, M + 20064), 4)
        red = small[:, 138:142]
        rb = red.unsqueeze(2).to_broadcast([P, 4, 16])
        free[b] = vcopy(flat(aff), banks[b][:, 0:64], tk)
        reduce(red, aff, ALU.max)
        t1 = tt(aff, aff, rb, ALU.subtract)
        t1 = act(ACT.Exp, flat(aff), flat(aff), t1)
        reduce(red, aff, ALU.add, t1)
        recip(red, red)
        t1 = tt(aff, aff, rb, ALU.mult)
        b = take()
        tk = transposes([(banks[b][0:16, 128 * t:128 * t + 128], aff[:, t, :]) for t in range(4)], t1)
        top = small[0:16, 144:208]
        free[b] = vcopy(wk[0], banks[b][0:16, :], tk)
        for r in range(8):
            o8 = top[:, 8 * r:8 * r + 8]
            chained(V, lambda e, o8=o8, s=wk[r % 2]: e.max(o8, s), ())
            chained(V, lambda e, o8=o8, s=wk[r % 2], o=wk[1 - r % 2]:
                    e.match_replace(out=o, in_to_replace=o8, in_values=s, imm_value=-1.0), ())
        ts(wk[0], wk[0], 0.0, None, ALU.is_lt, None)
        chained(V, lambda e: e.tensor_tensor_scan(wk[1], ones_row, wk[0], 0.0, ALU.mult, ALU.add), ())
        t1 = tt(wk[1], wk[1], wk[0], ALU.mult)

        H2 = v3(mem(4096, M), 4)
        for t in range(4):
            for half in range(2):
                b = take()
                tk = transposes([(banks[b][:, 128 * j:128 * j + 128], HT[:, 4 * half + j, 128 * t:128 * t + 128])
                                 for j in range(4)])
                free[b] = t_h2 = acopy(H2[:, t, 512 * half:512 * half + 512], banks[b][:, :], tk)
        b = take()
        tk = transposes([(banks[b][:, 16 * t:16 * t + 16], wk[1][:, 128 * t:128 * t + 128]) for t in range(4)], t1)
        free[b] = t_slot = vcopy(flat(slotT), banks[b][:, 0:64], tk)
        t_rt = now(V, A, PE)

        xsT = [v3(mem(1024, M + 4096 + 1024 * i), 8) for i in range(2)]
        Sp = [v3(mem(512, M + 6144 + 512 * i), 4) for i in range(2)]
        Sg = [v3(mem(512, M + 7168 + 512 * i), 4) for i in range(2)]
        SgT = [mem(512, M + 8192 + 512 * i) for i in range(2)]
        ab = [mem(2048, M + 9216), mem(2048, M + 21504)]
        hT = [v3(mem(2048, M + 11264), 16), v3(mem(2048, M + 23552), 16)]
        ys = mem(1024, M + 13312)
        stm = [mem(512, M + 14336 + 512 * i) for i in range(2)]
        xs_read, sp_read, sg_read, sgt_read = [None] * 2, [None] * 2, [None] * 2, [None] * 2
        ab_read, h_read, stm_read = [None] * 2, [None] * 2, [None] * 2
        ys_read = [None]
        gathered, t_gated = {}, {}

        def gather(p):
            i = p % 2
            s4 = Sp[i].rearrange("p t (e s) -> p t e s", e=2)
            g4 = Sg[i].rearrange("p t (e s) -> p t e s", e=2)
            io = iota1.unsqueeze(1).unsqueeze(1).to_broadcast([P, 4, 2, 64])
            sl = slotT[:, :, 2 * p:2 * p + 2].unsqueeze(3).to_broadcast([P, 4, 2, 64])
            af = aff[:, :, 2 * p:2 * p + 2].unsqueeze(3).to_broadcast([P, 4, 2, 64])
            t1 = tt(s4, io, sl, ALU.is_equal, *t_rt, sp_read[i])
            t2 = tt(g4, s4, af, ALU.mult, sg_read[i])

            def rows_of(half):
                def run():
                    b = take()
                    tk = mms([(banks[b][:, 128 * j:128 * j + 128],
                               H2[:, t, 512 * half + 128 * j:512 * half + 128 * j + 128], Sp[i][:, t, :], t == 0, t == 3)
                              for j in range(4) for t in range(4)], t1, t_h2)
                    free[b] = gathered[p] = vcopy(flat(xsT[i][:, 4 * half:4 * half + 4, :]), banks[b][:, :], tk,
                                                  xs_read[i])
                    sp_read[i] = tk
                return run

            def gates_of():
                b = take()
                sg_read[i] = tk = transposes([(banks[b][:, 128 * t:128 * t + 128], Sg[i][:, t, :]) for t in range(4)], t2)
                free[b] = t_gated[p] = vcopy(SgT[i], banks[b][:, :], tk, sgt_read[i])

            return [rows_of(0), rows_of(1), gates_of]

        def combine(p, t_y):
            i = p % 2

            def pair_of(d0):
                def run():
                    for d in (d0, d0 + 1):
                        b = take()
                        tk = mms([(banks[b][:, :], ys[:, 128 * d:128 * d + 128], SgT[i], True, True)], t_y, t_gated[p])
                        free[b] = t_xt[d] = stt(XT[:, d, :], banks[b][:, :], adaT[:, 40 + d, 0:1], XT[:, d, :],
                                                ALU.mult, ALU.add, tk)
                    ys_read[0] = sgt_read[i] = tk
                return run

            return [pair_of(d0) for d0 in range(0, 8, 2)]

        def pair_chunks(w, p, parts):
            a, b_ = load(parts(w[0, 2 * p])), load(parts(w[0, 2 * p + 1]))
            return a, b_

        def up(w, p, fc):
            (n0, s0_, a0_), (n1, s1_, a1_) = pair_chunks(w, p, lambda x_: cols(x_, 512 * fc, 512))
            b = take()
            ws = [v3(s0_, 8), v3(s1_, 8)]
            items = [(banks[b][64 * e:64 * e + 64, :], xsT[p % 2][:, k, 64 * e:64 * e + 64], ws[e][:, k, :],
                      k == 0, k == 7) for k in range(8) for e in range(2)]
            tk = mms(items, a0_, a1_, gathered[p])
            slot_free[n0] = slot_free[n1] = tk
            return b, tk

        def turn_h(p, fc, t_a):
            b = take()
            tk = transposes([(banks[b][:, 128 * j:128 * j + 128], ab[p % 2][:, 512 * fc + 128 * j:512 * fc + 128 * j + 128])
                             for j in range(4)], t_a)
            free[b] = vcopy(flat(hT[p % 2][:, 4 * fc:4 * fc + 4, :]), banks[b][:, :], tk, h_read[p % 2])
            return tk, free[b]

        for piece in gather(0):
            piece()
        work = []
        for p in range(8):
            i = p % 2
            late = None
            for fc in range(4):
                b, tk = up(I["w_gate"], p, fc)
                free[b] = t1 = act(ACT.Silu, stm[fc % 2], banks[b][:, :], tk, stm_read[fc % 2])
                if work:
                    work.pop(0)()
                b, tk = up(I["w_up"], p, fc)
                free[b] = t_a = tt(ab[i][:, 512 * fc:512 * fc + 512], banks[b][:, :], stm[fc % 2], ALU.mult, tk, t1,
                                   ab_read[i])
                stm_read[fc % 2] = t_a
                if late is not None:
                    turn_h(p, fc - 1, late)
                if work:
                    work.pop(0)()
                if fc == 1 and p < 7:
                    assert not work
                    work += gather(p + 1)
                late = t_a
            xs_read[i] = tk
            ab_read[i], t_hid = turn_h(p, 3, late)
            yb = [take(), take()]
            for kc in range(4):
                (n0, s0_, a0_), (n1, s1_, a1_) = pair_chunks(I["w_down"], p, lambda x_: rows(x_, 512 * kc, 4))
                ws = [v3(s0_, 4), v3(s1_, 4)]
                tk = mms([(banks[yb[f]][64 * e:64 * e + 64, :], hT[i][:, 4 * kc + k, 64 * e:64 * e + 64],
                           ws[e][:, k, 512 * f:512 * f + 512], kc + k == 0, kc == 3 and k == 3)
                          for k in range(4) for f in range(2) for e in range(2)], a0_, a1_, t_hid)
                slot_free[n0] = slot_free[n1] = tk
            h_read[i] = tk
            free[yb[0]] = acopy(ys[:, 0:512], banks[yb[0]][:, :], tk, ys_read[0])
            free[yb[1]] = t_y = acopy(ys[:, 512:1024], banks[yb[1]][:, :], tk)
            assert not work
            work = combine(p, t_y)
        stat_at["sq"] = [M + 15360, M + 15872]
        both = stat_begin([1.0, col["norm_final"]])
        for n, piece in enumerate(work):
            piece()
            if n:
                stat_add(both, 2 * n - 2)
                stat_add(both, 2 * n - 1)
        stat_add(both, 6)
        stat_add(both, 7)
        win2 = I["w_in_2"][0]
        wup = I["w_up_2"][0]

        def qparts(slot):
            dst = slot.rearrange("p (k i g c) -> p k i g c", k=8, i=4, g=2)
            return [(dst[:, :, i, g, :], win2[:, 256 * g + 64 * i:256 * g + 64 * i + 64].rearrange("(k p) c -> p k c", p=P))
                    for g in range(2) for i in range(4)]

        def w1parts(w1):
            return lambda slot: [(slot.rearrange("p (m n) -> p m n", m=16), w1[0].rearrange("(m p) n -> p m n", p=P))]

        def oparts(slot):
            dst = v3(slot, 4)
            src = I["w_o_nsa_2"][0].rearrange("(g i d) n -> g d i n", g=2, i=4)
            return [(dst[64 * g:64 * g + 64, :, :], src[g]) for g in range(2)]

        def upparts(c):
            def parts(slot):
                v = slot.rearrange("p (k n) -> p k n", k=8)
                return [(v[:, :, 256 * h:256 * h + 256],
                         wup[:, 2816 * h + 256 * c:2816 * h + 256 * c + 256].rearrange("(k p) n -> p k n", p=P))
                        for h in range(2)]
            return parts

        def downparts(h, k0, nk):
            def parts(slot):
                return [(slot[:, 0:512 * nk].rearrange("p (k n) -> p k n", k=nk),
                         I["w_down_2"][0][128 * k0:128 * (k0 + nk), 512 * h:512 * h + 512]
                         .rearrange("(k p) n -> p k n", p=P))]
            return parts

        KD = [(0, 8), (8, 8), (16, 6)]
        specs += [(cols(win2, 1816, 512), 4096, True), (cols(win2, 1304, 512), 4096, True),
                  (cols(win2, 512, 512), 4096, True), (cols(win2, 1024, 280), 2240, True), (qparts, 4096, True),
                  (w1parts(I["w_cmp_k1_2"]), 4096, False), (w1parts(I["w_cmp_v1_2"]), 4096, False),
                  (oparts, 4096, True), (cols(win2, 2328, 512), 4096, True), (cols(win2, 2840, 512), 4096, True),
                  (rows(I["w_conv_out_2"][0], 0, 4), 4096, True), (cols(win2, 3352, 512), 4096, True),
                  (cols(win2, 3864, 512), 4096, True), (cols(I["w_out_2"][0], 0, 512), 4096, True),
                  (cols(I["w_out_2"][0], 512, 512), 4096, True)]
        specs += [(upparts(c), 4096, True) for c in range(11)]
        specs += [(downparts(h, k0, nk), 512 * nk, True) for h in range(2) for k0, nk in KD]
        specs += [(lambda slot: [(slot[:, 0:2048].rearrange("p (k n) -> p k n", k=2),
                                  I["w_ple_2"][0].rearrange("(k p) n -> p k n", p=P))], 2048, True)]
        specs += [(cols(I["w_ple_gate_2"][0], 512 * h, 512), 4096, True) for h in range(2)]
        turns["pair"] = 0
        conv_chunk = prep_load()

        r1, rr, rstd = mem(512, M + 23136), mem(512, M + 23648), mem(512, M + 19584)
        b1_, b2_ = both["banks"]
        ts(rr, banks[b1_][:, :], EPS, EPS * EPS, ALU.mult, ALU.add, both["tk"])
        t1 = tt(rr, rr, banks[b2_][:, :], ALU.add)
        t1 = act(ACT.Sqrt, rr, rr, t1)
        t_r = recip(rr, rr, t1)
        gain12 = small[:, 560:568]
        t_g12 = tt(gain12, col["norm_final"], col["g_mix"], ALU.mult)
        UH, UL = v3(memR(4096, M), 8), v3(memR(4096, M + 4096), 8)
        FT = [M + 22112]

        def normed(gain, t_r, *waits, between=()):
            out_, f_read = [], [None, None]
            for d in range(8):
                if d % 2 == 0 and between:
                    between[d // 2]()
                f = mem(512, FT[0] + 512 * (d % 2))
                h, l = UH[:, d, :], UL[:, d, :]
                t1 = stt(f, XT[:, d, :], gain[:, d:d + 1], rstd, ALU.mult, ALU.mult, t_r, f_read[d % 2], *waits,
                         chain=False)
                t2 = chained(A, lambda e, f=f, h=h: e.activation(h, f, ACT.Copy), (t1, *waits))
                t3 = chained(G if d % 2 else V, lambda e, f=f, h=h, l=l:
                             e.tensor_tensor(l, f, h.bitcast(F32), ALU.subtract), (t1, t2, *waits))
                f_read[d % 2] = t3
                out_.append([t2, t3])
            return out_

        rstd_2, rstd = rstd, rr
        t_u = normed(gain12, t_r, *now(PE, V), between=division(*conv_chunk))
        t_r1 = stat_end(both, r1)
        free[b2_] = t_r1
        let_go(b2_)
        q2 = v3(mem(2048, M + 8192), 4)
        KZ = mem(2048, M + 10240).rearrange("p (b g t) -> p b g t", b=2, g=2)
        VS = mem(1024, M + 12288).rearrange("p (b t n) -> p b t n", b=2, t=4)
        GT = v3(mem(96, M + 13312), 4)
        kcat = [v3(mem(1024, M + 13440 + 1024 * i), 2) for i in range(2)]
        CO = v3(own(2048, M + 15488), 4)
        CI = v3(mem(2048, M + 17536), 4)
        RB = [mem(992, M + 21120 + 992 * i).rearrange("p (m g n) -> p m g n", m=16, g=2) for i in range(2)]
        pcs = [mem(256, M + 26752 + 256 * i) for i in range(2)]
        PS = [mem(2560, M + 2560 * i) for i in range(2)]
        PTr = [mem(2560, M + 5120), mem(2560, M + 21120)]
        pcT = v3(mem(1024, M + 23680), 2)
        OH, OL = v3(memR(2048, M + 13440), 4), v3(memR(2048, M + 24704), 4)
        t_b2 = now(PE, A, V)
        vset(KZ.rearrange("p b g t -> p (b g t)"), 0.0, *t_b2)
        KC = v3(small[:, 208:272], 2)
        HID = small[:, 272:400].rearrange("p (h g n) -> p h g n", h=2, g=2)
        VC = v3(small[:, 400:528], 2)
        t_kz = vset(small[:, 208:400], 0.0)

        ch = chunk()
        bs, tk = dfour(ch, 512, t_u)
        prep()
        for j in range(4):
            free[bs[j]] = t_cg = act(ACT.Sigmoid, CO[:, j, :], banks[bs[j]][:, :], tk, *t_b2)
        release(ch, tk)
        ch = chunk()
        for j in range(4):
            b, tk = dproj(ch, 512, j, None)
            free[b] = t_ci = tt(CI[:, j, :], banks[b][:, :], CO[:, j, :], ALU.mult, tk, t_cg, *t_b2)
            for d in (2 * j, 2 * j + 1):
                t_xn2 = stt(XT[:, d, :], XT[:, d, :], col["norm_final"][:, d:d + 1], r1, ALU.mult, ALU.mult, t_r1)
            if j == 1:
                prep()
        release(ch, tk)

        recip(r1, r1, t_xn2)
        t_r = tt(rstd_2, rr, r1, ALU.mult)
        rstd = rstd_2

        taps = []
        cw2 = col["conv_w_2"]
        for j in range(4):
            def first(j=j):
                return ts(CO[:, j, :], CI[:, j, :], cw2[:, 120 + j:121 + j], col["conv_b"][:, j:j + 1],
                          ALU.mult, ALU.add)
            taps.append(first)
            for s in range(1, 31):
                def tap(j=j, s=s):
                    k = 4 * (30 - s) + j
                    return stt(CO[:, j, s:], CI[:, j, :T - s], cw2[:, k:k + 1], CO[:, j, s:], ALU.mult, ALU.add)
                taps.append(tap)

        def conv_taps(n):
            for _ in range(n):
                if taps:
                    cur["conv"] = taps.pop(0)()

        ct = [mem(512, M + 24704 + 512 * i) for i in range(3)]

        def columns(ch, n, c0, m, func, i, *waits):
            wh, wl = (z[:, 0:8 * n].rearrange("p (k n) -> p k n", k=8) for z in (ch[3], ch[4]))
            s_ = slice(c0, c0 + m)
            b = take()
            items = []
            for k in range(8):
                items += three(banks[b][0:m, :], wh[:, k, s_], wl[:, k, s_], UH[:, k, :], UL[:, k, :], k == 0, k == 7,
                               quarter(ch, k, 8))
            tk = mms(items)
            free[b] = act(func, ct[i][0:m, :], banks[b][0:m, :], tk, *t_b2, *waits)
            return b, (ct[i][0:m, :], tk, free[b])

        def to_tokens(v, m, evac):
            b = take()
            tk = transposes([(banks[b][:, m * t:m * t + m], v[0][:, 128 * t:128 * t + 128]) for t in range(4)], v[2])
            free[b] = evac(v3(banks[b][:, 0:4 * m], 4), tk)
            return free[b]

        ch = chunk()
        for w_ in range(2):
            b, tk = dproj(ch, 512, w_, None)
            for g in range(2):
                for l2 in range(2):
                    free[b] = t_kc = acopy(kcat[w_][64 * l2:64 * l2 + 64, g, 0:512 - l2],
                                           banks[b][64 * g:64 * g + 64, l2:512], tk, *t_b2)
            conv_taps(2)
        prep()
        t_rb = []
        for w_, pos in enumerate((col["pos_k"], col["pos_v"])):
            for m in range(16):
                src = kcat[w_][:, :, 2 * m:2 * m + 481:16]
                t1 = ts(RB[w_][:, m, :, :], src, pos[:, m:m + 1], None, ALU.add, None, t_kc, *now(PE), *t_u[6], *t_u[7],
                        chain=(m == 0))
            t_rb.append(t1)
        b, tk = dproj(ch, 512, 2, None)
        conv_taps(4)
        for g in range(2):
            free[b] = acopy(KZ[64 * g:64 * g + 64, 0, g, :], banks[b][64 * g:64 * g + 64, :], tk, t_kz)
        b, v_s = columns(ch, 512, 384, 128, ACT.Copy, 0, *now(A))
        release(ch, v_s[1])
        conv_taps(8)
        ch = chunk()
        b, tk = dproj(ch, 280, 0, None)
        for g in range(2):
            free[b] = acopy(KZ[64 * g:64 * g + 64, 1, g, :], banks[b][64 * g:64 * g + 64, :], tk)
        to_tokens(v_s, 128, lambda bk, tk: vcopy(VS[:, 0, :, :], bk, tk, *t_b2))
        prep()
        conv_taps(8)
        b, v_w = columns(ch, 280, 128, 128, ACT.Copy, 1)
        b, v_g = columns(ch, 280, 256, 24, ACT.Sigmoid, 2)
        release(ch, v_g[1])
        conv_taps(8)
        to_tokens(v_w, 128, lambda bk, tk: vcopy(VS[:, 1, :, :], bk, tk))
        t_gt = to_tokens(v_g, 24, lambda bk, tk: vcopy(GT, bk, tk, *t_b2))
        ch = chunk()
        for i in range(4):
            b, tk = dproj(ch, 512, i, None)
            free[b] = t_q2 = act(ACT.Copy, q2[:, i, :], banks[b][:, :], tk, scale=0.125)
            conv_taps(6)
            if i == 1:
                prep()
        release(ch, tk)
        prep()

        for w_ in range(2):
            ch = chunk()
            w = v3(ch[2], 16)
            b = take()
            tk = mms([(banks[b][:, 64 * h:64 * h + 62], w[:, m, 128 * h:128 * h + 128],
                       RB[w_][:, m, :, :].rearrange("p g n -> p (g n)"), m == 0, m == 15)
                      for h in range(2) for m in range(16)], *ch[5], t_rb[w_])
            release(ch, tk)
            for h in range(2):
                free[b] = t1 = act(ACT.Gelu_apprx_tanh, HID[:, h, :, 0:31],
                                   v3(banks[b][:, 64 * h:64 * h + 62], 2), tk, t_kz, *now(PE))
            b = take()
            if w_ == 0:
                tk = mms([(banks[b][64 * g:64 * g + 64, 0:32], W2k[:, h, :], HID[:, h, g, :], h == 0, h == 1)
                          for g in range(2) for h in range(2)], t1, t_pin)
                for g in range(2):
                    free[b] = t_kcz = vcopy(KC[64 * g:64 * g + 64, g, :], banks[b][64 * g:64 * g + 64, 0:32], tk)
                conv_taps(8)
            else:
                tk = mms([(banks[b][0:32, 64 * g:64 * g + 64], HID[:, h, g, :], W2v[:, h, :], h == 0, h == 1)
                          for g in range(2) for h in range(2)], t1, t_pin)
                for i in range(4):
                    free[b] = t_vcz = vcopy(flat(VC[32 * i:32 * i + 32, :, :]), banks[b][0:32, 0:128], tk)
        t_cmp = now(PE, V, A, G)

        pc_read = [None, None]
        t_pc = {}

        def compressed(t):
            mx, sm = (small[:, 528 + 8 * z + 16 * (t % 2):536 + 8 * z + 16 * (t % 2)] for z in range(2))
            b = take()
            tk = mms([(banks[b][:, 32 * (4 * g + i):32 * (4 * g + i) + 32], q2[:, i, 128 * t:128 * t + 128], KC[:, g, :],
                       True, True) for g in range(2) for i in range(4)], t_q2, t_kcz)
            pc = pcs[t % 2].rearrange("p (j c) -> p j c", j=8)
            cm = cmask[:, t, :].unsqueeze(1).to_broadcast([P, 8, 32])
            free[b] = tt(pc, banks[b][:, 0:256].rearrange("p (j c) -> p j c", j=8), cm, ALU.add, tk, pc_read[t % 2], *t_cmp)
            reduce(mx, pc, ALU.max)
            ts(mx, mx, NEG / 10, None, ALU.max, None)
            t1 = tt(pc, pc, mx.unsqueeze(2).to_broadcast([P, 8, 32]), ALU.subtract)
            t1 = act(ACT.Exp, pc, pc, t1)
            reduce(sm, pc, ALU.add, t1)
            ts(sm, sm, 1e-30, None, ALU.max, None)
            recip(sm, sm)
            tt(sm, sm, GT[:, t, 0:8], ALU.mult, t_gt)
            t_pc[t] = tt(pc, pc, sm.unsqueeze(2).to_broadcast([P, 8, 32]), ALU.mult)

        def compressed_turned(t):
            b = take()
            pc_read[t % 2] = tk = transposes([(banks[b][:, 128 * g:128 * g + 128], pcs[t % 2][:, 128 * g:128 * g + 128])
                                              for g in range(2)], t_pc[t])
            free[b] = vcopy(pcT[:, :, 128 * t:128 * t + 128], v3(banks[b][:, 0:256], 2), tk)
            return free[b]

        off = [0, 128, 384, 768]
        offk = [0, 512, 896, 1152]
        turn["order"] = [2, 3, 4, 5, 6, 7]
        st = [small[:, 144 + 24 * i:144 + 24 * i + 24] for i in range(2)]
        ps_read = [[None, None], [None, None]]
        t_scaled = {}

        def scores(un, g):
            i, br = un // 2, un % 2
            Pb = PS[un % 2]
            nm, su, ri = st[un % 2][:, 0:8], st[un % 2][:, 8:16], st[un % 2][:, 16:24]
            for t in range(4):
                N = 128 * (t + 1)
                c0 = 128 * (t == 1)
                if t != 1:
                    b = take()
                    both_ = [(t, 0)] if t else [(0, 0), (1, 128)]
                    tk = mms([(banks[b][:, c:c + 128 * (t_ + 1)], q2[:, i, 128 * t_:128 * t_ + 128],
                               KZ[:, br, g, 0:128 * (t_ + 1)], True, True) for t_, c in both_], *t_cmp)
                o = Pb[:, 1280 * g + off[t]:1280 * g + off[t] + N]
                j = 4 * g + t
                free[b] = chained(V, lambda e, o=o, b=b, N=N, j=j, nm=nm, c0=c0: e.tensor_tensor_reduce(
                    o, banks[b][:, c0:c0 + N], causal[:, 512 - N:512], 1.0, -3e38, ALU.add, ALU.max, nm[:, j:j + 1]),
                    (tk, ps_read[un % 2][g], *t_cmp), chain=(t == 0))
            t1 = ts(nm[:, 4 * g:4 * g + 4], nm[:, 4 * g:4 * g + 4], -1.0, None, ALU.mult, None)
            for t in range(4):
                N = 128 * (t + 1)
                o = Pb[:, 1280 * g + off[t]:1280 * g + off[t] + N]
                j = 4 * g + t
                t2 = act(ACT.Exp, o, o, t1, bias=nm[:, j:j + 1], accum=su[:, j:j + 1], chain=(t == 0))
            t_sum[un, g] = t2

        t_sum = {}

        def weights(un, g):
            i, br = un // 2, un % 2
            Pb = PS[un % 2]
            su, ri = st[un % 2][:, 8:16], st[un % 2][:, 16:24]
            t3 = recip(ri[:, 4 * g:4 * g + 4], su[:, 4 * g:4 * g + 4], t_sum[un, g])
            for t in range(4):
                N = 128 * (t + 1)
                o = Pb[:, 1280 * g + off[t]:1280 * g + off[t] + N]
                j = 4 * g + t
                gi = 8 * (1 + br) + 4 * g + i
                t_scaled[un, g, t] = ts(o, o, ri[:, j:j + 1], GT[:, t, gi:gi + 1], ALU.mult, ALU.mult, t3, t_gt,
                                        lane=G, chain=(t == 0))

        ptr_read = [None, None]
        t_pt2 = {}

        def turned(un, g):
            Pb, Tb = PS[un % 2], PTr[un % 2]
            for kts in ([0], [1], [2, 3]):
                b = take()
                blocks = [(kt, t) for kt in kts for t in range(kt, 4)]
                tk = transposes([(banks[b][:, 128 * n:128 * n + 128],
                                  Pb[:, 1280 * g + off[t] + 128 * kt:1280 * g + off[t] + 128 * kt + 128])
                                 for n, (kt, t) in enumerate(blocks)], *[t_scaled[un, g, t] for kt, t in blocks])
                o = Tb[:, 1280 * g + offk[kts[0]]:1280 * g + offk[kts[0]] + 128 * len(blocks)]
                free[b] = t_ = (vcopy if kts[0] == 1 else acopy)(o, banks[b][:, 0:128 * len(blocks)], tk,
                                                                 ptr_read[un % 2])
                for kt in kts:
                    t_pt2[g, kt] = t_
            ps_read[un % 2][g] = tk

        def values(un):
            i, br = un // 2, un % 2
            Tb = PTr[un % 2]
            ob = i % 2
            items = []
            if br == 0:
                PE.wait(free[ob])
            else:
                items += [(banks[ob][64 * g:64 * g + 64, :], VC[32 * i:32 * i + 32, g, :], pcT[32 * i:32 * i + 32, g, :],
                           False, False) for g in range(2)]
            for kt in range(4):
                items += [(banks[ob][64 * g:64 * g + 64, 128 * kt:512], VS[:, br, kt, 64 * g:64 * g + 64],
                           Tb[:, 1280 * g + offk[kt]:1280 * g + offk[kt] + 512 - 128 * kt], br == 0 and kt == 0, False,
                           t_pt2[g, kt]) for g in range(2)]
            ptr_read[un % 2] = tk = mms(items, *([t_pct, t_vcz] if br else []), skip=True)
            if br == 1:
                t1 = chained(A, lambda e: e.activation(OH[:, i, :], banks[ob][:, :], ACT.Copy), (tk, *t_cmp))
                free[ob] = t_ol[i] = chained(V, lambda e: e.tensor_tensor(OL[:, i, :], banks[ob][:, :],
                                                                          OH[:, i, :].bitcast(F32), ALU.subtract),
                                             (t1, *t_cmp))

        t_ol = [None] * 4
        scores(0, 0)
        compressed(0)
        weights(0, 0)
        scores(0, 1)
        compressed(1)
        weights(0, 1)
        for un in range(8):
            for g in range(2):
                if un == 0:
                    compressed_turned(g)
                if un > 0:
                    turned(un, g)
                if un < 7:
                    scores(un + 1, g)
                if un == 0:
                    compressed(2 + g)
                    turned(un, g)
                else:
                    conv_taps(3 if un > 3 else 2)
                if un < 7:
                    weights(un + 1, g)
            values(un)
            if un == 1:
                prep()
            if un == 0:
                compressed_turned(2)
                t_pct = compressed_turned(3)
        t_at = now(PE, A, V, G)
        turn["order"] = list(range(8))

        FT[0] = M + 20096
        t_u = normed(col["g_mix"], t_r, *t_at)
        YAo = v3(own(4096, M + 8192), 8)
        YB = v3(mem(4096, M + 17536), 8)
        ytmp = [mem(512, M + 21632 + 512 * i) for i in range(2)]
        ch = chunk()
        for d in range(8):
            wh, wl = v3(ch[3], 4), v3(ch[4], 4)
            b = take()
            s_ = slice(128 * d, 128 * d + 128)
            items = []
            for i in range(4):
                items += three(banks[b][:, :], wh[:, i, s_], wl[:, i, s_], OH[:, i, :], OL[:, i, :], i == 0, i == 3, quarter(ch, i, 4), t_ol[i])
            tk = mms(items)
            free[b] = t_ya = acopy(YAo[:, d, :], banks[b][:, :], tk, *t_at)
            conv_taps(3)
            if d == 3:
                prep()
        release(ch, tk)
        def ln_mean():
            assert not taps
            b = take()
            tk = group(banks[b][:, :], [(onesC, CO[:, j, :]) for j in range(4)], cur["conv"])
            for j in range(4):
                t1 = tt(CO[:, j, :], CO[:, j, :], banks[b][:, :], ALU.subtract, tk, chain=(j == 0))
            free[b] = t1
            for j in range(4):
                t2 = act(ACT.Square, v3(mem(2048, M + 22656), 4)[:, j, :], CO[:, j, :], t1, *t_at, chain=(j == 0))
            return t2

        def ln_rest(t2):
            b = take()
            tk = mms([(banks[b][:, :], onesC, v3(mem(2048, M + 22656), 4)[:, j, :], j == 0, j == 3)
                      for j in range(4)], t2)
            rs2 = mem(512, M + 22656)
            act(ACT.Ln, rs2, banks[b][:, :], tk, bias=epst)
            free[b] = t2 = act(ACT.Exp, rs2, rs2, scale=-0.5)
            for j in range(4):
                t1 = tt(CO[:, j, :], CO[:, j, :], rs2, ALU.mult, t2, chain=(j == 0))
                t_co = act(ACT.Silu, CO[:, j, :], CO[:, j, :], t1, scale=col["ln_g"][:, j:j + 1],
                           bias=col["ln_b"][:, j:j + 1])
            return t_co

        yt_read = [None, None]
        for c in range(2):
            ch = chunk()
            for j in range(4):
                d = 4 * c + j
                b, tk = dproj(ch, 512, j, t_u)
                free[b] = t1 = act(ACT.Sigmoid, ytmp[d % 2], banks[b][:, :], tk, yt_read[d % 2], *t_at)
                yt_read[d % 2] = tt(YAo[:, d, :], YAo[:, d, :], ytmp[d % 2], ALU.mult, t1, t_ya)
                if j == 1:
                    prep()
                if c == 0 and j == 1:
                    t_mu = ln_mean()
                if c == 1 and j == 0:
                    t_co = ln_rest(t_mu)
                    CH, CL, t_cs = split(M + 22656, M + 15488, 2048, t_co, *now(PE, V, A))
            release(ch, tk)
        CH, CL = v3(CH, 4), v3(CL, 4)

        ch = chunk()
        for d in range(8):
            wh, wl = v3(ch[3], 4), v3(ch[4], 4)
            b = take()
            s_ = slice(128 * d, 128 * d + 128)
            items = []
            for i in range(4):
                items += three(banks[b][:, :], wh[:, i, s_], wl[:, i, s_], CH[:, i, :], CL[:, i, :], i == 0, i == 3,
                               quarter(ch, i, 4), t_cs)
            tk = mms(items)
            free[b] = t_yb = act(ACT.Identity, YB[:, d, :], banks[b][:, :], tk, t_cs, bias=col["b_co"][:, d:d + 1])
            if d == 3:
                prep()
        release(ch, tk)
        t_m = [None] * 8
        t_zm = now(PE, V, A)
        halves = [v3(memR(2048, M + 22656), 4), v3(memR(2048, M + 15488), 4)]
        MH = [halves[d // 4][:, d % 4, :] for d in range(8)]
        ML = v3(memR(4096, M + 8192), 8)
        for c in range(2):
            ch = chunk()
            for j in range(4):
                d = 4 * c + j
                b, tk = dproj(ch, 512, j, None)
                free[b] = t1 = act(ACT.Sigmoid, ytmp[d % 2], banks[b][:, :], tk, yt_read[d % 2], t_co, *now(V))
                tt(ytmp[d % 2], ytmp[d % 2], YB[:, d, :], ALU.mult, t1, t_yb)
                yt_read[d % 2] = t1 = tt(YAo[:, d, :], YAo[:, d, :], ytmp[d % 2], ALU.add)
                h, l, f = MH[d], ML[:, d, :], YAo[:, d, :]
                t1 = chained(A, lambda e, h=h, f=f: e.activation(h, f, ACT.Copy), (t1, *t_zm))
                t_m[d] = chained(G, lambda e, h=h, l=l, f=f: e.tensor_tensor(l, f, h.bitcast(F32), ALU.subtract), (t1,))
                if j == 1:
                    prep()
            release(ch, tk)
        stat_at["sq"] = [M + 26752, M + 27264]
        for half in range(2):
            ch = chunk()
            if half == 0:
                bs, tk = dfour(ch, 512, t_m, 8, MH, ML)
            prep()
            for j in range(4):
                d = 4 * half + j
                if half:
                    b = take()
                    wh, wl = v3(ch[3], 8), v3(ch[4], 8)
                    s_ = slice(128 * j, 128 * j + 128)
                    items = []
                    for k in range(8):
                        items += three(banks[b][:, :], wh[:, k, s_], wl[:, k, s_], MH[k], ML[:, k, :], k == 0, k == 7,
                                       quarter(ch, k, 8))
                    tk = mms(items)
                else:
                    b = bs[j]
                free[b] = t_xt[d] = tt(XT[:, d, :], banks[b][:, :], XT[:, d, :], ALU.add, tk)
                if half:
                    if j == 0:
                        st_ = stat_begin([1.0])
                        t_sq = now(PE, V, A, G)
                    else:
                        stat_add(st_, 2 * j - 2, *t_sq)
                        stat_add(st_, 2 * j - 1, *t_sq)
            release(ch, tk)
        stat_add(st_, 6)
        stat_add(st_, 7)

        rstd = mem(512, M + 24704)
        FT[0] = M + 25216
        t_r = stat_end(st_, rstd)
        t_u = normed(col["g_ffn"], t_r, *now(PE))
        GF = v3(mem(22 * 512, M + 8192), 22)
        fg = [mem(512, M + 19456 + 512 * i) for i in range(2)]
        fv = [mem(512, M + 20480 + 512 * i) for i in range(2)]
        f_read = [None, None]
        ptok = v3(mem(4 * 256, M + 26240), 4)
        SP.wait(*now(PE, V, A))
        SP.silent(lambda e: e.dma_start(ptok, I["p_2"][0, 0].rearrange("(t p) d -> p t d", p=P)).then_inc(s_pt, 16))

        def conv3(o, b, tk, t, *waits):
            w0, w1_, w2_ = col["fcw01"][:, t:t + 1], col["fcw01"][:, 44 + t:45 + t], col["fcw2"][:, t:t + 1]
            t1 = act(ACT.Identity, o, banks[b][:, :], tk, *waits, scale=w2_, bias=col["fcb"][:, t:t + 1])
            stt(o[:, 1:], banks[b][:, 0:T - 1], w1_, o[:, 1:], ALU.mult, ALU.add, t1)
            return stt(o[:, 2:], banks[b][:, 0:T - 2], w0, o[:, 2:], ALU.mult, ALU.add)

        t_f0 = now(PE, V)
        t_gf = {}
        for c in range(11):
            ch = chunk()
            if c == 0:
                bs, tk = dfour(ch, 512, t_u)
                prep()
            for j in range(2):
                t = 2 * c + j
                b, tk = (bs[j], tk) if c == 0 else dproj(ch, 512, j, None)
                free[b] = t1 = conv3(fg[t % 2], b, tk, t, f_read[t % 2], *t_f0)
                t2 = act(ACT.Gelu_apprx_tanh, fg[t % 2], fg[t % 2], t1)
                b, tk = (bs[2 + j], tk) if c == 0 else dproj(ch, 512, 2 + j, None)
                free[b] = t1 = conv3(fv[t % 2], b, tk, 22 + t, f_read[t % 2])
                f_read[t % 2] = t_gf[t] = tt(GF[:, t, :], fg[t % 2], fv[t % 2], ALU.mult, t2)
                if j == 0 and c:
                    prep()
            release(ch, tk)
        gh = [(memR(512, M + 21504 + 1024 * i), memR(512, M + 22016 + 1024 * i)) for i in range(4)]
        g_read = [now(PE, V)] * 4
        order = [kk for h in range(2) for kk in range(22)]
        made = []

        def make_g():
            n = len(made)
            if n >= len(order):
                return
            kk = order[n]
            xh, xl = gh[n % 4]
            t1 = chained(A, lambda e: e.activation(xh, GF[:, kk, :], ACT.Copy), (t_gf[kk], g_read[n % 4]))
            t2 = chained(V if n % 2 else G, lambda e: e.tensor_tensor(xl, GF[:, kk, :], xh.bitcast(F32), ALU.subtract),
                         (t1,))
            made.append((xh, xl, t2))

        for _ in range(3):
            make_g()
        stat_at["sq"] = [M + 25600, M + 27264]
        for h in range(2):
            bs = [take() for _ in range(4)]
            for k0, nk in KD:
                ch = chunk()
                wh, wl = v3(ch[3], nk), v3(ch[4], nk)
                for k in range(nk):
                    kk = k0 + k
                    n = 22 * h + kk
                    make_g()
                    xh, xl, t2 = made[n]
                    items = []
                    for j in range(4):
                        s_ = slice(128 * j, 128 * j + 128)
                        items += three(banks[bs[j]][:, :], wh[:, k, s_], wl[:, k, s_], xh, xl, kk == 0, kk == 21,
                                       quarter(ch, k, nk), t2)
                    g_read[n % 4] = tk = mms(items)
                    if h and kk in (8, 10, 12, 14):
                        if kk == 8:
                            st_ = stat_begin([1.0])
                        stat_add(st_, kk // 2 - 4)
                    if k == nk // 2:
                        prep()
                release(ch, tk)
            for j in range(4):
                d = 4 * h + j
                free[bs[j]] = t_xt[d] = tt(XT[:, d, :], banks[bs[j]][:, :], XT[:, d, :], ALU.add, tk)
        for d in range(4, 8):
            stat_add(st_, d)

        gate_chunk = prep_load()
        PH, PL = v3(memR(1024, M + 8192), 2), v3(memR(1024, M + 9216), 2)
        E = v3(mem(4096, M + 10240), 8)
        t_e0 = now(PE, V, A)
        t_ps = []
        for j in range(2):
            b = take()
            tk = transposes([(banks[b][:, 128 * t:128 * t + 128], ptok[:, t, 128 * j:128 * j + 128])
                             for t in range(4)], (s_pt, 16))
            t1 = chained(A, lambda e, b=b, j=j: e.activation(PH[:, j, :], banks[b][:, :], ACT.Copy), (tk, *t_e0))
            free[b] = chained(V, lambda e, b=b, j=j: e.tensor_tensor(PL[:, j, :], banks[b][:, :],
                                                                     PH[:, j, :].bitcast(F32), ALU.subtract),
                              (t1, *t_e0))
            t_ps.append(free[b])
        ch = prepared.pop(0)
        rstd = mem(512, M + 20480)
        FT[0] = M + 24704
        t_r = stat_end(st_, rstd, *now(V, PE))
        t_down = now(PE)
        e_bk = [dproj(ch, 1024, d, t_ps, PH, PL, 2) for d in range(8)]
        release(ch, e_bk[7][1])

        def keep_e(*ds):
            for d in ds:
                b, tk = e_bk[d]
                free[b] = (vcopy if d % 2 else acopy)(E[:, d, :], banks[b][:, :], tk, *t_e0)

        div = division(*gate_chunk)
        hooks = [div[0]] + [lambda q=q: (div[q](), keep_e(2 * q - 2, 2 * q - 1)) for q in (1, 2, 3)]
        t_u = normed(col["g_ple"], t_r, *t_down, between=hooks)
        keep_e(6, 7)
        t_e = now(V, A)
        for half in range(2):
            ch = chunk()
            if half == 0:
                bs, tk = dfour(ch, 512, t_u)
                prep()
            for j in range(4):
                d = 4 * half + j
                b, tk = dproj(ch, 512, j, None) if half else (bs[j], tk)
                free[b] = t1 = act(ACT.Sigmoid, fg[d % 2], banks[b][:, :], tk, *now(V))
                tt(fg[d % 2], fg[d % 2], E[:, d, :], ALU.mult, t1, *t_e)
                t_xt[d] = tt(XT[:, d, :], XT[:, d, :], fg[d % 2], ALU.add)
                if half:
                    if j == 0:
                        st_ = stat_begin([1.0])
                    else:
                        stat_add(st_, 2 * j - 2)
                        stat_add(st_, 2 * j - 1)
            release(ch, tk)
        stat_add(st_, 6)
        stat_add(st_, 7)
        t_r = stat_end(st_, rstd)
        toks = scaled(XT, col["g_final"], t_r)
        OUTT = v3(mem(4096, M), 4)
        s_out = sem("s_out")
        t_o = now(PE, V)
        o_v = out[0].rearrange("(t p) d -> p t d", p=P)
        for t in range(4):
            for half in range(2):
                b = take()
                tk = transposes([(banks[b][:, 128 * j:128 * j + 128], XT[:, 4 * half + j, 128 * t:128 * t + 128])
                                 for j in range(4)], *toks)
                free[b] = (vcopy if half else acopy)(OUTT[:, t, 512 * half:512 * half + 512], banks[b][:, :], tk, *t_o)
            SP.wait(*now(V, A))
            SP.silent(lambda e, t=t: e.dma_start(o_v[:, t, :], OUTT[:, t, :]).then_inc(s_out, 16))
        SP.wait((s_out, 64))

        block = ctx.enter_context(nc.Block())

        def play(lane):
            def body(e):
                for make in lane.queue:
                    make(e)
            return body

        block.sync(play(SP))
        block.scalar(play(A))
        block.vector(play(V))
        block.gpsimd(play(G))
        block.tensor(play(PE))


_INS = ["x", "c", "ctx", "c_ctx", "w_ada", "b_ada", "norm_mix", "norm_ffn", "w_in", "lb_logits", "hg_norm", "conv_w",
        "w_out", "w_router", "w_gate", "w_up", "w_down", "norm_final", "p_2", "g_mix_2", "w_in_2", "cmp_pos_k_2",
        "cmp_pos_v_2", "w_cmp_k1_2", "w_cmp_k2_2", "w_cmp_v1_2", "w_cmp_v2_2", "w_o_nsa_2", "conv_w_2", "conv_b_2",
        "conv_ln_g_2", "conv_ln_b_2", "w_conv_out_2", "b_conv_out_2", "w_out_2", "g_ffn_2", "w_up_2", "ffn_conv_w_2",
        "ffn_conv_b_2", "w_down_2", "g_ple_2", "w_ple_gate_2", "w_ple_2", "g_final_2"]


def kernel(**inputs):
    import numpy as _np
    import concourse.bacc as _bacc
    from concourse import mybir as _mybir
    from concourse.bass_utils import run_bass_kernel_spmd as _run

    nc = _bacc.Bacc("TRN2", target_bir_lowering=False, num_devices=1)
    arrays, aps = {}, {}
    for name in _INS:
        a = _np.ascontiguousarray(inputs[name])
        arrays[f"in_{name}_dram"] = a
        aps[name] = nc.dram_tensor(f"in_{name}_dram", a.shape, _mybir.dt.from_np(a.dtype), kind="ExternalInput").ap()
    out = nc.dram_tensor("out_0_dram", (1, 512, 1024), _mybir.dt.float32, kind="ExternalOutput").ap()
    build_program(nc, aps, out)
    r = _run(nc, [arrays], core_ids=[0])
    return r.results[0]["out_0_dram"]
```
